# Optimizing a Trainium2 kernel written in Bass

```python
import math
import jax
import jax.numpy as jnp
from jax import lax
import numpy as np

D_MODEL = 1024
BATCH = 1
SEQ = 256
DEPTH = 1

N_MIXERS = 2
RMS_EPS = 1e-5

SSD_EXPAND = 2
SSD_D_INNER = SSD_EXPAND * D_MODEL
SSD_HEADDIM = 64
SSD_N_HEADS = SSD_D_INNER // SSD_HEADDIM
SSD_N_GROUPS = 4
SSD_HEADS_PER_GROUP = SSD_N_HEADS // SSD_N_GROUPS
SSD_D_STATE = 128
SSD_D_CONV = 4
SSD_CHUNK = 128
SSD_GN = SSD_N_GROUPS * SSD_D_STATE
SSD_CONV_DIM = SSD_D_INNER + 2 * SSD_GN
SSD_IN_DIM = SSD_D_INNER + SSD_CONV_DIM + SSD_N_HEADS

DA_HEAD_DIM = 64
DA_N_HEADS = D_MODEL // (2 * DA_HEAD_DIM)
DA_Q_BLOCK = 128

MEM_LEN = 256
XA_N_HEADS = 4
XA_HEAD_DIM = D_MODEL // XA_N_HEADS

N_EXPERTS = 32
TOP_K = 4
D_FF = D_MODEL
SWIGLU_LIMIT = 7.0
SWIGLU_ALPHA = 1.702
MOE_BLOCK = 256

N_SSD_LAYERS = (DEPTH + N_MIXERS - 1) // N_MIXERS
N_DA_LAYERS = DEPTH // N_MIXERS

kernel_name = 'hybrid_ssd_diffattn_memxattn_moe'

def rms_norm(x, g):
    xf = x.astype(jnp.float32)
    y = xf * lax.rsqrt(jnp.mean(xf * xf, axis=-1, keepdims=True) + RMS_EPS)
    return (y * g.astype(jnp.float32)).astype(x.dtype)

def causal_depthwise_conv(u, w, b):
    k = w.shape[0]
    out = lax.conv_general_dilated(u, w[:, None, :].astype(u.dtype), window_strides=(1,), padding=[(k - 1, 0)],
                                   dimension_numbers=('NWC', 'WIO', 'NWC'), feature_group_count=u.shape[-1])
    return out + b.astype(u.dtype)

def ssd_chunked_scan(x, dt, a, b_in, c_in):
    bsz, seq = x.shape[0], x.shape[1]
    nc = seq // SSD_CHUNK
    L, G, J = SSD_CHUNK, SSD_N_GROUPS, SSD_HEADS_PER_GROUP
    xd = (x * dt[..., None]).reshape(bsz, nc, L, G, J, SSD_HEADDIM)
    da = jnp.moveaxis((dt * a).reshape(bsz, nc, L, G, J), 2, -1)
    bc = b_in.reshape(bsz, nc, L, G, SSD_D_STATE)
    cc = c_in.reshape(bsz, nc, L, G, SSD_D_STATE)
    a_cum = jnp.cumsum(da, axis=-1)
    causal = jnp.tril(jnp.ones((L, L), dtype=bool))
    decay = jnp.exp(jnp.where(causal, a_cum[..., :, None] - a_cum[..., None, :], -jnp.inf))
    cb = jnp.einsum('bclgn,bcsgn->bcgls', cc, bc)
    y_diag = jnp.einsum('bcgls,bcgjls,bcsgjp->bclgjp', cb, decay, xd)
    decay_to_end = jnp.exp(a_cum[..., -1:] - a_cum)
    chunk_states = jnp.einsum('bclgn,bcgjl,bclgjp->bcgjpn', bc, decay_to_end, xd)
    chunk_decay = jnp.exp(a_cum[..., -1])

    def step(state, inp):
        st, dec = inp
        return state * dec[..., None, None] + st, state

    init = jnp.zeros((bsz, G, J, SSD_HEADDIM, SSD_D_STATE), jnp.float32)
    _, prev = lax.scan(step, init, (jnp.moveaxis(chunk_states, 1, 0), jnp.moveaxis(chunk_decay, 1, 0)))
    prev = jnp.moveaxis(prev, 0, 1)
    y_off = jnp.einsum('bclgn,bcgjpn,bcgjl->bclgjp', cc, prev, jnp.exp(a_cum))
    return (y_diag + y_off).reshape(bsz, seq, SSD_N_HEADS, SSD_HEADDIM)

def ssd_mixer(h, w_in, conv_w, conv_b, dt_bias, a_log, d_skip, norm_g, w_out):
    bsz, seq, _ = h.shape
    proj = h @ w_in
    z = proj[..., :SSD_D_INNER]
    xbc = proj[..., SSD_D_INNER:SSD_D_INNER + SSD_CONV_DIM]
    dt_raw = proj[..., SSD_D_INNER + SSD_CONV_DIM:]
    xbc = jax.nn.silu(causal_depthwise_conv(xbc, conv_w, conv_b)).astype(jnp.float32)
    xs = xbc[..., :SSD_D_INNER].reshape(bsz, seq, SSD_N_HEADS, SSD_HEADDIM)
    b_in = xbc[..., SSD_D_INNER:SSD_D_INNER + SSD_GN].reshape(bsz, seq, SSD_N_GROUPS, SSD_D_STATE)
    c_in = xbc[..., SSD_D_INNER + SSD_GN:].reshape(bsz, seq, SSD_N_GROUPS, SSD_D_STATE)
    dt = jax.nn.softplus(dt_raw.astype(jnp.float32) + dt_bias.astype(jnp.float32))
    a = -jnp.exp(a_log.astype(jnp.float32))
    y = ssd_chunked_scan(xs, dt, a, b_in, c_in) + d_skip.astype(jnp.float32)[:, None] * xs
    u = y.reshape(bsz, seq, SSD_D_INNER) * jax.nn.silu(z.astype(jnp.float32))
    u = u.reshape(bsz, seq, SSD_N_GROUPS, SSD_D_INNER // SSD_N_GROUPS)
    u = u * lax.rsqrt(jnp.mean(u * u, axis=-1, keepdims=True) + RMS_EPS)
    u = u.reshape(bsz, seq, SSD_D_INNER) * norm_g.astype(jnp.float32)
    return u.astype(h.dtype) @ w_out

def diff_attention(h, w_qkv, lq1, lk1, lq2, lk2, subln_g, w_o, layer_idx):
    bsz, seq, _ = h.shape
    qkv = h @ w_qkv
    q = qkv[..., :D_MODEL].reshape(bsz, seq, DA_N_HEADS, 2, DA_HEAD_DIM)
    k = qkv[..., D_MODEL:2 * D_MODEL].reshape(bsz, seq, DA_N_HEADS, 2, DA_HEAD_DIM)
    v = qkv[..., 2 * D_MODEL:].reshape(bsz, seq, DA_N_HEADS, 2 * DA_HEAD_DIM)
    lambda_init = 0.8 - 0.6 * math.exp(-0.3 * layer_idx)
    lam = (jnp.exp(jnp.sum(lq1.astype(jnp.float32) * lk1.astype(jnp.float32)))
           - jnp.exp(jnp.sum(lq2.astype(jnp.float32) * lk2.astype(jnp.float32))) + lambda_init)
    scale = DA_HEAD_DIM ** -0.5
    nqb = seq // DA_Q_BLOCK
    q_blocks = jnp.swapaxes(q.reshape(bsz, nqb, DA_Q_BLOCK, DA_N_HEADS, 2, DA_HEAD_DIM), 0, 1)
    kpos = jnp.arange(seq)

    def one_block(args):
        q_blk, start = args
        s = jnp.einsum('bqhmd,bkhmd->bhmqk', q_blk, k).astype(jnp.float32) * scale
        qpos = start + jnp.arange(DA_Q_BLOCK)
        mask = kpos[None, :] <= qpos[:, None]
        p = jax.nn.softmax(jnp.where(mask, s, -jnp.inf), axis=-1)
        attn = p[:, :, 0] - lam * p[:, :, 1]
        return jnp.einsum('bhqk,bkhe->bqhe', attn.astype(v.dtype), v)

    o = lax.map(one_block, (q_blocks, jnp.arange(nqb) * DA_Q_BLOCK))
    o = jnp.swapaxes(o, 0, 1).reshape(bsz, seq, DA_N_HEADS, 2 * DA_HEAD_DIM)
    o = rms_norm(o, subln_g) * (1.0 - lambda_init)
    return o.reshape(bsz, seq, D_MODEL) @ w_o

def memory_cross_attention(h, mem_n, w_q, w_kv, w_o):
    bsz, seq, _ = h.shape
    m = mem_n.shape[1]
    q = (h @ w_q).reshape(bsz, seq, XA_N_HEADS, XA_HEAD_DIM)
    kv = mem_n @ w_kv
    k = kv[..., :D_MODEL].reshape(bsz, m, XA_N_HEADS, XA_HEAD_DIM)
    v = kv[..., D_MODEL:].reshape(bsz, m, XA_N_HEADS, XA_HEAD_DIM)
    s = jnp.einsum('bshd,bmhd->bhsm', q, k).astype(jnp.float32) * (XA_HEAD_DIM ** -0.5)
    p = jax.nn.softmax(s, axis=-1)
    o = jnp.einsum('bhsm,bmhd->bshd', p.astype(v.dtype), v).reshape(bsz, seq, D_MODEL)
    return o @ w_o

def moe_ffn(h, w_router, b_router, w_gate_up, b_gate_up, w_down, b_down):
    bsz, seq, d = h.shape
    t = bsz * seq
    ht = h.reshape(t, d)
    logits = (ht @ w_router).astype(jnp.float32) + b_router.astype(jnp.float32)
    top_logits, top_idx = lax.top_k(logits, TOP_K)
    gates = jax.nn.softmax(top_logits, axis=-1)
    n = t * TOP_K
    flat_e = top_idx.reshape(n)
    flat_tok = jnp.repeat(jnp.arange(t, dtype=jnp.int32), TOP_K)
    flat_g = gates.reshape(n)
    order = jnp.argsort(flat_e)
    sorted_e = flat_e[order]
    counts = jax.ops.segment_sum(jnp.ones((n,), jnp.int32), flat_e, num_segments=N_EXPERTS)
    padded = (counts + MOE_BLOCK - 1) // MOE_BLOCK * MOE_BLOCK
    start = jnp.cumsum(counts) - counts
    pend = jnp.cumsum(padded)
    pstart = pend - padded
    dest = pstart[sorted_e] + (jnp.arange(n, dtype=jnp.int32) - start[sorted_e])
    p_rows = -(-(n + N_EXPERTS * MOE_BLOCK) // MOE_BLOCK) * MOE_BLOCK
    nb = p_rows // MOE_BLOCK
    row_tok = jnp.full((p_rows,), t, jnp.int32).at[dest].set(flat_tok[order])
    row_gate = jnp.zeros((p_rows,), jnp.float32).at[dest].set(flat_g[order])
    blk_e = jnp.minimum(jnp.searchsorted(pend, jnp.arange(nb, dtype=jnp.int32) * MOE_BLOCK, side='right'), N_EXPERTS - 1)
    xs = ht[jnp.minimum(row_tok, t - 1)].reshape(nb, MOE_BLOCK, d)

    def expert_block(args):
        xb, e = args
        gu = xb @ w_gate_up[e] + b_gate_up[e]
        gate = jnp.minimum(gu[..., :D_FF], SWIGLU_LIMIT)
        up = jnp.clip(gu[..., D_FF:], -SWIGLU_LIMIT, SWIGLU_LIMIT)
        act = (up + 1.0) * (gate * jax.nn.sigmoid(gate * SWIGLU_ALPHA))
        return act @ w_down[e] + b_down[e]

    ys = lax.map(expert_block, (xs, blk_e)).reshape(p_rows, d)
    out = jnp.zeros((t, d), h.dtype).at[row_tok].add(ys * row_gate[:, None].astype(ys.dtype), mode='drop')
    return out.reshape(bsz, seq, d)

def setup_inputs(seed: int = 0) -> dict:
    key = jax.random.key(seed)
    ks = iter(jax.random.split(key, 48))
    f32 = jnp.float32

    def nrm(shape, scale):
        return jax.random.normal(next(ks), shape, f32) * scale

    def gain(shape):
        return 1.0 + nrm(shape, 0.02)

    ns, na, L = N_SSD_LAYERS, N_DA_LAYERS, DEPTH
    u = jax.random.uniform(next(ks), (ns, SSD_N_HEADS), f32)
    dt0 = jnp.exp(u * (math.log(0.1) - math.log(0.001)) + math.log(0.001))
    dt_bias = dt0 + jnp.log(-jnp.expm1(-dt0))
    a_log = jnp.log(jax.random.uniform(next(ks), (ns, SSD_N_HEADS), f32, 1.0, 16.0))
    return {
        'x': nrm((BATCH, SEQ, D_MODEL), 1.0),
        'mem': nrm((BATCH, MEM_LEN, D_MODEL), 1.0),
        'mixer_norm': gain((L, D_MODEL)),
        'xattn_norm': gain((L, D_MODEL)),
        'mem_norm': gain((L, D_MODEL)),
        'ffn_norm': gain((L, D_MODEL)),
        'ssd_w_in': nrm((ns, D_MODEL, SSD_IN_DIM), D_MODEL ** -0.5),
        'ssd_conv_w': nrm((ns, SSD_D_CONV, SSD_CONV_DIM), SSD_D_CONV ** -0.5),
        'ssd_conv_b': nrm((ns, SSD_CONV_DIM), 0.02),
        'ssd_dt_bias': dt_bias,
        'ssd_a_log': a_log,
        'ssd_d': gain((ns, SSD_N_HEADS)),
        'ssd_norm': gain((ns, SSD_D_INNER)),
        'ssd_w_out': nrm((ns, SSD_D_INNER, D_MODEL), SSD_D_INNER ** -0.5),
        'da_w_qkv': nrm((na, D_MODEL, 3 * D_MODEL), D_MODEL ** -0.5),
        'da_lambda_q1': nrm((na, DA_HEAD_DIM), 0.1),
        'da_lambda_k1': nrm((na, DA_HEAD_DIM), 0.1),
        'da_lambda_q2': nrm((na, DA_HEAD_DIM), 0.1),
        'da_lambda_k2': nrm((na, DA_HEAD_DIM), 0.1),
        'da_subln': gain((na, 2 * DA_HEAD_DIM)),
        'da_w_o': nrm((na, D_MODEL, D_MODEL), D_MODEL ** -0.5),
        'xa_w_q': nrm((L, D_MODEL, D_MODEL), D_MODEL ** -0.5),
        'xa_w_kv': nrm((L, D_MODEL, 2 * D_MODEL), D_MODEL ** -0.5),
        'xa_w_o': nrm((L, D_MODEL, D_MODEL), D_MODEL ** -0.5),
        'moe_w_router': nrm((L, D_MODEL, N_EXPERTS), D_MODEL ** -0.5),
        'moe_b_router': nrm((L, N_EXPERTS), 0.01),
        'moe_w_gate_up': nrm((L, N_EXPERTS, D_MODEL, 2 * D_FF), D_MODEL ** -0.5),
        'moe_b_gate_up': nrm((L, N_EXPERTS, 2 * D_FF), 0.02),
        'moe_w_down': nrm((L, N_EXPERTS, D_FF, D_MODEL), D_FF ** -0.5),
        'moe_b_down': nrm((L, N_EXPERTS, D_MODEL), 0.02),
        'final_norm': gain((D_MODEL,)),
    }

def reference(x, mem, mixer_norm, xattn_norm, mem_norm, ffn_norm,
              ssd_w_in, ssd_conv_w, ssd_conv_b, ssd_dt_bias, ssd_a_log, ssd_d, ssd_norm, ssd_w_out,
              da_w_qkv, da_lambda_q1, da_lambda_k1, da_lambda_q2, da_lambda_k2, da_subln, da_w_o,
              xa_w_q, xa_w_kv, xa_w_o,
              moe_w_router, moe_b_router, moe_w_gate_up, moe_b_gate_up, moe_w_down, moe_b_down,
              final_norm):
    h = x
    for i in range(DEPTH):
        hn = rms_norm(h, mixer_norm[i])
        j = i // N_MIXERS
        if i % N_MIXERS == 0:
            h = h + ssd_mixer(hn, ssd_w_in[j], ssd_conv_w[j], ssd_conv_b[j], ssd_dt_bias[j], ssd_a_log[j],
                              ssd_d[j], ssd_norm[j], ssd_w_out[j])
        else:
            h = h + diff_attention(hn, da_w_qkv[j], da_lambda_q1[j], da_lambda_k1[j], da_lambda_q2[j],
                                   da_lambda_k2[j], da_subln[j], da_w_o[j], i)
        h = h + memory_cross_attention(rms_norm(h, xattn_norm[i]), rms_norm(mem, mem_norm[i]),
                                       xa_w_q[i], xa_w_kv[i], xa_w_o[i])
        h = h + moe_ffn(rms_norm(h, ffn_norm[i]), moe_w_router[i], moe_b_router[i], moe_w_gate_up[i],
                        moe_b_gate_up[i], moe_w_down[i], moe_b_down[i])
    return rms_norm(h, final_norm)


_drawn_inputs = setup_inputs


def setup_inputs(seed=0):
    import zlib

    import numpy as np

    out = dict(_drawn_inputs(seed))
    spreads = {}
    factors = {'xattn_norm': 6.419,
     'mem_norm': 4.061,
     'moe_b_gate_up': 18.717,
     'moe_b_down': 21.455,
     'final_norm': 7.687,
     'ffn_norm': 4.194,
     'moe_b_router': 5.584}
    for name, (base, spread) in spreads.items():
        noise = np.random.default_rng([zlib.crc32(name.encode()), seed]).standard_normal(out[name].shape)
        drawn = base * np.exp(spread * noise) if base else spread * noise
        out[name] = jnp.asarray(drawn.astype(out[name].dtype))
    for name, factor in factors.items():
        out[name] = (out[name] * factor).astype(out[name].dtype)
    return out
```

```python
from contextlib import ExitStack

import concourse.bass as bass
from concourse import mybir

F32 = mybir.dt.float32
I32 = mybir.dt.int32
U32 = mybir.dt.uint32
ALU = mybir.AluOpType
ACT = mybir.ActivationFunctionType
AX_X = mybir.AxisListType.X
ds = bass.ds

P = 128
SEQ = 256
TC = SEQ // P
D = 1024
KD = D // P
DI = 2048
HEADS, HD, GROUPS, HPG = 32, 64, 4, 8
GW_ = DI // GROUPS
NCONV = 3072 // P
XH, XHD = 4, 256
NE, TOPK = 32, 4
SLOTS = 64
CHUNKS = SEQ // SLOTS
NCOL = NE * CHUNKS
DUMMY = NCOL
PAIRS = NE // 2
MAX_EXTRA = TOPK * SEQ // (SLOTS + 1)
EXTRA_PAIRS = (MAX_EXTRA + 1) // 2
EPS = 1e-5
LIMIT, ALPHA = 7.0, 1.702
WP = 4096
EP = 2048
EPIECES = 12


def build(nc, x, mem, mixer_norm, xattn_norm, mem_norm, ffn_norm, w_in, conv_w, conv_b, dt_bias, a_log,
          d_skip, ssd_norm, w_out, xa_w_q, xa_w_kv, xa_w_o, w_router, b_router, w_gate_up, b_gate_up,
          w_down, b_down, final_norm, out):
    with ExitStack() as ctx:
        def sb(name, shape, dt=F32):
            return ctx.enter_context(nc.sbuf_tensor(name, shape, dt))

        def sem(name):
            return ctx.enter_context(nc.semaphore(name))

        ring = sb("ring", [P, EPIECES * EP])
        wring = sb("wring", [P, 3 * WP])
        h = sb("h", [P, TC, D])
        xT = sb("xT", [P, KD, SEQ])
        memT = sb("memT", [P, KD, SEQ])
        kT = sb("kT", [P, KD, SEQ])
        vb = sb("vb", [P, TC, D])
        sq = sb("sq", [P, 2048])

        def part(base, first, end, r=None, **sizes):
            v = base[:, first:end]
            return v.rearrange(r, **sizes) if r else v

        zs = part(ring, 0, 4096, r="p (t n) -> p t n", t=TC)
        yb = part(ring, 4096, 8192, r="p (t n) -> p t n", t=TC)
        xd = part(ring, 8192, 12288, r="p (t n) -> p t n", t=TC)
        uT = part(ring, 12288, 16384, r="p (k s) -> p k s", k=16)
        bcT = part(ring, 16384, 18432, r="p (k s) -> p k s", k=8)
        cv = part(ring, 18432, 20480, r="p (b m s) -> p b m s", b=4, m=2)
        btok = part(ring, 18432, 18944, r="p (g n) -> p g n", g=GROUPS)
        xde = part(ring, 18944, 19456)
        ytmp = part(ring, 19456, 19968)
        cbm = part(ring, 19968, 20224, r="p (b l) -> p b l", b=2)
        mt = part(ring, 20480, 22528, r="p (b h l) -> p b h l", b=2, h=HPG)
        du = part(ring, 22528, 24576, r="p (b h l) -> p b h l", b=2, h=HPG)
        rows_a = part(ring, 20480, 20608)
        rows_b = part(ring, 20608, 20736)
        bg_rows = part(sq, 0, 512, r="p (n f) -> p n f", n=4)
        xn0 = part(ring, 4096, 6144, r="p (t n) -> p t n", t=TC)
        states = part(sq, 0, 2048, r="p (g n) -> p g n", g=GROUPS)
        xn2 = part(sq, 0, 2048, r="p (t n) -> p t n", t=TC)
        qT = part(sq, 0, 2048, r="p (k s) -> p k s", k=KD)
        pr = memT[:, :, :].rearrange("p (t h) m -> p t h m", t=TC)
        prT = kT[:, :, :].rearrange("p (h c) s -> p h c s", h=XH)
        wslot = [part(wring, WP * s, WP * (s + 1)) for s in range(3)]
        at = [0]

        def late(n, r=None, **kw):
            v = wring[:, at[0]:at[0] + n]
            at[0] += n
            return v.rearrange(r, **kw) if r else v

        xn = late(2048, "p (t n) -> p t n", t=TC)
        g_fin = late(D)
        xg = late(2 * 512, "p (j k s) -> p j k s", j=2, k=KD)
        gu = late(2 * 512, "p (g m s) -> p g m s", g=2, m=8)
        sg = late(2 * 256, "p (g m s) -> p g m s", g=2, m=4)
        act_t = late(512, "p (k s) -> p k s", k=KD)
        yT = late(1024, "p (k s) -> p k s", k=KD)
        ysb = late(1024)
        onehot = late(256, "p (j t s) -> p j t s", j=2, t=TC)
        scat = late(256, "p (t s) -> p t s", t=TC)
        scatT = late(256)
        b_dn = late(D)
        g_ffn = late(D)

        mask4 = late(2 * NCOL, "p (t c) -> p t c", t=TC)
        cst = sb("cst", [P, 4, P])
        ident, tri, stri, ones = (cst[:, n, :] for n in range(4))
        wdt = sb("wdt", [P, KD, HEADS])
        wrt = sb("wrt", [P, KD, NE])
        parT = sb("parT", [P, 160])
        convw_c, convb_c, g_mix, g_xa, g_mem, g_ssd = 0, 96, 120, 128, 136, 144
        bguT = sb("bguT", [P, NE * 16])
        small = sb("small", [P, 3, HEADS])
        b_rt = sb("b_rt", [P, NE])
        eps = sb("eps", [P, 1])
        nrm = sb("nrm", [P, 6, 2])
        rst = sb("rst", [P, 6, 2])
        dtv = sb("dtv", [P, TC, HEADS])
        dta = sb("dta", [P, TC, HEADS])
        dtb_ = sb("dtb_", [P, TC, HEADS])
        acm = sb("acm", [P, TC, HEADS])
        dec = sb("dec", [P, 2, HEADS])
        aneg = sb("aneg", [P, HEADS])
        ssu = sb("ssu", [P, 8])
        rsu = sb("rsu", [P, 8])
        att = sb("att", [P, 3, 8])
        lg = sb("lg", [P, TC, NE])
        mx8 = sb("mx8", [P, TC, 8])
        ix8 = sb("ix8", [P, TC, 8], U32)
        ix8f = sb("ix8f", [P, TC, 8])
        mask = sb("mask", [P, TC, NE])
        gate = sb("gate", [P, TC, NE])
        gsum = sb("gsum", [P, TC, 2])
        rank = sb("rank", [P, TC, NCOL + 4])
        gateT = sb("gateT", [P, SEQ])
        iota_i = sb("iota_i", [P, 64], I32)
        iota = sb("iota", [P, 64])
        col_i = sb("col_i", [P, 3], I32)
        col = sb("col", [P, 3])
        cnt = sb("cnt", [P, 3])
        pick = sb("pick", [P, 16])
        lst = sb("lst", [1, 48])
        lst_i = sb("lst_i", [1, 48], I32)

        ps = [ctx.enter_context(nc.psum_tensor(f"ps{b}", [P, 512], F32)) for b in range(8)]

        (ld_x, ld_mem, ld_rows, ld_small, ld_bg, ld_g, ld_bdn, ld_wdt, ld_wrt, cst_step, cst_done) = (
            sem(n) for n in ("ld_x", "ld_mem", "ld_rows", "ld_small", "ld_bg", "ld_g", "ld_bdn", "ld_wdt",
                             "ld_wrt", "cst_step", "cst_done"))
        w_ready = [sem(f"w_ready{s}") for s in range(3)]
        e_ready = [sem(f"e_ready{s}") for s in range(EPIECES)]
        (e_used, par_ps, par_sb, std, normed, nt_ps, nt_dve, nt_act, dt_ps, dt_e, dt_s, da_ok, ac_ps,
         u_ps, conv_done, silu_done, z_ps, z_done, xs_ps, xs_done, bt_ps, bt_sb, dec_in, dec_ok) = (
            sem(n) for n in ("e_used", "par_ps", "par_sb", "std", "normed", "nt_ps", "nt_dve",
                             "nt_act", "dt_ps", "dt_e", "dt_s", "da_ok", "ac_ps", "u_ps", "conv_done",
                             "silu_done", "z_ps", "z_done", "xs_ps", "xs_done", "bt_ps", "bt_sb", "dec_in",
                             "dec_ok"))
        (du_ok, prep_ps, diff_ok, cb_ok, exp_ok, mt_ok, main_ps, st_ok, xde_ok, y_read, u_ok, ssu_ok, kv_ps,
         kv_sb, stdu, un_ok, ut_ps, ut_dve, ut_act, wo_ps, h_ok) = (
            sem(n) for n in ("du_ok", "prep_ps", "diff_ok", "cb_ok", "exp_ok", "mt_ok", "main_ps", "st_ok",
                             "xde_ok", "y_read", "u_ok", "ssu_ok", "kv_ps", "kv_sb", "stdu", "un_ok", "ut_ps",
                             "ut_dve", "ut_act", "wo_ps", "h_ok"))
        (q_ps, q_sb, sc_ps, nmax, pexp, pn_ok, pT_ps, pT_sb, pv_ps, pv_sb) = (
            sem(n) for n in ("q_ps", "q_sb", "sc_ps", "nmax", "pexp", "pn_ok", "pT_ps", "pT_sb", "pv_ps",
                             "pv_sb"))
        (rt_ps, lmax, rexp, mask_ok, gate_ok, rank_ps, gt_ps, gt_sb, cnt_ps, val_ok, pos_ps, pick_ok, lst_ps,
         lst_ok) = (
            sem(n) for n in ("rt_ps", "lmax", "rexp", "mask_ok", "gate_ok", "rank_ps", "gt_ps", "gt_sb",
                             "cnt_ps", "val_ok", "pos_ps", "pick_ok", "lst_ps", "lst_ok"))
        (hot_ok, gathered, sc_ok, xg_ok, gu_free, gb_ok, sg_ok, av_ok, yT_ok, st_ps,
         scT_ok, yt_ps, y_dve, y_act, fin_ps, fsum, stdf, o_ok, ld_out) = (
            sem(n) for n in ("hot_ok", "gathered", "sc_ok", "xg_ok", "gu_free", "gb_ok",
                             "sg_ok", "av_ok", "yT_ok", "st_ps", "scT_ok", "yt_ps", "y_dve", "y_act",
                             "fin_ps", "fsum", "stdf", "o_ok", "ld_out"))

        def cols(w, row0, c0):
            return w[row0:row0 + D, c0:c0 + 512].rearrange("(k p) n -> p k n", p=P)

        pieces = [cols(w_in, 0, DI + DI), cols(w_in, 0, DI + DI + 512)]
        pieces += [cols(w_in, 0, DI + 512 * n) for n in range(4)]
        pieces += [cols(w_in, 0, 512 * n) for n in range(4)]
        pieces += [cols(xa_w_kv, 0, 512 * n) for n in range(4)]
        pieces += [cols(w_out, D * k, 512 * n) for k in range(2) for n in range(2)]
        pieces += [cols(xa_w_q, 0, 512 * n) for n in range(2)]
        pieces += [cols(xa_w_o, 0, 512 * n) for n in range(2)]
        W_U, W_Z, W_KV, W_OUT, W_Q, W_O = 0, 6, 10, 14, 18, 20

        def used(n):
            if n < W_Z:
                return u_ps, 2 * (n - W_U) + 2
            if n < W_KV:
                return z_ps, 2 * (n - W_Z) + 2
            if n < W_OUT:
                return kv_ps, 2 * (n - W_KV) + 2
            if n < W_Q:
                return wo_ps, n - W_OUT + 1
            return (q_ps, 2 * (n - W_Q) + 2) if n < W_O else (wo_ps, 5 + n - W_O)

        def wpiece(n):
            return wslot[n % 3].rearrange("p (k n) -> p k n", k=KD)

        gu_dram = w_gate_up.rearrange("e (k p) (a g n) -> e g a p k n", p=P, a=2, g=2)
        dn_dram = w_down.rearrange("e (k p) n -> e p k n", p=P)

        def epiece(s):
            return ring[:, EP * s:EP * (s + 1)].rearrange("p (k n) -> p k n", k=4 if s < 8 else 2)

        def load_expert_piece(sp, e, s):
            if s < 8:
                k = 4 * (s // 2 % 2)
                sp.dma_start(epiece(s), gu_dram[e, s // 4, s % 2, :, k:k + 4, :]).then_inc(e_ready[s], 16)
            else:
                k = 2 * (s - 8)
                sp.dma_start(epiece(s), dn_dram[e, :, k:k + 2, :]).then_inc(e_ready[s], 16)

        block = ctx.enter_context(nc.Block())

        @block.sync
        def _(sp):
            for t in range(TC):
                sp.dma_start(h[:, t, :], x[P * t:P * (t + 1), :]).then_inc(ld_x, 16)
            for n in range(3):
                sp.dma_start(wpiece(n), pieces[n]).then_inc(w_ready[n], 16)
            sp.dma_start(vb[:, :, :], mem.rearrange("(t p) d -> p t d", p=P)).then_inc(ld_mem, 16)
            for n in range(3, len(pieces)):
                signal, count = used(n - 3)
                sp.wait_ge(signal, count)
                sp.dma_start(wpiece(n), pieces[n]).then_inc(w_ready[n % 3], 16)
                if n == W_OUT + 4 + 2:
                    for s in range(EPIECES):
                        load_expert_piece(sp, 0, s)
            sp.wait_ge(wo_ps, 6)
            sp.dma_start(g_ffn, ffn_norm.partition_broadcast(P)).then_inc(ld_g, 16)
            sp.dma_start(g_fin, final_norm.partition_broadcast(P)).then_inc(ld_g, 16)
            sp.dma_start(b_dn[0:NE, :], b_down).then_inc(ld_bdn, 16)
            with sp.Fori(0, PAIRS - 1, 1) as i:
                for n in range(2 * EPIECES):
                    sp.wait_ge(e_used, 2 * EPIECES * i + (n + 1))
                    load_expert_piece(sp, 2 * i + (1 + n // EPIECES), n % EPIECES)
            for s in range(EPIECES):
                sp.wait_ge(e_used, (NE - 2) * EPIECES + s + 1)
                load_expert_piece(sp, NE - 1, s)
            sp.wait_ge(lst_ok, 1)
            extra = sp.value_load(lst_i[0:1, 32:33], min_val=0, max_val=MAX_EXTRA)
            with sp.Fori(0, EXTRA_PAIRS, 1) as q:
                with sp.If(extra > 2 * q):
                    for j in range(2):
                        e = sp.value_load(lst_i[0:1, ds(2 * q + (16 + j), 1)], min_val=0, max_val=NE - 1)
                        for s in range(EPIECES):
                            sp.wait_ge(e_used, 2 * EPIECES * q + (EPIECES * (NE + j - 1) + s + 1))
                            load_expert_piece(sp, e, s)
            for t in range(TC):
                sp.wait_ge(o_ok, t + 1)
                sp.dma_start(out[P * t:P * (t + 1), :], h[:, t, :]).then_inc(ld_out, 16)
            sp.wait_ge(ld_out, 16 * TC)

        @block.gpsimd
        def _(pool):
            step = [0]

            def settle(ins):
                ins.then_inc(cst_step, 1)
                step[0] += 1
                pool.wait_ge(cst_step, step[0])

            for s in (scT_ok, y_dve, y_act, yT_ok):
                pool.sem_inc(s, 1)
            pool.sem_inc(gathered, 2)
            nc.gpsimd.memset(eps[:, :], EPS)
            nc.gpsimd.memset(ident, 0.0)
            settle(nc.gpsimd.memset(cst[:, 1:4, :], 1.0))
            nc.gpsimd.affine_select(out=ident, in_=ident, compare_op=ALU.not_equal, fill=1.0, base=0,
                                    pattern=[[-1, P]], channel_multiplier=1)
            nc.gpsimd.affine_select(out=tri, in_=tri, compare_op=ALU.is_ge, fill=0.0, base=0,
                                    pattern=[[1, P]], channel_multiplier=-1)
            settle(nc.gpsimd.affine_select(out=stri, in_=stri, compare_op=ALU.is_gt, fill=0.0, base=0,
                                           pattern=[[1, P]], channel_multiplier=-1))
            settle(nc.gpsimd.iota(iota_i[:, :], pattern=[[1, 64]], base=0, channel_multiplier=0))
            for chunk in range(CHUNKS):
                r = slice(NE * chunk, NE * (chunk + 1))
                settle(nc.gpsimd.iota(col_i[r, 0:1], pattern=[[0, 1]], base=NE * chunk - DUMMY, channel_multiplier=1))
                settle(nc.gpsimd.iota(col_i[r, 1:2], pattern=[[0, 1]], base=0, channel_multiplier=1))
                least = SLOTS * chunk if chunk else 2 * SEQ
                settle(nc.gpsimd.iota(col_i[r, 2:3], pattern=[[0, 1]], base=least, channel_multiplier=0))
            nc.gpsimd.tensor_copy(iota[:, :], iota_i[:, :])
            nc.gpsimd.tensor_copy(col[:, :], col_i[:, :]).then_inc(cst_done, 1)
            pool.wait_ge(da_ok, 1)
            for i in range(2 * GROUPS):
                g, c = i // 2, i % 2
                if i >= 2:
                    pool.wait_ge(prep_ps, i - 1)
                a = dta[:, c, HPG * g:HPG * (g + 1)]
                nc.gpsimd.tensor_tensor(du[:, i % 2, :, :], tri.unsqueeze(1).to_broadcast([P, HPG, P]),
                                        a.unsqueeze(2).to_broadcast([P, HPG, P]), ALU.mult).then_inc(du_ok, 1)

        @block.tensor
        def _(pe):
            mm, tr = nc.tensor.matmul, nc.tensor.transpose

            def take(n):
                pe.wait_ge(w_ready[n % 3], 16 * (n // 3 + 1))
                return wpiece(n)

            pe.wait_ge(cst_done, 1)
            pe.wait_ge(ld_rows, 96)
            tr(ps[7][:, 0:120], rows_a[0:120, :], ident[0:120, 0:120])
            tr(ps[7][:, 128:168], rows_b[0:40, :], ident[0:40, 0:40]).then_inc(par_ps, 1)

            def norm_transposes(n, src):
                pe.wait_ge(normed, 2 * n + 2)
                for b in range(4):
                    for k in (2 * b, 2 * b + 1):
                        for t in range(TC):
                            at_ = (k % 2) * SEQ + t * P
                            last = tr(ps[b][:, at_:at_ + P], src[:, t, k * P:(k + 1) * P], ident)
                    last.then_inc(nt_ps, 1)

            def await_nt(n):
                pe.wait_ge(nt_dve, 4 * n + 4)
                pe.wait_ge(nt_act, 4 * n + 4)

            norm_transposes(0, xn0)
            pe.wait_ge(ld_bg, 16)
            for n in range(4):
                last = tr(ps[5][:, n * P:(n + 1) * P], bg_rows[:, n, :], ident)
            last.then_inc(par_ps, 1)
            await_nt(0)
            pe.wait_ge(ld_wdt, 16)
            for t in range(TC):
                for k in range(KD):
                    last = mm(ps[6][:, HEADS * t:HEADS * (t + 1)], xT[:, k, P * t:P * (t + 1)], wdt[:, k, :],
                              start=k == 0, stop=k == KD - 1)
            last.then_inc(dt_ps, 1)

            def project_T(n, banks, src, done, guard):
                w = take(n)
                for b in range(2):
                    guard(b)
                    for m in range(2):
                        for k in range(KD):
                            c0 = (2 * b + m) * P
                            last = mm(ps[banks[b]][:, SEQ * m:SEQ * (m + 1)], w[:, k, c0:c0 + P], src[:, k, :],
                                      start=k == 0, stop=k == KD - 1)
                    last.then_inc(done, 1)

            for p in range(6):
                project_T(W_U + p, (2 * (p % 2), 2 * (p % 2) + 1), xT, u_ps,
                          lambda b: pe.wait_ge(conv_done, 2 * (p - 2) + b + 1) if p >= 2 else None)
            pe.wait_ge(conv_done, 12)
            norm_transposes(1, vb)
            for q in range(4):
                w = take(W_Z + q)
                for t in range(TC):
                    if q >= 2:
                        pe.wait_ge(z_done, 2 * (q - 2) + t + 1)
                    elif q == 0 and t == 0:
                        await_nt(1)
                    for k in range(KD):
                        last = mm(ps[2 * (q % 2) + t][:, :], xT[:, k, P * t:P * (t + 1)], w[:, k, :],
                                  start=k == 0, stop=k == KD - 1)
                    last.then_inc(z_ps, 1)
                pe.wait_ge(silu_done, 2 * q + 6)
                for t in range(TC):
                    if q >= 1:
                        pe.wait_ge(xs_done, 2 * (q - 1) + t + 1)
                    elif t == 1:
                        pe.wait_ge(par_sb, 2)
                    for m in range(4):
                        last = tr(ps[4 + t][:, P * m:P * (m + 1)], uT[:, 4 * q + m, P * t:P * (t + 1)], ident)
                    last.then_inc(xs_ps, 1)
            for g in range(GROUPS):
                last = tr(ps[7][:, P * g:P * (g + 1)], bcT[:, g, 0:P], ident)
            last.then_inc(bt_ps, 1)
            pe.wait_ge(da_ok, 1)
            for c in range(TC):
                mm(ps[6][:, 32 * c:32 * c + 32], tri, dta[:, c, :], start=True, stop=True)
            mm(ps[6][:, 64:96], ones, dta[:, 0, :], start=True, stop=True).then_inc(ac_ps, 1)

            def prep(i):
                g, c = i // 2, i % 2
                pe.wait_ge(du_ok, i + 1)
                if i:
                    pe.wait_ge(diff_ok, i)
                    pe.wait_ge(cb_ok, i)
                else:
                    pe.wait_ge(z_done, 8)
                    pe.wait_ge(xs_done, 8)
                for b in range(2):
                    mm(ps[2 + b][:, :], ones, du[:, i % 2, 4 * b:4 * b + 4, :], start=True, stop=True)
                mm(ps[4][:, 0:P], bcT[:, g, P * c:P * (c + 1)], bcT[:, 4 + g, P * c:P * (c + 1)],
                   start=True, stop=True).then_inc(prep_ps, 1)

            def keys_values(i):
                n, half = W_KV + i // 2, i % 2
                w = take(n)
                if i >= 2:
                    pe.wait_ge(kv_sb, i - 1)
                if i < 4:
                    for m in range(2):
                        for k in range(KD):
                            c0 = (2 * half + m) * P
                            last = mm(ps[i % 2][:, SEQ * m:SEQ * (m + 1)], w[:, k, c0:c0 + P], memT[:, k, :],
                                      start=k == 0, stop=k == KD - 1)
                else:
                    for k in range(KD):
                        last = mm(ps[i % 2][:, :], memT[:, k, P * half:P * (half + 1)], w[:, k, :],
                                  start=k == 0, stop=k == KD - 1)
                last.then_inc(kv_ps, 1)

            def scan(i):
                g, c = i // 2, i % 2
                pe.wait_ge(mt_ok, i + 1)
                if i:
                    pe.wait_ge(y_read, i)
                for j in range(HPG):
                    c0 = GW_ * g + HD * j
                    last = mm(ps[5][:, HD * j:HD * (j + 1)], mt[:, i % 2, j, :], xd[:, c, c0:c0 + HD],
                              start=True, stop=True)
                if c == 0:
                    pe.wait_ge(xde_ok, g + 1)
                    pe.wait_ge(bt_sb, 1)
                    if g == 0:
                        pe.wait_ge(dec_in, 1)
                    mm(ps[6][:, :], btok[:, g, :], xde, start=True, stop=True).then_inc(main_ps, 1)
                else:
                    pe.wait_ge(st_ok, g + 1)
                    mm(ps[6][:, :], bcT[:, 4 + g, P:2 * P], states[:, g, :], start=True,
                       stop=True).then_inc(main_ps, 1)

            prep(0)
            for i in range(2 * GROUPS):
                keys_values(i)
                if i + 1 < 2 * GROUPS:
                    prep(i + 1)
                scan(i)
            pe.wait_ge(kv_sb, 8)
            pe.wait_ge(diff_ok, 8)
            for j in range(8):
                pe.wait_ge(un_ok, 2 * (j // 2) + 2)
                if j >= 4:
                    pe.wait_ge(ut_dve if j % 2 == 0 else ut_act, (j - 4) // 2 + 1)
                for k in (2 * j, 2 * j + 1):
                    for t in range(TC):
                        at_ = (k % 2) * SEQ + t * P
                        last = tr(ps[j % 4][:, at_:at_ + P], yb[:, t, k * P:(k + 1) * P], ident)
                last.then_inc(ut_ps, 1)
            pe.wait_ge(y_read, 8)
            for kh in range(2):
                pe.wait_ge(ut_dve, 2 * kh + 2)
                pe.wait_ge(ut_act, 2 * kh + 2)
                for n in range(2):
                    w = take(W_OUT + 2 * kh + n)
                    for t in range(TC):
                        for k in range(KD):
                            last = mm(ps[4 + 2 * n + t][:, :], uT[:, KD * kh + k, P * t:P * (t + 1)],
                                      w[:, k, :], start=kh == 0 and k == 0, stop=kh == 1 and k == KD - 1)
                    last.then_inc(wo_ps, 1)

            norm_transposes(2, xn2)
            await_nt(2)
            for a in range(2):
                project_T(W_Q + a, (4 + 2 * a, 5 + 2 * a), xT, q_ps, lambda b: None)
            for hd in range(XH):
                pe.wait_ge(q_sb, hd + 1)
                for t in range(TC):
                    for kk in (2 * hd, 2 * hd + 1):
                        last = mm(ps[hd][:, SEQ * t:SEQ * (t + 1)], qT[:, kk, P * t:P * (t + 1)], kT[:, kk, :],
                                  start=kk == 2 * hd, stop=kk == 2 * hd + 1)
                last.then_inc(sc_ps, 1)
            for hd in range(XH):
                pe.wait_ge(pn_ok, 2 * hd + 2)
                for mc in range(2):
                    for t in range(TC):
                        at_ = mc * SEQ + t * P
                        last = tr(ps[4 + hd][:, at_:at_ + P], pr[:, t, hd, P * mc:P * (mc + 1)], ident)
                last.then_inc(pT_ps, 1)
            for hd in range(XH):
                pe.wait_ge(pT_sb, hd + 1)
                for dv in range(2):
                    for mc in range(2):
                        c0 = XHD * hd + P * dv
                        last = mm(ps[hd][:, SEQ * dv:SEQ * (dv + 1)], vb[:, mc, c0:c0 + P], prT[:, hd, mc, :],
                                  start=mc == 0, stop=mc == 1)
                last.then_inc(pv_ps, 1)
            pe.wait_ge(pv_sb, XH)
            for n in range(2):
                w = take(W_O + n)
                for t in range(TC):
                    for k in range(KD):
                        last = mm(ps[4 + 2 * n + t][:, :], xT[:, k, P * t:P * (t + 1)], w[:, k, :],
                                  start=k == 0, stop=k == KD - 1)
                last.then_inc(wo_ps, 1)

            norm_transposes(3, xn)
            for n in range(2):
                for t in range(TC):
                    last = mm(ps[4 + 2 * n + t][:, :], ident, h[:, t, 512 * n:512 * (n + 1)], start=True,
                              stop=False)
            await_nt(3)
            pe.wait_ge(ld_wrt, 16)
            for t in range(TC):
                for k in range(KD):
                    last = mm(ps[0][:, NE * t:NE * (t + 1)], xT[:, k, P * t:P * (t + 1)], wrt[:, k, :],
                              start=k == 0, stop=k == KD - 1)
            last.then_inc(rt_ps, 1)
            pe.wait_ge(mask_ok, 1)
            mm(ps[1][:, 0:NE], stri, mask[:, 0, :], start=True, stop=True)
            mm(ps[1][:, NE:2 * NE], stri, mask[:, 1, :], start=True, stop=False)
            mm(ps[1][:, NE:2 * NE], ones, mask[:, 0, :], start=False, stop=True).then_inc(rank_ps, 1)
            for t in range(TC):
                last = mm(ps[2][:, 0:1], mask4[:, t, :], ones[:, 0:1], start=t == 0, stop=t == TC - 1)
            last.then_inc(cnt_ps, 1)
            pe.wait_ge(val_ok, 1)
            mm(ps[2][:, 2:3], stri, cnt[:, 0:1], start=True, stop=True).then_inc(pos_ps, 1)
            pe.wait_ge(pick_ok, 1)
            mm(ps[3][0:1, 0:16], col[:, 0:1], pick[:, :], start=True, stop=True)
            mm(ps[3][0:1, 16:32], col[:, 1:2], pick[:, :], start=True, stop=True)
            mm(ps[3][0:1, 32:33], cnt[:, 0:1], ones[:, 0:1], start=True, stop=True).then_inc(lst_ps, 1)
            pe.wait_ge(gate_ok, 1)
            for t in range(TC):
                last = tr(ps[0][0:NE, P * t:P * (t + 1)], gate[:, t, :], ident)
            last.then_inc(gt_ps, 1)
            pe.wait_ge(gt_sb, 1)
            pe.wait_ge(lst_ok, 1)

            def expert_round(i):
                def gather(j):
                    pe.wait_ge(hot_ok, 2 * i + (j + 1))
                    if j == 0:
                        pe.wait_ge(scT_ok, i + 1)
                    else:
                        pe.wait_ge(xg_ok, 2 * i + 1)
                    for k in range(KD):
                        for t in range(TC):
                            last = mm(ps[2][:, SLOTS * k:SLOTS * (k + 1)], xn[:, t, P * k:P * (k + 1)],
                                      onehot[:, j, t, :], start=t == 0, stop=t == TC - 1)
                    last.then_inc(gathered, 1)

                def gate_up(j):
                    pe.wait_ge(xg_ok, 2 * i + (j + 1))
                    for g in range(2):
                        if j == 0 and g == 0:
                            pe.wait_ge(y_dve, i + 1)
                        elif j == 0:
                            pe.wait_ge(y_act, i + 1)
                        else:
                            pe.wait_ge(gu_free, 4 * i + (g + 1))
                        for s in range(4 * g, 4 * g + 4):
                            pe.wait_ge(e_ready[s], 32 * i + 16 * (j + 1))
                            w = epiece(s)
                            a = s % 2
                            for kk in range(4):
                                k = 4 * (s // 2 % 2) + kk
                                for m in range(4):
                                    c0 = (4 * a + m) * SLOTS
                                    last = mm(ps[g][:, c0:c0 + SLOTS], w[:, kk, P * m:P * (m + 1)],
                                              xg[:, j, k, :], start=k == 0 and a == 0 and m == 0,
                                              stop=k == KD - 1, skip_group_check=True)
                            last.then_inc(e_used, 1)

                def down(j):
                    if j == 0:
                        pe.wait_ge(yT_ok, 2 * i + 1)
                    else:
                        pe.wait_ge(yT_ok, 2 * i + 2)
                    for s in range(8, EPIECES):
                        if s % 2 == 0:
                            pe.wait_ge(av_ok, 4 * i + (2 * j + (s - 8) // 2 + 1))
                        pe.wait_ge(e_ready[s], 32 * i + 16 * (j + 1))
                        w = epiece(s)
                        for kk in range(2):
                            k = 2 * (s - 8) + kk
                            for m in range(KD):
                                last = mm(ps[3][:, SLOTS * m:SLOTS * (m + 1)], w[:, kk, P * m:P * (m + 1)],
                                          act_t[:, k, :], start=k == 0 and m == 0, stop=k == KD - 1,
                                          skip_group_check=True)
                        last.then_inc(e_used, 1)

                gather(0)
                gate_up(0)
                gather(1)
                down(0)
                pe.wait_ge(sc_ok, i + 1)
                pe.wait_ge(xg_ok, 2 * i + 2)
                for t in range(TC):
                    last = tr(ps[2][:, P * t:P * (t + 1)], scat[:, t, :], ident)
                last.then_inc(st_ps, 1)
                gate_up(1)
                down(1)
                pe.wait_ge(yT_ok, 2 * i + 3)
                for n in range(2):
                    for k in range(4):
                        last = tr(ps[n][:, P * k:P * (k + 1)], yT[:, 4 * n + k, :], ident)
                    last.then_inc(yt_ps, 1)
                pe.wait_ge(scT_ok, i + 2)
                for n in range(2):
                    if n == 0:
                        pe.wait_ge(y_dve, i + 2)
                    else:
                        pe.wait_ge(y_act, i + 2)
                    for t in range(TC):
                        last = mm(ps[4 + 2 * n + t][:, :], scatT[:, P * t:P * (t + 1)],
                                  ysb[:, 512 * n:512 * (n + 1)], start=False, stop=False,
                                  skip_group_check=True)

            with pe.Fori(0, PAIRS, 1) as i:
                expert_round(i)
            extra = pe.value_load(lst_i[0:1, 32:33], min_val=0, max_val=MAX_EXTRA)
            with pe.Fori(PAIRS, PAIRS + EXTRA_PAIRS, 1) as i:
                with pe.If(extra > 2 * i - 2 * PAIRS):
                    expert_round(i)
            pe.wait_ge(ld_bdn, 16)
            for t in range(TC):
                for n in range(2):
                    last = mm(ps[4 + 2 * n + t][:, :], gateT[0:NE, P * t:P * (t + 1)],
                              b_dn[0:NE, 512 * n:512 * (n + 1)], start=False, stop=True)
                last.then_inc(fin_ps, 1)

        @block.scalar
        def _(act):
            def fn(out_, in_, func, **kw):
                return nc.scalar.activation(out_, in_, func, **kw)

            act.dma_start(rows_a[0:96, :], conv_w.rearrange("j (c p) -> (j c) p", p=P)).then_inc(ld_rows, 16)
            act.dma_start(rows_a[96:120, :], conv_b.rearrange("(c p) -> c p", p=P)).then_inc(ld_rows, 16)
            for r0, v in ((0, mixer_norm), (8, xattn_norm), (16, mem_norm), (24, ssd_norm)):
                n = v.shape[0] // P
                act.dma_start(rows_b[r0:r0 + n, :], v.rearrange("(c p) -> c p", p=P)).then_inc(ld_rows, 16)
            for n, v in enumerate((dt_bias, a_log, d_skip)):
                act.dma_start(small[:, n, :], v.partition_broadcast(P)).then_inc(ld_small, 16)
            act.dma_start(b_rt[:, :], b_router.partition_broadcast(P)).then_inc(ld_small, 16)
            act.dma_start(wdt[:, :, :], w_in[:, 5120:5152].rearrange("(k p) n -> p k n", p=P)).then_inc(ld_wdt, 16)
            act.dma_start(bg_rows, b_gate_up.rearrange("e (f q) -> (e f) q", q=P).rearrange(
                "(n p) q -> p n q", p=P)).then_inc(ld_bg, 16)
            act.dma_start(wrt[:, :, :], w_router.rearrange("(k p) n -> p k n", p=P)).then_inc(ld_wrt, 16)

            def norm_stats(n, src, junk):
                for t in range(TC):
                    fn(junk[:, t, :], src[:, t, :], ACT.Square, accum_out=nrm[:, n, t:t + 1])
                act.drain()
                fn(nrm[:, n, :], nrm[:, n, :], ACT.Sqrt, bias=eps[:, 0:1], scale=1.0 / D).then_inc(std, 1)

            def norm_out(n, dst, gains):
                for k in range(4, KD):
                    act.wait_ge(nt_ps, 4 * n + k // 2 + 1)
                    src = ps[k // 2][:, SEQ * (k % 2):SEQ * (k % 2 + 1)]
                    scale = 1.0 if gains is None else parT[:, gains + k:gains + k + 1]
                    fn(dst[:, k, :], src, ACT.Copy, scale=scale).then_inc(nt_act, 1)

            act.wait_ge(cst_done, 1)
            act.wait_ge(ld_x, 32)
            norm_stats(0, h, xn0)
            act.wait_ge(ld_mem, 16)
            norm_stats(1, vb, part(ring, 8192, 10240, r="p (t n) -> p t n", t=TC))
            act.wait_ge(ld_small, 64)
            fn(aneg[:, :], small[:, 1, :], ACT.Exp)
            act.wait_ge(par_sb, 1)
            norm_out(0, xT, g_mix)
            act.wait_ge(dt_e, 1)
            fn(dta[:, :, :], dta[:, :, :], ACT.Exp).then_inc(dt_s, 1)
            for n in range(12):
                act.wait_ge(conv_done, n + 1)
                p, b = n // 2, n % 2
                dst = bcT[:, 4 * p + 2 * b:4 * p + 2 * b + 2, :] if p < 2 else \
                    uT[:, 4 * (p - 2) + 2 * b:4 * (p - 2) + 2 * b + 2, :]
                fn(dst, cv[:, n % 4, :, :], ACT.Silu).then_inc(silu_done, 1)
            norm_out(1, memT, g_mem)
            for n in range(8):
                q, t = n // 2, n % 2
                act.wait_ge(z_ps, n + 1)
                fn(zs[:, t, 512 * q:512 * (q + 1)], ps[2 * (q % 2) + t][:, :], ACT.Silu).then_inc(z_done, 1)
            act.wait_ge(bt_ps, 1)
            act.drain()
            fn(btok, ps[7][:, :].rearrange("p (g n) -> p g n", g=GROUPS), ACT.Copy).then_inc(bt_sb, 1)
            act.wait_ge(dec_in, 1)
            fn(dec[:, :, :], dec[:, :, :], ACT.Exp).then_inc(dec_ok, 1)

            def square_u(i):
                g, c = i // 2, i % 2
                u = slice(GW_ * g, GW_ * (g + 1))
                act.wait_ge(u_ok, i + 1)
                fn(zs[:, c, u], yb[:, c, u], ACT.Square, accum_out=ssu[:, i:i + 1])

            def state_out(i):
                if i % 2 == 0:
                    act.wait_ge(main_ps, i + 1)
                    fn(states[:, i // 2, :], ps[6][:, :], ACT.Copy).then_inc(st_ok, 1)

            for i in range(2 * GROUPS):
                act.wait_ge(diff_ok, i + 1)
                fn(mt[:, i % 2, :, :], mt[:, i % 2, :, :], ACT.Exp).then_inc(exp_ok, 1)
                act.wait_ge(kv_ps, i + 1)
                src = ps[i % 2][:, :]
                if i < 4:
                    fn(kT[:, 2 * i:2 * i + 2, :], src.rearrange("p (m s) -> p m s", m=2),
                       ACT.Copy).then_inc(kv_sb, 1)
                else:
                    n = (i - 4) // 2
                    fn(vb[:, i % 2, 512 * n:512 * (n + 1)], src, ACT.Copy).then_inc(kv_sb, 1)
                if i:
                    state_out(i - 1)
                    square_u(i - 1)
            square_u(2 * GROUPS - 1)
            act.drain()
            fn(rsu[:, :], ssu[:, :], ACT.Sqrt, bias=eps[:, 0:1], scale=1.0 / GW_).then_inc(stdu, 1)
            for j in range(1, 8, 2):
                act.wait_ge(ut_ps, j + 1)
                for k in (2 * j, 2 * j + 1):
                    last = fn(uT[:, k, :], ps[j % 4][:, SEQ * (k % 2):SEQ * (k % 2 + 1)], ACT.Copy,
                              scale=parT[:, g_ssd + k:g_ssd + k + 1])
                last.then_inc(ut_act, 1)

            act.wait_ge(h_ok, 4)
            norm_stats(2, h, xn2)
            norm_out(2, xT, g_xa)
            for b in range(4):
                act.wait_ge(q_ps, b + 1)
                fn(qT[:, 2 * b:2 * b + 2, :], ps[4 + b][:, :].rearrange("p (m s) -> p m s", m=2), ACT.Copy,
                   scale=XHD ** -0.5).then_inc(q_sb, 1)
            for hd in range(XH):
                act.wait_ge(nmax, hd + 1)
                for t in range(TC):
                    n = 2 * hd + t
                    last = fn(pr[:, t, hd, :], ps[hd][:, SEQ * t:SEQ * (t + 1)], ACT.Exp,
                              bias=att[:, 0, n:n + 1], accum_out=att[:, 1, n:n + 1])
                last.then_inc(pexp, 1)
            for hd in range(XH):
                act.wait_ge(pv_ps, hd + 1)
                fn(xT[:, 2 * hd:2 * hd + 2, :], ps[hd][:, :].rearrange("p (m s) -> p m s", m=2),
                   ACT.Copy).then_inc(pv_sb, 1)

            act.wait_ge(h_ok, 8)
            norm_stats(3, h, xn)
            norm_out(3, xT, None)
            act.wait_ge(lmax, 1)
            for t in range(TC):
                last = fn(gate[:, t, :], lg[:, t, :], ACT.Exp, bias=gsum[:, t, 0:1])
            last.then_inc(rexp, 1)

            def expert_round(i):
                def tokens(j):
                    act.wait_ge(gathered, 2 * i + (j + 3))
                    fn(xg[:, j, :, :], ps[2][:, :].rearrange("p (k s) -> p k s", k=KD),
                       ACT.Copy).then_inc(xg_ok, 1)

                def sigmoids(j):
                    for g in range(2):
                        act.wait_ge(gb_ok, 4 * i + (2 * j + g + 1))
                        fn(sg[:, g, :, :], gu[:, g, 0:4, :], ACT.Sigmoid, scale=ALPHA).then_inc(sg_ok, 1)

                def down_out(j):
                    act.wait_ge(e_used, 2 * EPIECES * i + EPIECES * (j + 1))
                    fn(yT[:, :, SLOTS * j:SLOTS * (j + 1)], ps[3][:, :].rearrange("p (k s) -> p k s", k=KD),
                       ACT.Copy).then_inc(yT_ok, 1)

                tokens(0)
                sigmoids(0)
                tokens(1)
                down_out(0)
                sigmoids(1)
                down_out(1)
                act.wait_ge(yt_ps, 2 * i + 2)
                fn(ysb[:, 512:1024], ps[1][:, :], ACT.Copy).then_inc(y_act, 1)

            with act.Fori(0, PAIRS, 1) as i:
                expert_round(i)
            act.wait_ge(lst_ok, 1)
            extra = act.value_load(lst_i[0:1, 32:33], min_val=0, max_val=MAX_EXTRA)
            with act.Fori(PAIRS, PAIRS + EXTRA_PAIRS, 1) as i:
                with act.If(extra > 2 * i - 2 * PAIRS):
                    expert_round(i)
            act.wait_ge(fin_ps, 2)
            for t in range(TC):
                for n in range(2):
                    last = fn(xn[:, t, 512 * n:512 * (n + 1)], ps[4 + 2 * n + t][:, :], ACT.Square,
                              accum_out=nrm[:, 4 + t, n:n + 1])
            last.then_inc(fsum, 1)
            act.wait_ge(fsum, 2)
            fn(rst[:, 4, :], rst[:, 4, :], ACT.Sqrt, bias=eps[:, 0:1], scale=1.0 / D).then_inc(stdf, 1)

        @block.vector
        def _(dve):
            v = nc.vector
            dve.wait_ge(par_ps, 1)
            v.tensor_copy(parT[:, 0:120], ps[7][:, 0:120])
            v.tensor_copy(parT[:, 120:160], ps[7][:, 128:168]).then_inc(par_sb, 1)

            def norm(n, dst, src):
                dve.wait_ge(std, n + 1)
                v.reciprocal(rst[:, n, :], nrm[:, n, :])
                dve.drain()
                for t in range(TC):
                    v.tensor_scalar(dst[:, t, :], src[:, t, :], rst[:, n, t:t + 1], None,
                                    ALU.mult).then_inc(normed, 1)

            def norm_out(n, dst, gains):
                for k in range(4):
                    dve.wait_ge(nt_ps, 4 * n + k // 2 + 1)
                    src = ps[k // 2][:, SEQ * (k % 2):SEQ * (k % 2 + 1)]
                    if gains is None:
                        v.tensor_copy(dst[:, k, :], src).then_inc(nt_dve, 1)
                    else:
                        v.tensor_scalar(dst[:, k, :], src, parT[:, gains + k:gains + k + 1], None,
                                        ALU.mult).then_inc(nt_dve, 1)

            norm(0, xn0, h)
            norm_out(0, xT, g_mix)
            dve.wait_ge(par_ps, 2)
            v.tensor_copy(bguT[:, :], ps[5][:, :]).then_inc(par_sb, 1)
            dve.wait_ge(dt_ps, 1)
            dve.wait_ge(ld_small, 64)
            v.tensor_tensor(dtv[:, :, :], ps[6][:, 0:64].rearrange("p (t n) -> p t n", t=TC),
                            small[:, 0, :].unsqueeze(1).to_broadcast([P, TC, HEADS]), ALU.add)
            dve.drain()
            v.tensor_scalar(dta[:, :, :], dtv[:, :, :], 0.0, None, ALU.min)
            dve.drain()
            v.tensor_scalar(dtv[:, :, :], dtv[:, :, :], 0.0, None, ALU.max)
            dve.drain()
            v.tensor_tensor(dta[:, :, :], dta[:, :, :], dtv[:, :, :], ALU.subtract).then_inc(dt_e, 1)
            dve.wait_ge(dt_s, 1)
            v.tensor_scalar(dtb_[:, :, :], dta[:, :, :], 2.0, None, ALU.add)
            dve.drain()
            v.reciprocal(dtb_[:, :, :], dtb_[:, :, :])
            dve.drain()
            v.tensor_tensor(dta[:, :, :], dta[:, :, :], dtb_[:, :, :], ALU.mult)
            dve.drain()
            v.tensor_tensor(dtb_[:, :, :], dta[:, :, :], dta[:, :, :], ALU.mult)
            dve.drain()
            v.tensor_scalar(acm[:, :, :], dtb_[:, :, :], 1.0 / 17, None, ALU.mult)
            for n in (15, 13, 11, 9, 7, 5, 3):
                dve.drain()
                v.scalar_tensor_tensor(out=acm[:, :, :], in0=acm[:, :, :], scalar=1.0 / n, in1=dtb_[:, :, :],
                                       op0=ALU.add, op1=ALU.mult)
            dve.drain()
            v.scalar_tensor_tensor(out=dta[:, :, :], in0=acm[:, :, :], scalar=1.0, in1=dta[:, :, :],
                                   op0=ALU.add, op1=ALU.mult)
            dve.drain()
            v.scalar_tensor_tensor(out=dtv[:, :, :], in0=dta[:, :, :], scalar=2.0, in1=dtv[:, :, :],
                                   op0=ALU.mult, op1=ALU.add)
            dve.drain()
            for t in range(TC):
                last = v.scalar_tensor_tensor(out=dta[:, t, :], in0=dtv[:, t, :], scalar=-1.0, in1=aneg[:, :],
                                              op0=ALU.mult, op1=ALU.mult)
            last.then_inc(da_ok, 1)
            norm(1, vb, vb)

            for n in range(12):
                p, b = n // 2, n % 2
                c0 = (16 + 4 * p if p < 2 else 4 * (p - 2)) + 2 * b
                dve.wait_ge(u_ps, n + 1)
                if n >= 4:
                    dve.wait_ge(silu_done, n - 3)
                for m in range(2):
                    w = convw_c + 3 * NCONV + c0 + m
                    v.tensor_scalar(cv[:, n % 4, m, :], ps[2 * (p % 2) + b][:, SEQ * m:SEQ * (m + 1)],
                                    parT[:, w:w + 1], parT[:, convb_c + c0 + m:convb_c + c0 + m + 1],
                                    ALU.mult, ALU.add)
                for j in (2, 1, 0):
                    dve.drain()
                    for m in range(2):
                        w = convw_c + j * NCONV + c0 + m
                        back = 3 - j
                        src = ps[2 * (p % 2) + b][:, SEQ * m:SEQ * (m + 1) - back]
                        last = v.scalar_tensor_tensor(out=cv[:, n % 4, m, back:], in0=src,
                                                      scalar=parT[:, w:w + 1], in1=cv[:, n % 4, m, back:],
                                                      op0=ALU.mult, op1=ALU.add)
                last.then_inc(conv_done, 1)
            norm_out(1, memT, g_mem)

            def by_head(ap):
                return ap.rearrange("p (j d) -> p j d", d=HD)

            def spread(ap):
                return ap.unsqueeze(2).to_broadcast([P, HPG, HD])

            for n in range(8):
                q, t = n // 2, n % 2
                hs, cs = slice(HPG * q, HPG * (q + 1)), slice(GW_ * q, GW_ * (q + 1))
                dve.wait_ge(xs_ps, n + 1)
                v.tensor_tensor(by_head(xd[:, t, cs]), by_head(ps[4 + t][:, :]), spread(dtv[:, t, hs]), ALU.mult)
                v.tensor_tensor(by_head(yb[:, t, cs]), by_head(ps[4 + t][:, :]), spread(small[:, 2, hs]),
                                ALU.mult).then_inc(xs_done, 1)
            dve.wait_ge(ac_ps, 1)
            v.tensor_copy(acm[:, :, :], ps[6][:, 0:64].rearrange("p (t n) -> p t n", t=TC))
            dve.drain()
            v.tensor_copy(dec[:, 1, :], acm[:, 1, :])
            v.tensor_tensor(dec[:, 0, :], ps[6][:, 64:96], acm[:, 0, :], ALU.subtract).then_inc(dec_in, 1)

            def decays(i):
                g, c = i // 2, i % 2
                dve.wait_ge(prep_ps, i + 1)
                v.tensor_tensor(cbm[:, i % 2, :], ps[4][:, 0:P], tri, ALU.mult).then_inc(cb_ok, 1)
                for j in range(HPG):
                    hcol = HPG * g + j
                    last = v.tensor_scalar(mt[:, i % 2, j, :], ps[2 + j // 4][:, P * (j % 4):P * (j % 4 + 1)],
                                           acm[:, c, hcol:hcol + 1], 0.0, ALU.subtract, ALU.min)
                last.then_inc(diff_ok, 1)

            decays(0)
            for i in range(2 * GROUPS):
                g, c = i // 2, i % 2
                gs, hs = slice(GW_ * g, GW_ * (g + 1)), slice(HPG * g, HPG * (g + 1))
                if c == 0:
                    dve.wait_ge(dec_ok, 1)
                    v.tensor_tensor(by_head(xde), by_head(xd[:, 0, gs]), spread(dec[:, 0, hs]),
                                    ALU.mult).then_inc(xde_ok, 1)
                dve.wait_ge(exp_ok, i + 1)
                v.tensor_tensor(mt[:, i % 2, :, :], mt[:, i % 2, :, :],
                                cbm[:, i % 2, :].unsqueeze(1).to_broadcast([P, HPG, P]), ALU.mult).then_inc(mt_ok, 1)
                if i + 1 < 2 * GROUPS:
                    decays(i + 1)
                dve.wait_ge(main_ps, i + 1)
                if c == 1:
                    v.tensor_tensor(by_head(ytmp), by_head(ps[6][:, :]), spread(dec[:, 1, hs]), ALU.mult)
                v.tensor_tensor(yb[:, c, gs], yb[:, c, gs], ps[5][:, :], ALU.add).then_inc(y_read, 1)
                if c == 1:
                    dve.drain()
                    v.tensor_tensor(yb[:, c, gs], yb[:, c, gs], ytmp, ALU.add)
                dve.drain()
                v.tensor_tensor(yb[:, c, gs], yb[:, c, gs], zs[:, c, gs], ALU.mult).then_inc(u_ok, 1)
            dve.wait_ge(stdu, 1)
            v.reciprocal(rsu[:, :], rsu[:, :])
            dve.drain()
            for i in range(2 * GROUPS):
                g, c = i // 2, i % 2
                gs = slice(GW_ * g, GW_ * (g + 1))
                v.tensor_scalar(yb[:, c, gs], yb[:, c, gs], rsu[:, i:i + 1], None, ALU.mult).then_inc(un_ok, 1)
            for j in range(0, 8, 2):
                dve.wait_ge(ut_ps, j + 1)
                for k in (2 * j, 2 * j + 1):
                    last = v.tensor_scalar(uT[:, k, :], ps[j % 4][:, SEQ * (k % 2):SEQ * (k % 2 + 1)],
                                           parT[:, g_ssd + k:g_ssd + k + 1], None, ALU.mult)
                last.then_inc(ut_dve, 1)

            def add_out(first):
                for n in range(2):
                    dve.wait_ge(wo_ps, first + n)
                    for t in range(TC):
                        r = h[:, t, 512 * n:512 * (n + 1)]
                        v.tensor_tensor(r, r, ps[4 + 2 * n + t][:, :], ALU.add).then_inc(h_ok, 1)

            add_out(3)

            norm(2, xn2, h)
            norm_out(2, xT, g_xa)
            for hd in range(XH):
                dve.wait_ge(sc_ps, hd + 1)
                v.tensor_reduce(att[:, 0, 2 * hd:2 * hd + 2], ps[hd][:, :].rearrange("p (t m) -> p t m", t=TC),
                                AX_X, ALU.max, negate=True).then_inc(nmax, 1)
            for hd in range(XH):
                dve.wait_ge(pexp, hd + 1)
                v.reciprocal(att[:, 2, 2 * hd:2 * hd + 2], att[:, 1, 2 * hd:2 * hd + 2])
                dve.drain()
                for t in range(TC):
                    n = 2 * hd + t
                    v.tensor_scalar(pr[:, t, hd, :], pr[:, t, hd, :], att[:, 2, n:n + 1], None,
                                    ALU.mult).then_inc(pn_ok, 1)
            for hd in range(XH):
                dve.wait_ge(pT_ps, hd + 1)
                v.tensor_copy(prT[:, hd, :, :], ps[4 + hd][:, :].rearrange("p (c s) -> p c s", c=2)).then_inc(pT_sb, 1)
            add_out(5)

            dve.wait_ge(std, 4)
            dve.wait_ge(ld_g, 32)
            v.reciprocal(rst[:, 3, :], nrm[:, 3, :])
            dve.drain()
            for t in range(TC):
                v.scalar_tensor_tensor(out=xn[:, t, :], in0=h[:, t, :], scalar=rst[:, 3, t:t + 1], in1=g_ffn,
                                       op0=ALU.mult, op1=ALU.mult).then_inc(normed, 1)
            v.memset(rank[:, :, NCOL:NCOL + 4], -1.0)
            norm_out(3, xT, None)
            dve.wait_ge(rt_ps, 1)
            v.tensor_tensor(lg[:, :, :], ps[0][:, 0:2 * NE].rearrange("p (t n) -> p t n", t=TC),
                            b_rt[:, :].unsqueeze(1).to_broadcast([P, TC, NE]), ALU.add)
            dve.drain()
            for t in range(TC):
                v.max(mx8[:, t, :], lg[:, t, :])
            dve.drain()
            v.tensor_scalar(gsum[:, :, 0], mx8[:, :, 0], -1.0, None, ALU.mult).then_inc(lmax, 1)
            for t in range(TC):
                v.max_index(ix8[:, t, :], mx8[:, t, :], lg[:, t, :])
            dve.drain()
            v.tensor_copy(ix8f[:, :, :], ix8[:, :, :])
            dve.drain()
            for t in range(TC):
                v.tensor_scalar(mask[:, t, :], iota[:, 0:NE], ix8f[:, t, 0:1], None, ALU.is_equal)
            for n in range(1, TOPK):
                dve.drain()
                for t in range(TC):
                    v.scalar_tensor_tensor(out=mask[:, t, :], in0=iota[:, 0:NE], scalar=ix8f[:, t, n:n + 1],
                                           in1=mask[:, t, :], op0=ALU.is_equal, op1=ALU.add)
            dve.drain()
            for t in range(TC):
                last = v.tensor_copy(mask4[:, t, :].rearrange("p (c e) -> p c e", e=NE),
                                     mask[:, t, :].unsqueeze(1).to_broadcast([P, CHUNKS, NE]))
            last.then_inc(mask_ok, 1)
            dve.wait_ge(rexp, 1)
            v.tensor_tensor(gate[:, :, :], gate[:, :, :], mask[:, :, :], ALU.mult)
            dve.drain()
            v.tensor_reduce(gsum[:, :, 1], gate[:, :, :], AX_X, ALU.add)
            dve.drain()
            v.reciprocal(gsum[:, :, 0], gsum[:, :, 1])
            dve.drain()
            v.tensor_tensor(gate[:, :, :], gate[:, :, :], gsum[:, :, 0].unsqueeze(2).to_broadcast([P, TC, NE]),
                            ALU.mult).then_inc(gate_ok, 1)
            dve.wait_ge(rank_ps, 1)
            v.scalar_tensor_tensor(out=rank[:, :, 0:NE], in0=ps[1][:, 0:2 * NE].rearrange("p (t n) -> p t n", t=TC),
                                   scalar=1.0, in1=mask[:, :, :], op0=ALU.add, op1=ALU.mult)
            dve.drain()
            for chunk in range(CHUNKS - 1, -1, -1):
                v.tensor_scalar(rank[:, :, NE * chunk:NE * (chunk + 1)], rank[:, :, 0:NE],
                                -1.0 - SLOTS * chunk, None, ALU.add)
            dve.wait_ge(cnt_ps, 1)
            v.tensor_tensor(cnt[:, 0:1], ps[2][:, 0:1], col[:, 2:3], ALU.is_gt).then_inc(val_ok, 1)
            dve.wait_ge(pos_ps, 1)
            v.tensor_copy(cnt[:, 1:2], ps[2][:, 2:3])
            dve.drain()
            v.tensor_scalar(pick[:, :], iota[:, 0:16], cnt[:, 1:2], cnt[:, 0:1], ALU.is_equal,
                            ALU.mult).then_inc(pick_ok, 1)
            dve.wait_ge(lst_ps, 1)
            v.tensor_scalar(lst[0:1, 0:16], ps[3][0:1, 0:16], float(DUMMY), None, ALU.add)
            v.tensor_copy(lst[0:1, 16:33], ps[3][0:1, 16:33])
            dve.drain()
            v.tensor_copy(lst_i[0:1, 0:33], lst[0:1, 0:33]).then_inc(lst_ok, 1)
            dve.wait_ge(gt_ps, 1)
            v.tensor_copy(gateT[0:NE, :], ps[0][0:NE, 0:SEQ]).then_inc(gt_sb, 1)
            dve.drain()

            def expert_round(i, column, expert):
                for j in range(2):
                    dve.wait_ge(gathered, 2 * i + (j + 1))
                    for t in range(TC):
                        last = v.tensor_scalar(onehot[:, j, t, :], iota[:, :], rank[:, t, ds(column[j], 1)], None,
                                               ALU.is_equal)
                    last.then_inc(hot_ok, 1)
                for j in range(2):
                    for t in range(TC):
                        last = v.tensor_scalar(scat[:, t, SLOTS * j:SLOTS * (j + 1)], iota[:, :],
                                               rank[:, t, ds(column[j], 1)], gate[:, t, ds(expert[j], 1)],
                                               ALU.is_equal, ALU.mult)
                last.then_inc(sc_ok, 1)

                def swiglu(j):
                    for g in range(2):
                        dve.wait_ge(e_used, 2 * EPIECES * i + (EPIECES * j + 4 * (g + 1)))
                        bias = bguT[:, ds(expert[j] * 16, 16)].rearrange("p (a f) -> p a f", a=2)[
                            :, :, 4 * g:4 * g + 4].unsqueeze(3).to_broadcast([P, 2, 4, SLOTS])
                        v.tensor_tensor(gu[:, g, :, :].rearrange("p (a m) s -> p a m s", a=2),
                                        ps[g][:, :].rearrange("p (a m s) -> p a m s", a=2, m=4), bias,
                                        ALU.add).then_inc(gu_free, 1)
                        dve.drain()
                        v.tensor_scalar(gu[:, g, 0:4, :], gu[:, g, 0:4, :], LIMIT, None, ALU.min).then_inc(gb_ok, 1)
                        v.tensor_scalar(gu[:, g, 4:8, :], gu[:, g, 4:8, :], LIMIT, -LIMIT, ALU.min, ALU.max)
                        dve.drain()
                        v.scalar_tensor_tensor(out=gu[:, g, 4:8, :], in0=gu[:, g, 4:8, :], scalar=1.0,
                                               in1=gu[:, g, 0:4, :], op0=ALU.add, op1=ALU.mult)
                        dve.drain()
                        dve.wait_ge(sg_ok, 4 * i + (2 * j + g + 1))
                        v.tensor_tensor(act_t[:, 4 * g:4 * g + 4, :], gu[:, g, 4:8, :], sg[:, g, :, :],
                                        ALU.mult).then_inc(av_ok, 1)

                swiglu(0)
                dve.wait_ge(st_ps, i + 1)
                v.tensor_copy(scatT, ps[2][:, 0:SEQ]).then_inc(scT_ok, 1)
                swiglu(1)
                dve.wait_ge(yt_ps, 2 * i + 1)
                v.tensor_copy(ysb[:, 0:512], ps[0][:, :]).then_inc(y_dve, 1)

            with dve.Fori(0, PAIRS, 1) as i:
                expert_round(i, [2 * i, 2 * i + 1], [2 * i, 2 * i + 1])
            extra = dve.value_load(lst_i[0:1, 32:33], min_val=0, max_val=MAX_EXTRA)
            with dve.Fori(0, EXTRA_PAIRS, 1) as q:
                with dve.If(extra > 2 * q):
                    column = [dve.value_load(lst_i[0:1, ds(2 * q + j, 1)], min_val=0, max_val=DUMMY)
                              for j in range(2)]
                    expert = [dve.value_load(lst_i[0:1, ds(2 * q + (16 + j), 1)], min_val=0, max_val=NE - 1)
                              for j in range(2)]
                    expert_round(q + PAIRS, column, expert)

            dve.wait_ge(fsum, 1)
            v.tensor_tensor(rst[:, 4, :], nrm[:, 4:6, 0], nrm[:, 4:6, 1], ALU.add).then_inc(fsum, 1)
            dve.wait_ge(stdf, 1)
            v.reciprocal(rst[:, 5, :], rst[:, 4, :])
            dve.drain()
            for t in range(TC):
                for n in range(2):
                    last = v.scalar_tensor_tensor(out=h[:, t, 512 * n:512 * (n + 1)], in0=ps[4 + 2 * n + t][:, :],
                                                  scalar=rst[:, 5, t:t + 1], in1=g_fin[:, 512 * n:512 * (n + 1)],
                                                  op0=ALU.mult, op1=ALU.mult)
                last.then_inc(o_ok, 1)


_INS = ["x", "mem", "mixer_norm", "xattn_norm", "mem_norm", "ffn_norm", "ssd_w_in", "ssd_conv_w", "ssd_conv_b",
        "ssd_dt_bias", "ssd_a_log", "ssd_d", "ssd_norm", "ssd_w_out", "xa_w_q", "xa_w_kv", "xa_w_o",
        "moe_w_router", "moe_b_router", "moe_w_gate_up", "moe_b_gate_up", "moe_w_down", "moe_b_down",
        "final_norm"]


def kernel(**inputs):
    import numpy as np
    from concourse import bacc
    from concourse.bass_utils import run_bass_kernel_spmd

    nc = bacc.Bacc("TRN2", target_bir_lowering=False, num_devices=1)
    arrays, args = {}, []
    for name in _INS:
        a = np.ascontiguousarray(inputs[name])
        if name != "final_norm":
            a = a.reshape(a.shape[1:])
        arrays[f"in_{name}"] = a
        args.append(nc.dram_tensor(f"in_{name}", a.shape, mybir.dt.from_np(a.dtype), kind="ExternalInput").ap())
    args.append(nc.dram_tensor("out", (SEQ, D), F32, kind="ExternalOutput").ap())
    build(nc, *args)
    r = run_bass_kernel_spmd(nc, [arrays], core_ids=[0])
    return r.results[0]["out"].reshape(1, SEQ, D)
```

```python
from contextlib import ExitStack

import concourse.bass as bass
from concourse import mybir

F32 = mybir.dt.float32
F32R = mybir.dt.float32r
I32 = mybir.dt.int32
U32 = mybir.dt.uint32
ALU = mybir.AluOpType
ACT = mybir.ActivationFunctionType
AX_X = mybir.AxisListType.X
ds = bass.ds

P = 128
SEQ = 256
TC = SEQ // P
D = 1024
KD = D // P
DI = 2048
HEADS, HD, GROUPS, HPG = 32, 64, 4, 8
GW_ = DI // GROUPS
NCONV = 3072 // P
XH, XHD = 4, 256
NE, TOPK = 32, 4
SLOTS = 64
CHUNKS = SEQ // SLOTS
NCOL = NE * CHUNKS
DUMMY = NCOL
PAIRS = NE // 2
MAX_EXTRA = TOPK * SEQ // (SLOTS + 1)
EXTRA_PAIRS = (MAX_EXTRA + 1) // 2
EPS = 1e-5
LIMIT, ALPHA = 7.0, 1.702
WP = 4096
EP = 2048
EPIECES = 12
RSLOTS = 8
HSLOTS = 4


def build(nc, x, mem, mixer_norm, xattn_norm, mem_norm, ffn_norm, w_in, conv_w, conv_b, dt_bias, a_log,
          d_skip, ssd_norm, w_out, xa_w_q, xa_w_kv, xa_w_o, w_router, b_router, w_gate_up, b_gate_up,
          w_down, b_down, final_norm, out):
    with ExitStack() as ctx:
        def sb(name, shape, dt=F32):
            return ctx.enter_context(nc.sbuf_tensor(name, shape, dt))

        def sem(name):
            return ctx.enter_context(nc.semaphore(name))

        def big(name, floats):
            start = -(-nc.sbuf_base // 32) * 32
            return sb(name, [P, floats]), start

        ring, ring_at = big("ring", (RSLOTS + HSLOTS) * EP)
        wring, wring_at = big("wring", 3 * WP)
        mid, mid_at = big("mid", HSLOTS * EP)
        h = sb("h", [P, TC, D])
        sq = sb("sq", [P, 2048])

        def part(base, first, end, r=None, **sizes):
            v = base[:, first:end]
            return v.rearrange(r, **sizes) if r else v

        lo_ring = nc.alloc_sbuf_tensor_at("lo_ring", [P, HSLOTS * EP], F32R, offset=ring_at + 4 * RSLOTS * EP)
        hi_ring = nc.alloc_sbuf_tensor_at("hi_ring", [P, HSLOTS * EP], F32R, offset=mid_at)
        toks = nc.alloc_sbuf_tensor_at("toks", [P, 3072], F32R, offset=wring_at)
        xT = part(mid, 0, 2048, r="p (k s) -> p k s", k=KD)
        memT = part(mid, 2048, 4096, r="p (k s) -> p k s", k=KD)
        kT = part(mid, 4096, 6144, r="p (k s) -> p k s", k=KD)
        vb = part(mid, 6144, 8192, r="p (t n) -> p t n", t=TC)
        zs = part(ring, 0, 4096, r="p (t n) -> p t n", t=TC)
        yb = part(ring, 4096, 8192, r="p (t n) -> p t n", t=TC)
        xd = part(ring, 8192, 12288, r="p (t n) -> p t n", t=TC)
        uT = part(ring, 12288, 16384, r="p (k s) -> p k s", k=16)
        bcT = part(ring, 16384, 18432, r="p (k s) -> p k s", k=8)
        cv = part(ring, 18432, 20480, r="p (b m s) -> p b m s", b=4, m=2)
        btok = part(ring, 18432, 18944, r="p (g n) -> p g n", g=GROUPS)
        xde = part(ring, 18944, 19456)
        ytmp = part(ring, 19456, 19968)
        cbm = part(ring, 19968, 20224, r="p (b l) -> p b l", b=2)
        mt = part(ring, 20480, 22528, r="p (b h l) -> p b h l", b=2, h=HPG)
        du = part(ring, 22528, 24576, r="p (b h l) -> p b h l", b=2, h=HPG)
        rows_a = part(ring, 20480, 20608)
        rows_b = part(ring, 20608, 20736)
        bg_rows = part(sq, 0, 512, r="p (n f) -> p n f", n=4)
        xn0 = part(ring, 4096, 6144, r="p (t n) -> p t n", t=TC)
        states = part(sq, 0, 2048, r="p (g n) -> p g n", g=GROUPS)
        xn2 = part(sq, 0, 2048, r="p (t n) -> p t n", t=TC)
        qT = part(sq, 0, 2048, r="p (k s) -> p k s", k=KD)
        g_ffn = part(sq, 0, D)
        mask4 = part(sq, D, D + 2 * NCOL, r="p (t c) -> p t c", t=TC)
        pr = part(ring, 16384, 18432, r="p (t h m) -> p t h m", t=TC, h=XH)
        prT = part(mid, 4096, 6144, r="p (h c s) -> p h c s", h=XH, c=2)
        wslot = [part(wring, WP * s, WP * (s + 1)) for s in range(3)]
        at = [3072]

        def late(n, r=None, **kw):
            v = wring[:, at[0]:at[0] + n]
            at[0] += n
            return v.rearrange(r, **kw) if r else v

        xn = late(2048, "p (t n) -> p t n", t=TC)
        g_fin = late(D)
        xs = part(toks, 0, 2048, r="p (k j q) -> p k j q", k=KD, j=2)
        act_s = part(toks, 2048, 3072, r="p (k q) -> p k q", k=KD)
        gus = late(2048)
        gu = late(2 * 512, "p (g m s) -> p g m s", g=2, m=8)
        sg = late(2 * 256, "p (g m s) -> p g m s", g=2, m=4)
        act_f = late(512, "p (k s) -> p k s", k=KD)
        ysb = late(1024)
        onehot = late(256, "p (t s) -> p t s", t=TC)
        scat = late(256, "p (t s) -> p t s", t=TC)
        scatT = late(512, "p (j t) -> p j t", j=2)

        cst = sb("cst", [P, 4, P])
        ident, tri, stri, ones = (cst[:, n, :] for n in range(4))
        wdt = sb("wdt", [P, KD, HEADS])
        wrt = sb("wrt", [P, KD, NE])
        parT = sb("parT", [P, 160])
        convw_c, convb_c, g_mix, g_xa, g_mem, g_ssd = 0, 96, 120, 128, 136, 144
        bguT = sb("bguT", [P, NE * 16])
        stack = sb("stack", [P, SLOTS])
        small = sb("small", [P, 3, HEADS])
        b_rt = sb("b_rt", [P, NE])
        eps = sb("eps", [P, 1])
        warm = sb("warm", [P, 1])
        nrm = sb("nrm", [P, 6, 2])
        rst = sb("rst", [P, 6, 2])
        dtv = sb("dtv", [P, TC, HEADS])
        dta = sb("dta", [P, TC, HEADS])
        dtb_ = sb("dtb_", [P, TC, HEADS])
        acm = sb("acm", [P, TC, HEADS])
        dec = sb("dec", [P, 2, HEADS])
        aneg = sb("aneg", [P, HEADS])
        ssu = sb("ssu", [P, 8])
        rsu = sb("rsu", [P, 8])
        att = sb("att", [P, 3, 8])
        lg = sb("lg", [P, TC, NE])
        mx8 = sb("mx8", [P, TC, 8])
        ix8 = sb("ix8", [P, TC, 8], U32)
        ix8f = sb("ix8f", [P, TC, 8])
        mask = sb("mask", [P, TC, NE])
        gate = sb("gate", [P, TC, NE])
        gsum = sb("gsum", [P, TC, 2])
        rank = sb("rank", [P, TC, NCOL + 4])
        iota_i = sb("iota_i", [P, 2 * SLOTS], I32)
        iota = sb("iota", [P, 2 * SLOTS])
        col_i = sb("col_i", [P, 3], I32)
        col = sb("col", [P, 3])
        cnt = sb("cnt", [P, 3])
        pick = sb("pick", [P, 16])
        lst = sb("lst", [1, 48])
        lst_i = sb("lst_i", [1, 48], I32)

        ps = [ctx.enter_context(nc.psum_tensor(f"ps{b}", [P, 512], F32)) for b in range(8)]

        (ld_x, ld_mem, ld_rows, ld_small, ld_bg, ld_g, ld_bdn, ld_wdt, ld_wrt, cst_step, cst_done) = (
            sem(n) for n in ("ld_x", "ld_mem", "ld_rows", "ld_small", "ld_bg", "ld_g", "ld_bdn", "ld_wdt",
                             "ld_wrt", "cst_step", "cst_done"))
        w_ready = [sem(f"w_ready{s}") for s in range(3)]
        e_ready = [sem(f"e_ready{s}") for s in range(RSLOTS)]
        (e_used, par_ps, par_sb, std, normed, nt_ps, nt_dve, nt_act, dt_ps, dt_e, dt_s, da_ok, ac_ps,
         u_ps, conv_done, silu_done, z_ps, z_done, xs_ps, xs_done, bt_ps, bt_sb, dec_in, dec_ok) = (
            sem(n) for n in ("e_used", "par_ps", "par_sb", "std", "normed", "nt_ps", "nt_dve",
                             "nt_act", "dt_ps", "dt_e", "dt_s", "da_ok", "ac_ps", "u_ps", "conv_done",
                             "silu_done", "z_ps", "z_done", "xs_ps", "xs_done", "bt_ps", "bt_sb", "dec_in",
                             "dec_ok"))
        (du_ok, prep_ps, diff_ok, cb_ok, exp_ok, mt_ok, main_ps, st_ok, xde_ok, y_read, u_ok, ssu_ok, kv_ps,
         kv_sb, stdu, un_ok, ut_ps, ut_dve, ut_act, wo_ps, h_ok) = (
            sem(n) for n in ("du_ok", "prep_ps", "diff_ok", "cb_ok", "exp_ok", "mt_ok", "main_ps", "st_ok",
                             "xde_ok", "y_read", "u_ok", "ssu_ok", "kv_ps", "kv_sb", "stdu", "un_ok", "ut_ps",
                             "ut_dve", "ut_act", "wo_ps", "h_ok"))
        (q_ps, q_sb, sc_ps, nmax, pexp, pn_ok, pT_ps, pT_sb, pv_ps, pv_sb) = (
            sem(n) for n in ("q_ps", "q_sb", "sc_ps", "nmax", "pexp", "pn_ok", "pT_ps", "pT_sb", "pv_ps",
                             "pv_sb"))
        (rt_ps, lmax, rexp, mask_ok, gate_ok, rank_ps, cnt_ps, val_ok, pos_ps, pick_ok, lst_ps, lst_ok) = (
            sem(n) for n in ("rt_ps", "lmax", "rexp", "mask_ok", "gate_ok", "rank_ps", "cnt_ps", "val_ok",
                             "pos_ps", "pick_ok", "lst_ps", "lst_ok"))
        stack_ok, fadd = sem("stack_ok"), sem("fadd")
        (hi_ok, lo_ok, hot_ok, gathered, xh_ok, xs_ok, gv_ok, t_ps, gu_free, gb_ok, sg_ok, av_ok, sc_ok, st_ps,
         sT_ok, y_ok, fin_ps, fsum, stdf, o_ok, ld_out) = (
            sem(n) for n in ("hi_ok", "lo_ok", "hot_ok", "gathered", "xh_ok", "xs_ok", "gv_ok", "t_ps",
                             "gu_free", "gb_ok", "sg_ok", "av_ok", "sc_ok", "st_ps", "sT_ok", "y_ok", "fin_ps", "fsum", "stdf", "o_ok", "ld_out"))

        def cols(w, row0, c0):
            return w[row0:row0 + D, c0:c0 + 512].rearrange("(k p) n -> p k n", p=P)

        pieces = [cols(w_in, 0, DI + DI), cols(w_in, 0, DI + DI + 512)]
        pieces += [cols(w_in, 0, DI + 512 * n) for n in range(4)]
        pieces += [cols(w_in, 0, 512 * n) for n in range(4)]
        pieces += [cols(xa_w_kv, 0, 512 * n) for n in range(3)]
        pieces += [cols(w_out, D * k, 512 * n) for k in range(2) for n in range(2)]
        pieces += [cols(xa_w_kv, 0, 512 * 3)]
        pieces += [cols(xa_w_q, 0, 512 * n) for n in range(2)]
        pieces += [cols(xa_w_o, 0, 512 * n) for n in range(2)]
        W_U, W_Z, W_OUT, W_Q, W_O = 0, 6, 13, 18, 20
        KV_PIECE = (10, 11, 12, 17)
        KV_BANK = (0, 1, 0, 1, 0, 1, 0, 7)
        KV_FILL = (2, 1, 1, 1, 1, 1, 1, 0)

        def used(n):
            if n < W_Z:
                return u_ps, 2 * (n - W_U) + 2
            if n < KV_PIECE[0]:
                return z_ps, 2 * (n - W_Z) + 2
            if n in KV_PIECE:
                return kv_ps, 2 * KV_PIECE.index(n) + 2
            if n < W_Q:
                return wo_ps, (1, 2, 5, 6)[n - W_OUT]
            return (q_ps, 2 * (n - W_Q) + 2) if n < W_O else (wo_ps, 9 + n - W_O)

        def wpiece(n):
            return wslot[n % 3].rearrange("p (k n) -> p k n", k=KD)

        gu_dram = w_gate_up.rearrange("e (k p) (a g n) -> e g a p k n", p=P, a=2, g=2)
        dn_dram = w_down.rearrange("e (k p) n -> e p k n", p=P)

        def view(base, slot, s):
            return base[:, EP * slot:EP * (slot + 1)].rearrange("p (k n) -> p k n", k=4 if s < 8 else 2)

        def raw(n):
            return view(ring, n % RSLOTS, n % EPIECES)

        def split(s):
            return view(hi_ring, s % HSLOTS, s), view(lo_ring, s % HSLOTS, s)


        def load_expert_piece(sp, e, n):
            s = n % EPIECES
            if s < 8:
                k = 4 * (s // 2 % 2)
                src = gu_dram[e, s // 4, s % 2, :, k:k + 4, :]
            else:
                k = 2 * (s - 8)
                src = dn_dram[e, :, k:k + 2, :]
            sp.dma_start(raw(n), src).then_inc(e_ready[n % RSLOTS], 16)

        block = ctx.enter_context(nc.Block())

        @block.sync
        def _(sp):
            for t in range(TC):
                sp.dma_start(h[:, t, :], x[P * t:P * (t + 1), :]).then_inc(ld_x, 16)
            for r0, v in ((16, mem_norm), (24, ssd_norm)):
                n = v.shape[0] // P
                sp.dma_start(rows_b[r0:r0 + n, :], v.rearrange("(c p) -> c p", p=P)).then_inc(ld_rows, 16)
            sp.wait_ge(ld_rows, 96)
            sp.dma_start(wpiece(0), pieces[0]).then_inc(w_ready[0], 16)
            sp.dma_start(wdt[:, :, :], w_in[:, 5120:5152].rearrange("(k p) n -> p k n", p=P)).then_inc(ld_wdt, 16)
            for n, v in enumerate((dt_bias, a_log, d_skip)):
                sp.dma_start(small[:, n, :], v.partition_broadcast(P)).then_inc(ld_small, 16)
            sp.dma_start(b_rt[:, :], b_router.partition_broadcast(P)).then_inc(ld_small, 16)
            sp.dma_start(bg_rows, b_gate_up.rearrange("e (f q) -> (e f) q", q=P).rearrange(
                "(n p) q -> p n q", p=P)).then_inc(ld_bg, 16)
            sp.dma_start(wpiece(1), pieces[1]).then_inc(w_ready[1], 16)
            sp.dma_start(vb[:, :, :], mem.rearrange("(t p) d -> p t d", p=P)).then_inc(ld_mem, 16)
            sp.dma_start(wpiece(2), pieces[2]).then_inc(w_ready[2], 16)
            sp.dma_start(wrt[:, :, :], w_router.rearrange("(k p) n -> p k n", p=P)).then_inc(ld_wrt, 16)
            for n in range(3, len(pieces)):
                signal, count = used(n - 3)
                sp.wait_ge(signal, count)
                sp.dma_start(wpiece(n), pieces[n]).then_inc(w_ready[n % 3], 16)
                if n == W_Q + 1:
                    for s in range(RSLOTS):
                        load_expert_piece(sp, 0, s)
            sp.wait_ge(sc_ps, XH)
            sp.dma_start(g_ffn, ffn_norm.partition_broadcast(P)).then_inc(ld_g, 16)
            sp.wait_ge(wo_ps, 10)
            sp.dma_start(g_fin, final_norm.partition_broadcast(P)).then_inc(ld_g, 16)
            sp.dma_start(ysb[0:NE, :], b_down).then_inc(ld_bdn, 16)
            with sp.Fori(0, PAIRS - 1, 1) as i:
                for n in range(RSLOTS, RSLOTS + 2 * EPIECES):
                    sp.wait_ge(lo_ok, 2 * EPIECES * i + (n - RSLOTS + 1))
                    load_expert_piece(sp, 2 * i + n // EPIECES, n)
            for n in range(RSLOTS, 2 * EPIECES):
                sp.wait_ge(lo_ok, EPIECES * (NE - 2) + n - RSLOTS + 1)
                load_expert_piece(sp, NE - 2 + n // EPIECES, n)
            sp.wait_ge(lst_ok, 1)
            extra = sp.value_load(lst_i[0:1, 32:33], min_val=0, max_val=MAX_EXTRA)
            with sp.Fori(0, EXTRA_PAIRS, 1) as q:
                with sp.If(extra > 2 * q):
                    for j in range(2):
                        e = sp.value_load(lst_i[0:1, ds(2 * q + (16 + j), 1)], min_val=0, max_val=NE - 1)
                        for n in range(EPIECES * j, EPIECES * (j + 1)):
                            sp.wait_ge(lo_ok, 2 * EPIECES * q + (EPIECES * NE + n - RSLOTS + 1))
                            load_expert_piece(sp, e, n)
            for t in range(TC):
                sp.wait_ge(o_ok, t + 1)
                sp.dma_start(out[P * t:P * (t + 1), :], h[:, t, :]).then_inc(ld_out, 16)
            sp.wait_ge(ld_out, 16 * TC)

        @block.gpsimd
        def _(pool):
            step = [0]

            def settle(ins):
                ins.then_inc(cst_step, 1)
                step[0] += 1
                pool.wait_ge(cst_step, step[0])

            pool.sem_inc(e_used, HSLOTS - 1)
            nc.gpsimd.memset(eps[:, :], EPS)
            nc.gpsimd.memset(ident, 0.0)
            settle(nc.gpsimd.memset(cst[:, 1:4, :], 1.0))
            nc.gpsimd.affine_select(out=ident, in_=ident, compare_op=ALU.not_equal, fill=1.0, base=0,
                                    pattern=[[-1, P]], channel_multiplier=1)
            nc.gpsimd.affine_select(out=tri, in_=tri, compare_op=ALU.is_ge, fill=0.0, base=0,
                                    pattern=[[1, P]], channel_multiplier=-1)
            settle(nc.gpsimd.affine_select(out=stri, in_=stri, compare_op=ALU.is_gt, fill=0.0, base=0,
                                           pattern=[[1, P]], channel_multiplier=-1))
            settle(nc.gpsimd.iota(iota_i[:, :], pattern=[[0, 2], [1, SLOTS]], base=0, channel_multiplier=0))
            for chunk in range(CHUNKS):
                r = slice(NE * chunk, NE * (chunk + 1))
                settle(nc.gpsimd.iota(col_i[r, 0:1], pattern=[[0, 1]], base=NE * chunk - DUMMY, channel_multiplier=1))
                settle(nc.gpsimd.iota(col_i[r, 1:2], pattern=[[0, 1]], base=0, channel_multiplier=1))
                least = SLOTS * chunk if chunk else 2 * SEQ
                settle(nc.gpsimd.iota(col_i[r, 2:3], pattern=[[0, 1]], base=least, channel_multiplier=0))
            nc.gpsimd.tensor_copy(iota[:, :], iota_i[:, :])
            nc.gpsimd.tensor_copy(col[:, :], col_i[:, :]).then_inc(cst_done, 1)
            pool.wait_ge(da_ok, 1)
            for i in range(2 * GROUPS):
                g, c = i // 2, i % 2
                if i >= 2:
                    pool.wait_ge(prep_ps, i - 1)
                a = dta[:, c, HPG * g:HPG * (g + 1)]
                nc.gpsimd.tensor_tensor(du[:, i % 2, :, :], tri.unsqueeze(1).to_broadcast([P, HPG, P]),
                                        a.unsqueeze(2).to_broadcast([P, HPG, P]), ALU.mult).then_inc(du_ok, 1)

        @block.tensor
        def _(pe):
            mm, tr = nc.tensor.matmul, nc.tensor.transpose

            def take(n):
                pe.wait_ge(w_ready[n % 3], 16 * (n // 3 + 1))
                return wpiece(n)

            pe.wait_ge(cst_done, 1)
            pe.wait_ge(ld_rows, 96)
            tr(ps[7][:, 0:120], rows_a[0:120, :], ident[0:120, 0:120])
            tr(ps[7][:, 128:168], rows_b[0:40, :], ident[0:40, 0:40]).then_inc(par_ps, 1)

            def norm_transposes(n, src, bank0=0, filler=None):
                for t in range(TC):
                    pe.wait_ge(normed, 2 * n + t + 1)
                    for b in range(4):
                        for k in (2 * b, 2 * b + 1):
                            at_ = (k % 2) * SEQ + t * P
                            last = tr(ps[bank0 + b][:, at_:at_ + P], src[:, t, k * P:(k + 1) * P], ident)
                        if t == TC - 1:
                            last.then_inc(nt_ps, 1)
                    if t == 0 and filler:
                        filler(t)

            def await_nt(n):
                pe.wait_ge(nt_dve, 4 * n + 4)
                pe.wait_ge(nt_act, 4 * n + 4)

            norm_transposes(0, xn0)
            await_nt(0)

            def dt_and_biases():
                pe.wait_ge(ld_wdt, 16)
                for t in range(TC):
                    for k in range(KD):
                        last = mm(ps[6][:, HEADS * t:HEADS * (t + 1)], xT[:, k, P * t:P * (t + 1)],
                                  wdt[:, k, :], start=k == 0, stop=k == KD - 1)
                last.then_inc(dt_ps, 1)
                pe.wait_ge(ld_bg, 16)
                for n in range(4):
                    last = tr(ps[5][:, n * P:(n + 1) * P], bg_rows[:, n, :], ident)
                last.then_inc(par_ps, 1)

            def project_T(n, banks, src, done, guard):
                w = take(n)
                for b in range(2):
                    guard(b)
                    for m in range(2):
                        for k in range(KD):
                            c0 = (2 * b + m) * P
                            last = mm(ps[banks[b]][:, SEQ * m:SEQ * (m + 1)], w[:, k, c0:c0 + P], src[:, k, :],
                                      start=k == 0, stop=k == KD - 1)
                    last.then_inc(done, 1)

            for p in range(6):
                project_T(W_U + p, (2 * (p % 2), 2 * (p % 2) + 1), xT, u_ps,
                          lambda b: pe.wait_ge(conv_done, 2 * (p - 2) + b + 1) if p >= 2 else None)
                if p == 0:
                    dt_and_biases()
            def x_tokens(q):
                pe.wait_ge(silu_done, 2 * q + 6)
                for t in range(TC):
                    if q >= 1:
                        pe.wait_ge(xs_done, 2 * (q - 1) + t + 1)
                    for m in range(4):
                        last = tr(ps[4 + t][:, P * m:P * (m + 1)], uT[:, 4 * q + m, P * t:P * (t + 1)], ident)
                    last.then_inc(xs_ps, 1)

            for q in range(4):
                w = take(W_Z + q)
                for t in range(TC):
                    if q >= 2:
                        pe.wait_ge(z_done, 2 * (q - 2) + t + 1)
                    else:
                        pe.wait_ge(conv_done, 9 + 2 * q + t)
                    for k in range(KD):
                        last = mm(ps[2 * (q % 2) + t][:, :], xT[:, k, P * t:P * (t + 1)], w[:, k, :],
                                  start=k == 0, stop=k == KD - 1)
                    last.then_inc(z_ps, 1)
                if q == 0:
                    pe.wait_ge(par_sb, 2)
                    pe.wait_ge(dt_e, 1)
                    norm_transposes(1, vb, 4)
                else:
                    if q == 1:
                        await_nt(1)
                    x_tokens(q - 1)
            x_tokens(3)
            for g in range(GROUPS):
                last = tr(ps[7][:, P * g:P * (g + 1)], bcT[:, g, 0:P], ident)
            last.then_inc(bt_ps, 1)
            pe.wait_ge(da_ok, 1)
            for c in range(TC):
                mm(ps[6][:, 32 * c:32 * c + 32], tri, dta[:, c, :], start=True, stop=True)
            mm(ps[6][:, 64:96], ones, dta[:, 0, :], start=True, stop=True).then_inc(ac_ps, 1)

            def prep(i):
                g, c = i // 2, i % 2
                pe.wait_ge(du_ok, i + 1)
                if i:
                    pe.wait_ge(diff_ok, i)
                    pe.wait_ge(cb_ok, i)
                else:
                    pe.wait_ge(z_done, 8)
                    pe.wait_ge(xs_done, 8)
                for b in range(2):
                    mm(ps[2 + b][:, :], ones, du[:, i % 2, 4 * b:4 * b + 4, :], start=True, stop=True)
                mm(ps[4][:, 0:P], bcT[:, g, P * c:P * (c + 1)], bcT[:, 4 + g, P * c:P * (c + 1)],
                   start=True, stop=True).then_inc(prep_ps, 1)

            def keys_values(quarter):
                i, half = quarter // 2, quarter // 2 % 2
                w = take(KV_PIECE[i // 2])
                bank = ps[KV_BANK[i]]
                if 2 <= i < 6 and quarter % 2 == 0:
                    pe.wait_ge(kv_sb, i - 1)
                if i < 4:
                    m = quarter % 2
                    for k in range(KD):
                        c0 = (2 * half + m) * P
                        last = mm(bank[:, SEQ * m:SEQ * (m + 1)], w[:, k, c0:c0 + P], memT[:, k, :],
                                  start=k == 0, stop=k == KD - 1)
                else:
                    for k in range(4 * (quarter % 2), 4 * (quarter % 2) + 4):
                        last = mm(bank[:, :], memT[:, k, P * half:P * (half + 1)], w[:, k, :],
                                  start=k == 0, stop=k == KD - 1)
                if quarter % 2:
                    last.then_inc(kv_ps, 1)

            def scan(i):
                g, c = i // 2, i % 2
                pe.wait_ge(mt_ok, i + 1)
                if i:
                    pe.wait_ge(y_read, i)
                for j in range(HPG):
                    c0 = GW_ * g + HD * j
                    last = mm(ps[5][:, HD * j:HD * (j + 1)], mt[:, i % 2, j, :], xd[:, c, c0:c0 + HD],
                              start=True, stop=True)
                if c == 0:
                    pe.wait_ge(xde_ok, g + 1)
                    pe.wait_ge(bt_sb, 1)
                    if g == 0:
                        pe.wait_ge(dec_in, 1)
                    mm(ps[6][:, :], btok[:, g, :], xde, start=True, stop=True).then_inc(main_ps, 1)
                else:
                    pe.wait_ge(st_ok, g + 1)
                    mm(ps[6][:, :], bcT[:, 4 + g, P:2 * P], states[:, g, :], start=True,
                       stop=True).then_inc(main_ps, 1)

            prep(0)
            quarter = 0
            for i in range(2 * GROUPS):
                for _ in range(KV_FILL[i]):
                    keys_values(quarter)
                    quarter += 1
                if i + 1 < 2 * GROUPS:
                    prep(i + 1)
                scan(i)
            for quarter in range(quarter, 12):
                keys_values(quarter)
            pe.wait_ge(diff_ok, 8)
            for j in range(8):
                if j == 2:
                    pe.wait_ge(kv_sb, 6)
                pe.wait_ge(un_ok, 2 * (j // 2) + 2)
                if j >= 4:
                    pe.wait_ge(ut_dve if j % 2 == 0 else ut_act, (j - 4) // 2 + 1)
                for k in (2 * j, 2 * j + 1):
                    for t in range(TC):
                        at_ = (k % 2) * SEQ + t * P
                        last = tr(ps[(j + 2) % 4][:, at_:at_ + P], yb[:, t, k * P:(k + 1) * P], ident)
                last.then_inc(ut_ps, 1)
            pe.wait_ge(y_read, 8)
            for kh in range(2):
                pe.wait_ge(ut_dve, 2 * kh + 2)
                pe.wait_ge(ut_act, 2 * kh + 2)
                for n, t in ((0, 0), (0, 1), (1, 0), (1, 1)) if kh == 0 else ((0, 0), (1, 0), (0, 1), (1, 1)):
                    w = take(W_OUT + 2 * kh + n)
                    for k in range(KD):
                        last = mm(ps[4 + 2 * n + t][:, :], uT[:, KD * kh + k, P * t:P * (t + 1)],
                                  w[:, k, :], start=kh == 0 and k == 0, stop=kh == 1 and k == KD - 1)
                    if t == 1 or kh == 1:
                        last.then_inc(wo_ps, 1)

            keys_values(12)
            keys_values(13)
            pe.wait_ge(kv_sb, 7)
            norm_transposes(2, xn2)
            await_nt(2)
            for a in range(2):
                project_T(W_Q + a, (4 + 2 * a, 5 + 2 * a), xT, q_ps, lambda b: None)
            for hd in range(XH):
                pe.wait_ge(q_sb, hd + 1)
                for t in range(TC):
                    for kk in (2 * hd, 2 * hd + 1):
                        last = mm(ps[hd][:, SEQ * t:SEQ * (t + 1)], qT[:, kk, P * t:P * (t + 1)], kT[:, kk, :],
                                  start=kk == 2 * hd, stop=kk == 2 * hd + 1)
                last.then_inc(sc_ps, 1)
            keys_values(14)
            keys_values(15)
            for hd in range(XH):
                if hd == XH - 1:
                    pe.wait_ge(kv_sb, 8)
                pe.wait_ge(pn_ok, 2 * hd + 2)
                for mc in range(2):
                    for t in range(TC):
                        at_ = mc * SEQ + t * P
                        last = tr(ps[4 + hd][:, at_:at_ + P], pr[:, t, hd, P * mc:P * (mc + 1)], ident)
                last.then_inc(pT_ps, 1)
            for hd in range(XH):
                pe.wait_ge(pT_sb, hd + 1)
                for dv in range(2):
                    for mc in range(2):
                        c0 = XHD * hd + P * dv
                        last = mm(ps[hd][:, SEQ * dv:SEQ * (dv + 1)], vb[:, mc, c0:c0 + P], prT[:, hd, mc, :],
                                  start=mc == 0, stop=mc == 1)
                last.then_inc(pv_ps, 1)
            pe.wait_ge(pv_sb, XH)
            for t in range(TC):
                for n in range(2):
                    w = take(W_O + n)
                    for k in range(KD):
                        last = mm(ps[4 + 2 * n + t][:, :], xT[:, k, P * t:P * (t + 1)], w[:, k, :],
                                  start=k == 0, stop=k == KD - 1)
                    last.then_inc(wo_ps, 1)

            def start_sums(t):
                for n in range(2):
                    mm(ps[4 + 2 * n + t][:, :], ident, h[:, t, 512 * n:512 * (n + 1)], start=True, stop=True)

            norm_transposes(3, xn, 0, start_sums)
            await_nt(3)
            pe.wait_ge(ld_wrt, 16)
            for t in range(TC):
                for k in range(KD):
                    last = mm(ps[0][:, NE * t:NE * (t + 1)], xT[:, k, P * t:P * (t + 1)], wrt[:, k, :],
                              start=k == 0, stop=k == KD - 1)
            last.then_inc(rt_ps, 1)
            start_sums(1)
            pe.wait_ge(mask_ok, 1)
            mm(ps[1][:, 0:NE], stri, mask[:, 0, :], start=True, stop=True)
            mm(ps[1][:, NE:2 * NE], stri, mask[:, 1, :], start=True, stop=False)
            mm(ps[1][:, NE:2 * NE], ones, mask[:, 0, :], start=False, stop=True).then_inc(rank_ps, 1)
            for t in range(TC):
                last = mm(ps[3][:, 64:65], mask4[:, t, :], ones[:, 0:1], start=t == 0, stop=t == TC - 1)
            last.then_inc(cnt_ps, 1)
            def scatter_transpose(bank, count):
                pe.wait_ge(sc_ok, count)
                for t in range(TC):
                    last = tr(ps[bank][:, P * t:P * (t + 1)], scat[:, t, :], ident)
                last.then_inc(st_ps, 1)

            def scatter(j, y_count, t_count):
                pe.wait_ge(y_ok, y_count)
                pe.wait_ge(sT_ok, t_count)
                for n in range(2):
                    for t in range(TC):
                        last = mm(ps[4 + 2 * n + t][:, :], scatT[:, j, P * t:P * (t + 1)],
                                  ysb[:, 512 * n:512 * (n + 1)], start=False, stop=True,
                                  skip_group_check=True)
                return last

            def gather(count):
                pe.wait_ge(hot_ok, count)
                for k in range(KD):
                    for t in range(TC):
                        last = mm(ps[k // 4][:, P * (k % 4):P * (k % 4 + 1)], xn[:, t, P * k:P * (k + 1)],
                                  onehot[:, t, :], start=t == 0, stop=t == TC - 1)
                    if k % 4 == 3:
                        last.then_inc(gathered, 1)

            gather(1)
            pe.wait_ge(stack_ok, 1)
            scatter_transpose(2, 1)
            pe.wait_ge(val_ok, 1)
            mm(ps[3][:, 66:67], stri, cnt[:, 0:1], start=True, stop=True).then_inc(pos_ps, 1)
            pe.wait_ge(pick_ok, 1)
            mm(ps[3][0:1, 0:16], col[:, 0:1], pick[:, :], start=True, stop=True)
            mm(ps[3][0:1, 16:32], col[:, 1:2], pick[:, :], start=True, stop=True)
            mm(ps[3][0:1, 32:33], cnt[:, 0:1], ones[:, 0:1], start=True, stop=True).then_inc(lst_ps, 1)
            pe.wait_ge(ld_bdn, 16)
            pe.wait_ge(sT_ok, 1)
            pe.wait_ge(lst_ok, 1)
            for n in range(2):
                last = mm(ps[2 + n][:, :], ident[0:NE, :], ysb[0:NE, 512 * n:512 * (n + 1)], start=True, stop=True)
            last.then_inc(e_used, 1)

            def expert_pass(i, j, further):
                def parts(s):
                    pe.wait_ge(lo_ok, 2 * EPIECES * i + (EPIECES * j + s + 1))
                    return split(s)

                if j == 0:
                    pe.wait_ge(xs_ok, 2 * i + (4 if further else 2))
                else:
                    pe.wait_ge(gu_free, 4 * i + 2)
                for g in range(2):
                    if g == 1:
                        pe.wait_ge(y_ok, 4 * i + (2 * j + 2))
                    for s in range(4 * g, 4 * g + 4):
                        a, k0 = s % 2, 4 * (s // 2 % 2)
                        w = parts(s)
                        for kk in range(4):
                            k = k0 + kk
                            for h_l in range(2):
                                last = mm(ps[2 * g + a][:, :], xs[:, k, j, :], w[h_l][:, kk, :],
                                          start=k == 0 and h_l == 0, stop=k == KD - 1 and h_l == 1)
                        last.then_inc(e_used, 1)
                for g in range(2):
                    pe.wait_ge(gv_ok, 8 * i + (4 * j + 2 * g + 2))
                    for f in range(8):
                        c0 = 1024 * g + P * f
                        last = mm(ps[g][:, SLOTS * f:SLOTS * (f + 1)], gus[:, c0:c0 + P], stack[:, :],
                                  start=True, stop=True)
                    last.then_inc(t_ps, 1)
                scatter_transpose(2, 2 * i + (j + 2))
                if not further:
                    scatter(1 - j, 4 * i + (2 * j + 2), 2 * i + (j + 1))
                    if j == 1:
                        pe.wait_ge(gu_free, 4 * i + 4)
                        gather(i + 2)
                pe.wait_ge(sT_ok, 2 * i + (j + 2))
                for s in range(8, EPIECES):
                    if s % 2 == 0:
                        pe.wait_ge(av_ok, 4 * i + (2 * j + (s - 8) // 2 + 1))
                    w = parts(s)
                    for kk in range(2):
                        k = 2 * (s - 8) + kk
                        for n in range(2):
                            for h_l in range(2):
                                last = mm(ps[2 + n][:, :], act_s[:, k, :],
                                          w[h_l][:, kk, 512 * n:512 * (n + 1)],
                                          start=k == 0 and h_l == 0, stop=k == KD - 1 and h_l == 1)
                    last.then_inc(e_used, 1)
                if further:
                    scatter(j, 4 * i + (2 * j + 4), 2 * i + (j + 2))

            with pe.Fori(0, PAIRS, 1) as i:
                expert_pass(i, 0, False)
                expert_pass(i, 1, False)
            scatter(1, 2 * NE + 2, NE + 1)
            extra = pe.value_load(lst_i[0:1, 32:33], min_val=0, max_val=MAX_EXTRA)
            with pe.Fori(PAIRS, PAIRS + EXTRA_PAIRS, 1) as i:
                with pe.If(extra > 2 * i - 2 * PAIRS):
                    pe.wait_ge(gu_free, 4 * i)
                    gather(i + 2)
                    expert_pass(i, 0, True)
                    expert_pass(i, 1, True)
            pe.wait_ge(xs_ok, 2 * PAIRS + 2)
            mm(ps[0][:, 0:1], ones, ones[:, 0:1], start=True, stop=True).then_inc(fin_ps, 1)

        @block.scalar
        def _(act):
            def fn(out_, in_, func, **kw):
                return nc.scalar.activation(out_, in_, func, **kw)

            act.dma_start(rows_a[0:96, :], conv_w.rearrange("j (c p) -> (j c) p", p=P)).then_inc(ld_rows, 16)
            act.dma_start(rows_a[96:120, :], conv_b.rearrange("(c p) -> c p", p=P)).then_inc(ld_rows, 16)
            for r0, v in ((0, mixer_norm), (8, xattn_norm)):
                act.dma_start(rows_b[r0:r0 + KD, :], v.rearrange("(c p) -> c p", p=P)).then_inc(ld_rows, 16)

            def norm_stats(n, src, junk):
                for t in range(TC):
                    if n >= 2:
                        act.wait_ge(h_ok, 4 * (n - 2) + 2 * t + 2)
                    fn(junk[:, t, :], src[:, t, :], ACT.Square, accum_out=nrm[:, n, t:t + 1])
                    act.drain()
                    fn(nrm[:, n, t:t + 1], nrm[:, n, t:t + 1], ACT.Sqrt, bias=eps[:, 0:1],
                       scale=1.0 / D).then_inc(std, 1)

            def load_sqrt():
                fn(warm[:, 0:1], eps[:, 0:1], ACT.Sqrt)
                act.drain()

            def norm_out(n, dst, gains, bank0=0):
                for k in range(4, KD):
                    act.wait_ge(nt_ps, 4 * n + k // 2 + 1)
                    src = ps[bank0 + k // 2][:, SEQ * (k % 2):SEQ * (k % 2 + 1)]
                    scale = 1.0 if gains is None else parT[:, gains + k:gains + k + 1]
                    fn(dst[:, k, :], src, ACT.Copy, scale=scale).then_inc(nt_act, 1)

            act.wait_ge(cst_done, 1)
            load_sqrt()
            act.wait_ge(ld_x, 32)
            norm_stats(0, h, xn0)
            act.wait_ge(par_sb, 1)
            norm_out(0, xT, g_mix)
            act.wait_ge(ld_small, 64)
            fn(aneg[:, :], small[:, 1, :], ACT.Exp)
            act.wait_ge(dt_e, 1)
            fn(dta[:, :, :], dta[:, :, :], ACT.Exp).then_inc(dt_s, 1)
            act.wait_ge(ld_mem, 16)
            norm_stats(1, vb, part(ring, 8192, 10240, r="p (t n) -> p t n", t=TC))
            for n in range(12):
                act.wait_ge(conv_done, n + 1)
                p, b = n // 2, n % 2
                dst = bcT[:, 4 * p + 2 * b:4 * p + 2 * b + 2, :] if p < 2 else \
                    uT[:, 4 * (p - 2) + 2 * b:4 * (p - 2) + 2 * b + 2, :]
                fn(dst, cv[:, n % 4, :, :], ACT.Silu).then_inc(silu_done, 1)
            norm_out(1, memT, g_mem, 4)
            for n in range(8):
                q, t = n // 2, n % 2
                act.wait_ge(z_ps, n + 1)
                fn(zs[:, t, 512 * q:512 * (q + 1)], ps[2 * (q % 2) + t][:, :], ACT.Silu).then_inc(z_done, 1)
            act.wait_ge(bt_ps, 1)
            act.drain()
            fn(btok, ps[7][:, :].rearrange("p (g n) -> p g n", g=GROUPS), ACT.Copy).then_inc(bt_sb, 1)
            act.wait_ge(dec_in, 1)
            fn(dec[:, :, :], dec[:, :, :], ACT.Exp).then_inc(dec_ok, 1)

            def square_u(i):
                g, c = i // 2, i % 2
                u = slice(GW_ * g, GW_ * (g + 1))
                act.wait_ge(u_ok, i + 1)
                fn(zs[:, c, u], yb[:, c, u], ACT.Square, accum_out=ssu[:, i:i + 1])

            def state_out(i):
                if i % 2 == 0:
                    act.wait_ge(main_ps, i + 1)
                    fn(states[:, i // 2, :], ps[6][:, :], ACT.Copy).then_inc(st_ok, 1)

            def kv_out(i):
                act.wait_ge(kv_ps, i + 1)
                src = ps[KV_BANK[i]][:, :]
                if i < 4:
                    fn(kT[:, 2 * i:2 * i + 2, :], src.rearrange("p (m s) -> p m s", m=2),
                       ACT.Copy).then_inc(kv_sb, 1)
                else:
                    n = (i - 4) // 2
                    fn(vb[:, i % 2, 512 * n:512 * (n + 1)], src, ACT.Copy).then_inc(kv_sb, 1)

            for i in range(2 * GROUPS):
                act.wait_ge(diff_ok, i + 1)
                fn(mt[:, i % 2, :, :], mt[:, i % 2, :, :], ACT.Exp).then_inc(exp_ok, 1)
                for half in range(sum(KV_FILL[:i]) // 2, sum(KV_FILL[:i + 1]) // 2):
                    kv_out(half)
                if i:
                    state_out(i - 1)
                    square_u(i - 1)
            square_u(2 * GROUPS - 1)
            act.drain()
            fn(rsu[:, :], ssu[:, :], ACT.Sqrt, bias=eps[:, 0:1], scale=1.0 / GW_).then_inc(stdu, 1)
            for half in range(sum(KV_FILL) // 2, 6):
                kv_out(half)
            for j in range(1, 8, 2):
                act.wait_ge(ut_ps, j + 1)
                for k in (2 * j, 2 * j + 1):
                    last = fn(uT[:, k, :], ps[(j + 2) % 4][:, SEQ * (k % 2):SEQ * (k % 2 + 1)], ACT.Copy,
                              scale=parT[:, g_ssd + k:g_ssd + k + 1])
                last.then_inc(ut_act, 1)

            norm_stats(2, h, xn2)
            kv_out(6)
            norm_out(2, xT, g_xa)
            for b in range(4):
                act.wait_ge(q_ps, b + 1)
                fn(qT[:, 2 * b:2 * b + 2, :], ps[4 + b][:, :].rearrange("p (m s) -> p m s", m=2), ACT.Copy,
                   scale=XHD ** -0.5).then_inc(q_sb, 1)
            for hd in range(XH):
                act.wait_ge(nmax, hd + 1)
                for t in range(TC):
                    n = 2 * hd + t
                    last = fn(pr[:, t, hd, :], ps[hd][:, SEQ * t:SEQ * (t + 1)], ACT.Exp,
                              bias=att[:, 0, n:n + 1], accum_out=att[:, 1, n:n + 1])
                last.then_inc(pexp, 1)
            kv_out(7)
            for hd in range(XH):
                act.wait_ge(pv_ps, hd + 1)
                fn(xT[:, 2 * hd:2 * hd + 2, :], ps[hd][:, :].rearrange("p (m s) -> p m s", m=2),
                   ACT.Copy).then_inc(pv_sb, 1)

            load_sqrt()
            norm_stats(3, h, xn)
            norm_out(3, xT, None)
            act.wait_ge(lmax, 1)
            for t in range(TC):
                last = fn(gate[:, t, :], lg[:, t, :], ACT.Exp, bias=gsum[:, t, 0:1])
            last.then_inc(rexp, 1)

            def tokens_hi(count):
                for b in range(2):
                    act.wait_ge(gathered, count + b)
                    fn(xs[:, 4 * b:4 * b + 4, :, 0:SLOTS],
                       ps[b][:, :].rearrange("p (k j s) -> p k j s", k=4, j=2), ACT.Copy).then_inc(xh_ok, 1)

            def scatter_out(j, bank, count):
                act.wait_ge(st_ps, count)
                fn(scatT[:, j, :], ps[bank][:, 0:SEQ], ACT.Copy).then_inc(sT_ok, 1)

            def down_out(used_count):
                act.wait_ge(e_used, used_count)
                for n in range(2):
                    fn(ysb[:, 512 * n:512 * (n + 1)], ps[2 + n][:, :], ACT.Copy).then_inc(y_ok, 1)

            tokens_hi(1)
            scatter_out(1, 2, 1)

            def expert_pass(i, j, further):
                def hi(s):
                    n = EPIECES * j + s
                    act.wait_ge(e_ready[n % RSLOTS], 48 * i + 16 * (n // RSLOTS + 1))
                    act.wait_ge(e_used, 2 * EPIECES * i + (n + 1))
                    fn(split(s)[0], raw(n), ACT.Copy).then_inc(hi_ok, 1)

                def gate_up_out(g):
                    act.wait_ge(e_used, 2 * EPIECES * i + (HSLOTS + EPIECES * j + 4 * g + 4))
                    for a in range(2):
                        c0 = 1024 * g + 512 * a
                        fn(gus[:, c0:c0 + 512], ps[2 * g + a][:, :], ACT.Copy).then_inc(gv_ok, 1)

                for s in range(4):
                    hi(s)
                if not further:
                    down_out(2 * EPIECES * i + (HSLOTS + EPIECES * j))
                hi(4)
                hi(5)
                gate_up_out(0)
                for s in range(6, 10):
                    hi(s)
                gate_up_out(1)
                hi(10)
                for g in range(2):
                    act.wait_ge(gb_ok, 4 * i + (2 * j + g + 1))
                    fn(sg[:, g, :, :], gu[:, g, 0:4, :], ACT.Sigmoid, scale=ALPHA).then_inc(sg_ok, 1)
                scatter_out(j, 2, 2 * i + (j + 2))
                hi(11)
                if further:
                    down_out(2 * EPIECES * i + (HSLOTS + EPIECES * (j + 1)))
                elif j == 1:
                    tokens_hi(2 * i + 3)

            with act.Fori(0, PAIRS, 1) as i:
                expert_pass(i, 0, False)
                expert_pass(i, 1, False)
            down_out(HSLOTS + EPIECES * NE)
            act.wait_ge(lst_ok, 1)
            extra = act.value_load(lst_i[0:1, 32:33], min_val=0, max_val=MAX_EXTRA)
            with act.Fori(PAIRS, PAIRS + EXTRA_PAIRS, 1) as i:
                with act.If(extra > 2 * i - 2 * PAIRS):
                    tokens_hi(2 * i + 3)
                    expert_pass(i, 0, True)
                    expert_pass(i, 1, True)
            load_sqrt()
            act.wait_ge(fin_ps, 1)
            for t in range(TC):
                for n in range(2):
                    last = fn(xn[:, t, 512 * n:512 * (n + 1)], ps[4 + 2 * n + t][:, :], ACT.Square,
                              accum_out=nrm[:, 4 + t, n:n + 1])
                last.then_inc(fsum, 1)
            for t in range(TC):
                act.wait_ge(fadd, t + 1)
                fn(rst[:, 4, t:t + 1], rst[:, 4, t:t + 1], ACT.Sqrt, bias=eps[:, 0:1],
                   scale=1.0 / D).then_inc(stdf, 1)

        @block.vector
        def _(dve):
            v = nc.vector
            dve.wait_ge(cst_done, 1)
            v.tensor_tensor(stack[:, :], ident[:, 0:SLOTS], ident[:, SLOTS:P], ALU.add).then_inc(stack_ok, 1)
            dve.wait_ge(par_ps, 1)
            v.tensor_copy(parT[:, 0:120], ps[7][:, 0:120])
            v.tensor_copy(parT[:, 120:160], ps[7][:, 128:168]).then_inc(par_sb, 1)

            def norm_chunk(n, t, dst, src, gains=None):
                dve.wait_ge(std, 2 * n + t + 1)
                v.reciprocal(rst[:, n, t:t + 1], nrm[:, n, t:t + 1])
                dve.drain()
                if gains is None:
                    v.tensor_scalar(dst[:, t, :], src[:, t, :], rst[:, n, t:t + 1], None,
                                    ALU.mult).then_inc(normed, 1)
                else:
                    v.scalar_tensor_tensor(out=dst[:, t, :], in0=src[:, t, :], scalar=rst[:, n, t:t + 1],
                                           in1=gains, op0=ALU.mult, op1=ALU.mult).then_inc(normed, 1)

            def norm_out(n, dst, gains, bank0=0):
                for k in range(4):
                    dve.wait_ge(nt_ps, 4 * n + k // 2 + 1)
                    src = ps[bank0 + k // 2][:, SEQ * (k % 2):SEQ * (k % 2 + 1)]
                    if gains is None:
                        v.tensor_copy(dst[:, k, :], src).then_inc(nt_dve, 1)
                    else:
                        v.tensor_scalar(dst[:, k, :], src, parT[:, gains + k:gains + k + 1], None,
                                        ALU.mult).then_inc(nt_dve, 1)

            for t in range(TC):
                norm_chunk(0, t, xn0, h)
            norm_out(0, xT, g_mix)
            dve.wait_ge(dt_ps, 1)
            dve.wait_ge(ld_small, 64)
            v.tensor_tensor(dtv[:, :, :], ps[6][:, 0:64].rearrange("p (t n) -> p t n", t=TC),
                            small[:, 0, :].unsqueeze(1).to_broadcast([P, TC, HEADS]), ALU.add)
            dve.drain()
            v.tensor_scalar(dta[:, :, :], dtv[:, :, :], 0.0, None, ALU.min)
            dve.drain()
            v.tensor_scalar(dtv[:, :, :], dtv[:, :, :], 0.0, None, ALU.max)
            dve.drain()
            v.tensor_tensor(dta[:, :, :], dta[:, :, :], dtv[:, :, :], ALU.subtract).then_inc(dt_e, 1)
            dve.wait_ge(dt_s, 1)
            v.tensor_scalar(dtb_[:, :, :], dta[:, :, :], 2.0, None, ALU.add)
            dve.drain()
            v.reciprocal(dtb_[:, :, :], dtb_[:, :, :])
            dve.drain()
            v.tensor_tensor(dta[:, :, :], dta[:, :, :], dtb_[:, :, :], ALU.mult)
            dve.drain()
            v.tensor_tensor(dtb_[:, :, :], dta[:, :, :], dta[:, :, :], ALU.mult)
            dve.drain()
            v.tensor_scalar(acm[:, :, :], dtb_[:, :, :], 1.0 / 17, None, ALU.mult)
            for n in (15, 13, 11, 9, 7, 5, 3):
                dve.drain()
                v.scalar_tensor_tensor(out=acm[:, :, :], in0=acm[:, :, :], scalar=1.0 / n, in1=dtb_[:, :, :],
                                       op0=ALU.add, op1=ALU.mult)
            dve.drain()
            v.scalar_tensor_tensor(out=dta[:, :, :], in0=acm[:, :, :], scalar=1.0, in1=dta[:, :, :],
                                   op0=ALU.add, op1=ALU.mult)
            dve.drain()
            v.scalar_tensor_tensor(out=dtv[:, :, :], in0=dta[:, :, :], scalar=2.0, in1=dtv[:, :, :],
                                   op0=ALU.mult, op1=ALU.add)
            dve.drain()
            for t in range(TC):
                last = v.scalar_tensor_tensor(out=dta[:, t, :], in0=dtv[:, t, :], scalar=-1.0, in1=aneg[:, :],
                                              op0=ALU.mult, op1=ALU.mult)
            last.then_inc(da_ok, 1)
            dve.wait_ge(par_ps, 2)
            v.tensor_copy(bguT[:, :], ps[5][:, :]).then_inc(par_sb, 1)

            for n in range(12):
                if n == 8:
                    for t in range(TC):
                        norm_chunk(1, t, vb, vb)
                p, b = n // 2, n % 2
                c0 = (16 + 4 * p if p < 2 else 4 * (p - 2)) + 2 * b
                dve.wait_ge(u_ps, n + 1)
                if n >= 4:
                    dve.wait_ge(silu_done, n - 3)
                for m in range(2):
                    w = convw_c + 3 * NCONV + c0 + m
                    v.tensor_scalar(cv[:, n % 4, m, :], ps[2 * (p % 2) + b][:, SEQ * m:SEQ * (m + 1)],
                                    parT[:, w:w + 1], parT[:, convb_c + c0 + m:convb_c + c0 + m + 1],
                                    ALU.mult, ALU.add)
                for j in (2, 1, 0):
                    dve.drain()
                    for m in range(2):
                        w = convw_c + j * NCONV + c0 + m
                        back = 3 - j
                        src = ps[2 * (p % 2) + b][:, SEQ * m:SEQ * (m + 1) - back]
                        last = v.scalar_tensor_tensor(out=cv[:, n % 4, m, back:], in0=src,
                                                      scalar=parT[:, w:w + 1], in1=cv[:, n % 4, m, back:],
                                                      op0=ALU.mult, op1=ALU.add)
                last.then_inc(conv_done, 1)
            norm_out(1, memT, g_mem, 4)

            def by_head(ap):
                return ap.rearrange("p (j d) -> p j d", d=HD)

            def spread(ap):
                return ap.unsqueeze(2).to_broadcast([P, HPG, HD])

            for n in range(8):
                q, t = n // 2, n % 2
                hs, cs = slice(HPG * q, HPG * (q + 1)), slice(GW_ * q, GW_ * (q + 1))
                dve.wait_ge(xs_ps, n + 1)
                v.tensor_tensor(by_head(xd[:, t, cs]), by_head(ps[4 + t][:, :]), spread(dtv[:, t, hs]), ALU.mult)
                v.tensor_tensor(by_head(yb[:, t, cs]), by_head(ps[4 + t][:, :]), spread(small[:, 2, hs]),
                                ALU.mult).then_inc(xs_done, 1)
            dve.wait_ge(ac_ps, 1)
            v.tensor_copy(acm[:, :, :], ps[6][:, 0:64].rearrange("p (t n) -> p t n", t=TC))
            dve.drain()
            v.tensor_copy(dec[:, 1, :], acm[:, 1, :])
            v.tensor_tensor(dec[:, 0, :], ps[6][:, 64:96], acm[:, 0, :], ALU.subtract).then_inc(dec_in, 1)

            def decays(i):
                g, c = i // 2, i % 2
                dve.wait_ge(prep_ps, i + 1)
                v.tensor_tensor(cbm[:, i % 2, :], ps[4][:, 0:P], tri, ALU.mult).then_inc(cb_ok, 1)
                for j in range(HPG):
                    hcol = HPG * g + j
                    last = v.tensor_scalar(mt[:, i % 2, j, :], ps[2 + j // 4][:, P * (j % 4):P * (j % 4 + 1)],
                                           acm[:, c, hcol:hcol + 1], 0.0, ALU.subtract, ALU.min)
                last.then_inc(diff_ok, 1)

            decays(0)
            for i in range(2 * GROUPS):
                g, c = i // 2, i % 2
                gs, hs = slice(GW_ * g, GW_ * (g + 1)), slice(HPG * g, HPG * (g + 1))
                if c == 0:
                    dve.wait_ge(dec_ok, 1)
                    v.tensor_tensor(by_head(xde), by_head(xd[:, 0, gs]), spread(dec[:, 0, hs]),
                                    ALU.mult).then_inc(xde_ok, 1)
                dve.wait_ge(exp_ok, i + 1)
                v.tensor_tensor(mt[:, i % 2, :, :], mt[:, i % 2, :, :],
                                cbm[:, i % 2, :].unsqueeze(1).to_broadcast([P, HPG, P]), ALU.mult).then_inc(mt_ok, 1)
                if i + 1 < 2 * GROUPS:
                    decays(i + 1)
                dve.wait_ge(main_ps, i + 1)
                if c == 1:
                    v.tensor_tensor(by_head(ytmp), by_head(ps[6][:, :]), spread(dec[:, 1, hs]), ALU.mult)
                v.tensor_tensor(yb[:, c, gs], yb[:, c, gs], ps[5][:, :], ALU.add).then_inc(y_read, 1)
                if c == 1:
                    dve.drain()
                    v.tensor_tensor(yb[:, c, gs], yb[:, c, gs], ytmp, ALU.add)
                dve.drain()
                v.tensor_tensor(yb[:, c, gs], yb[:, c, gs], zs[:, c, gs], ALU.mult).then_inc(u_ok, 1)
            dve.wait_ge(stdu, 1)
            v.reciprocal(rsu[:, :], rsu[:, :])
            dve.drain()
            for i in range(2 * GROUPS):
                g, c = i // 2, i % 2
                gs = slice(GW_ * g, GW_ * (g + 1))
                v.tensor_scalar(yb[:, c, gs], yb[:, c, gs], rsu[:, i:i + 1], None, ALU.mult).then_inc(un_ok, 1)
            for j in range(0, 8, 2):
                dve.wait_ge(ut_ps, j + 1)
                for k in (2 * j, 2 * j + 1):
                    last = v.tensor_scalar(uT[:, k, :], ps[(j + 2) % 4][:, SEQ * (k % 2):SEQ * (k % 2 + 1)],
                                           parT[:, g_ssd + k:g_ssd + k + 1], None, ALU.mult)
                last.then_inc(ut_dve, 1)

            def add_out(first, t):
                for n in range(2):
                    dve.wait_ge(wo_ps, first + 2 * t + n)
                    r = h[:, t, 512 * n:512 * (n + 1)]
                    v.tensor_tensor(r, r, ps[4 + 2 * n + t][:, :], ALU.add).then_inc(h_ok, 1)

            for t in range(TC):
                add_out(3, t)
                norm_chunk(2, t, xn2, h)
            norm_out(2, xT, g_xa)
            for hd in range(XH):
                dve.wait_ge(sc_ps, hd + 1)
                v.tensor_reduce(att[:, 0, 2 * hd:2 * hd + 2], ps[hd][:, :].rearrange("p (t m) -> p t m", t=TC),
                                AX_X, ALU.max, negate=True).then_inc(nmax, 1)
            for hd in range(XH):
                dve.wait_ge(pexp, hd + 1)
                v.reciprocal(att[:, 2, 2 * hd:2 * hd + 2], att[:, 1, 2 * hd:2 * hd + 2])
                dve.drain()
                for t in range(TC):
                    n = 2 * hd + t
                    v.tensor_scalar(pr[:, t, hd, :], pr[:, t, hd, :], att[:, 2, n:n + 1], None,
                                    ALU.mult).then_inc(pn_ok, 1)
            for hd in range(XH):
                dve.wait_ge(pT_ps, hd + 1)
                v.tensor_copy(prT[:, hd, :, :], ps[4 + hd][:, :].rearrange("p (c s) -> p c s", c=2)).then_inc(pT_sb, 1)

            v.memset(rank[:, :, NCOL:NCOL + 4], -1.0)
            dve.wait_ge(ld_g, 32)
            for t in range(TC):
                add_out(7, t)
                norm_chunk(3, t, xn, h, g_ffn)
            norm_out(3, xT, None)
            dve.wait_ge(rt_ps, 1)
            v.tensor_tensor(lg[:, :, :], ps[0][:, 0:2 * NE].rearrange("p (t n) -> p t n", t=TC),
                            b_rt[:, :].unsqueeze(1).to_broadcast([P, TC, NE]), ALU.add)
            dve.drain()
            for t in range(TC):
                v.max(mx8[:, t, :], lg[:, t, :])
            dve.drain()
            v.tensor_scalar(gsum[:, :, 0], mx8[:, :, 0], -1.0, None, ALU.mult).then_inc(lmax, 1)
            for t in range(TC):
                v.max_index(ix8[:, t, :], mx8[:, t, :], lg[:, t, :])
            dve.drain()
            v.tensor_copy(ix8f[:, :, :], ix8[:, :, :])
            dve.drain()
            for t in range(TC):
                v.tensor_scalar(mask[:, t, :], iota[:, 0:NE], ix8f[:, t, 0:1], None, ALU.is_equal)
            for n in range(1, TOPK):
                dve.drain()
                for t in range(TC):
                    v.scalar_tensor_tensor(out=mask[:, t, :], in0=iota[:, 0:NE], scalar=ix8f[:, t, n:n + 1],
                                           in1=mask[:, t, :], op0=ALU.is_equal, op1=ALU.add)
            dve.drain()
            for t in range(TC):
                last = v.tensor_copy(mask4[:, t, :].rearrange("p (c e) -> p c e", e=NE),
                                     mask[:, t, :].unsqueeze(1).to_broadcast([P, CHUNKS, NE]))
            last.then_inc(mask_ok, 1)
            dve.wait_ge(rexp, 1)
            v.tensor_tensor(gate[:, :, :], gate[:, :, :], mask[:, :, :], ALU.mult)
            dve.drain()
            v.tensor_reduce(gsum[:, :, 1], gate[:, :, :], AX_X, ALU.add)
            dve.drain()
            v.reciprocal(gsum[:, :, 0], gsum[:, :, 1])
            dve.drain()
            v.tensor_tensor(gate[:, :, :], gate[:, :, :], gsum[:, :, 0].unsqueeze(2).to_broadcast([P, TC, NE]),
                            ALU.mult).then_inc(gate_ok, 1)
            dve.wait_ge(rank_ps, 1)
            v.scalar_tensor_tensor(out=rank[:, :, 0:NE], in0=ps[1][:, 0:2 * NE].rearrange("p (t n) -> p t n", t=TC),
                                   scalar=1.0, in1=mask[:, :, :], op0=ALU.add, op1=ALU.mult)
            dve.drain()
            for chunk in range(CHUNKS - 1, -1, -1):
                v.tensor_scalar(rank[:, :, NE * chunk:NE * (chunk + 1)], rank[:, :, 0:NE],
                                -1.0 - SLOTS * chunk, None, ALU.add)
            dve.drain()

            def one_hot(column):
                for j in range(2):
                    for t in range(TC):
                        last = v.tensor_scalar(onehot[:, t, SLOTS * j:SLOTS * (j + 1)], iota[:, 0:SLOTS],
                                               rank[:, t, ds(column[j], 1)], None, ALU.is_equal)
                last.then_inc(hot_ok, 1)

            def tokens_lo(count):
                for b in range(2):
                    dve.wait_ge(xh_ok, count + b)
                    v.tensor_tensor(xs[:, 4 * b:4 * b + 4, :, SLOTS:2 * SLOTS],
                                    ps[b][:, :].rearrange("p (k j s) -> p k j s", k=4, j=2),
                                    xs[:, 4 * b:4 * b + 4, :, 0:SLOTS].bitcast(F32), ALU.subtract).then_inc(xs_ok, 1)

            one_hot([0, 1])
            v.memset(scat[:, :, :], 0.0)
            dve.drain()
            v.tensor_copy(scat[:, :, 0:NE], gate[:, :, :]).then_inc(sc_ok, 1)
            dve.wait_ge(cnt_ps, 1)
            v.tensor_tensor(cnt[:, 0:1], ps[3][:, 64:65], col[:, 2:3], ALU.is_gt).then_inc(val_ok, 1)
            tokens_lo(1)
            dve.wait_ge(pos_ps, 1)
            v.tensor_copy(cnt[:, 1:2], ps[3][:, 66:67])
            dve.drain()
            v.tensor_scalar(pick[:, :], iota[:, 0:16], cnt[:, 1:2], cnt[:, 0:1], ALU.is_equal,
                            ALU.mult).then_inc(pick_ok, 1)
            dve.wait_ge(lst_ps, 1)
            v.tensor_scalar(lst[0:1, 0:16], ps[3][0:1, 0:16], float(DUMMY), None, ALU.add)
            v.tensor_copy(lst[0:1, 16:33], ps[3][0:1, 16:33])
            dve.drain()
            v.tensor_copy(lst_i[0:1, 0:33], lst[0:1, 0:33]).then_inc(lst_ok, 1)

            def expert_pass(i, j, further, column, expert):
                def lo(s):
                    n = EPIECES * j + s
                    hi, lo_ = split(s)
                    dve.wait_ge(hi_ok, 2 * EPIECES * i + (n + 1))
                    v.tensor_tensor(lo_, raw(n), hi.bitcast(F32), ALU.subtract).then_inc(lo_ok, 1)

                dve.wait_ge(st_ps, 2 * i + (j + 1))
                for t in range(TC):
                    last = v.tensor_scalar(scat[:, t, :], iota[:, :], rank[:, t, ds(column, 1)],
                                           gate[:, t, ds(expert, 1)], ALU.is_equal, ALU.mult)
                last.then_inc(sc_ok, 1)
                for s in range(10):
                    lo(s)
                for g in range(2):
                    dve.wait_ge(t_ps, 4 * i + (2 * j + g + 1))
                    bias = bguT[:, ds(expert * 16, 16)].rearrange("p (a f) -> p a f", a=2)[
                        :, :, 4 * g:4 * g + 4].unsqueeze(3).to_broadcast([P, 2, 4, SLOTS])
                    v.tensor_tensor(gu[:, g, :, :].rearrange("p (a m) s -> p a m s", a=2),
                                    ps[g][:, :].rearrange("p (a m s) -> p a m s", a=2, m=4), bias,
                                    ALU.add).then_inc(gu_free, 1)
                    dve.drain()
                    v.tensor_scalar(gu[:, g, 0:4, :], gu[:, g, 0:4, :], LIMIT, None, ALU.min).then_inc(gb_ok, 1)
                    v.tensor_scalar(gu[:, g, 4:8, :], gu[:, g, 4:8, :], LIMIT, -LIMIT, ALU.min, ALU.max)
                dve.drain()
                for g in range(2):
                    v.scalar_tensor_tensor(out=gu[:, g, 4:8, :], in0=gu[:, g, 4:8, :], scalar=1.0,
                                           in1=gu[:, g, 0:4, :], op0=ALU.add, op1=ALU.mult)
                dve.drain()
                for g in range(2):
                    dve.wait_ge(sg_ok, 4 * i + (2 * j + g + 1))
                    v.tensor_tensor(act_f[:, 4 * g:4 * g + 4, :], gu[:, g, 4:8, :], sg[:, g, :, :], ALU.mult)
                dve.drain()
                for g in range(2):
                    v.tensor_copy(act_s[:, 4 * g:4 * g + 4, 0:SLOTS], act_f[:, 4 * g:4 * g + 4, :])
                dve.drain()
                for g in range(2):
                    v.tensor_tensor(act_s[:, 4 * g:4 * g + 4, SLOTS:2 * SLOTS],
                                    act_f[:, 4 * g:4 * g + 4, :], act_s[:, 4 * g:4 * g + 4, 0:SLOTS].bitcast(F32),
                                    ALU.subtract).then_inc(av_ok, 1)
                lo(10)
                lo(11)

            with dve.Fori(0, PAIRS, 1) as i:
                dve.wait_ge(gathered, 2 * i + 2)
                one_hot([2 * i + 2, 2 * i + 3])
                expert_pass(i, 0, False, 2 * i, 2 * i)
                expert_pass(i, 1, False, 2 * i + 1, 2 * i + 1)
                tokens_lo(2 * i + 3)
            extra = dve.value_load(lst_i[0:1, 32:33], min_val=0, max_val=MAX_EXTRA)
            with dve.Fori(0, EXTRA_PAIRS, 1) as q:
                with dve.If(extra > 2 * q):
                    column = [dve.value_load(lst_i[0:1, ds(2 * q + j, 1)], min_val=0, max_val=DUMMY)
                              for j in range(2)]
                    expert = [dve.value_load(lst_i[0:1, ds(2 * q + (16 + j), 1)], min_val=0, max_val=NE - 1)
                              for j in range(2)]
                    i = q + PAIRS
                    dve.wait_ge(gathered, 2 * i + 2)
                    one_hot(column)
                    tokens_lo(2 * i + 3)
                    for j in range(2):
                        expert_pass(i, j, True, column[j], expert[j])

            for t in range(TC):
                dve.wait_ge(fsum, t + 1)
                v.tensor_tensor(rst[:, 4, t:t + 1], nrm[:, 4 + t, 0:1], nrm[:, 4 + t, 1:2], ALU.add).then_inc(fadd, 1)
            for t in range(TC):
                dve.wait_ge(stdf, t + 1)
                v.reciprocal(rst[:, 5, t:t + 1], rst[:, 4, t:t + 1])
                dve.drain()
                for n in range(2):
                    last = v.scalar_tensor_tensor(out=h[:, t, 512 * n:512 * (n + 1)], in0=ps[4 + 2 * n + t][:, :],
                                                  scalar=rst[:, 5, t:t + 1], in1=g_fin[:, 512 * n:512 * (n + 1)],
                                                  op0=ALU.mult, op1=ALU.mult)
                last.then_inc(o_ok, 1)


_INS = ["x", "mem", "mixer_norm", "xattn_norm", "mem_norm", "ffn_norm", "ssd_w_in", "ssd_conv_w", "ssd_conv_b",
        "ssd_dt_bias", "ssd_a_log", "ssd_d", "ssd_norm", "ssd_w_out", "xa_w_q", "xa_w_kv", "xa_w_o",
        "moe_w_router", "moe_b_router", "moe_w_gate_up", "moe_b_gate_up", "moe_w_down", "moe_b_down",
        "final_norm"]


def kernel(**inputs):
    import numpy as np
    from concourse import bacc
    from concourse.bass_utils import run_bass_kernel_spmd

    nc = bacc.Bacc("TRN2", target_bir_lowering=False, num_devices=1)
    arrays, args = {}, []
    for name in _INS:
        a = np.ascontiguousarray(inputs[name])
        if name != "final_norm":
            a = a.reshape(a.shape[1:])
        arrays[f"in_{name}"] = a
        args.append(nc.dram_tensor(f"in_{name}", a.shape, mybir.dt.from_np(a.dtype), kind="ExternalInput").ap())
    args.append(nc.dram_tensor("out", (SEQ, D), F32, kind="ExternalOutput").ap())
    build(nc, *args)
    r = run_bass_kernel_spmd(nc, [arrays], core_ids=[0])
    return r.results[0]["out"].reshape(1, SEQ, D)
```

```python
from contextlib import ExitStack

import concourse.bass as bass
from concourse import mybir

F32 = mybir.dt.float32
F32R = mybir.dt.float32r
I32 = mybir.dt.int32
U32 = mybir.dt.uint32
ALU = mybir.AluOpType
ACT = mybir.ActivationFunctionType
AX_X = mybir.AxisListType.X
ds = bass.ds

P = 128
SEQ = 256
TC = SEQ // P
D = 1024
KD = D // P
DI = 2048
HEADS, HD, GROUPS, HPG = 32, 64, 4, 8
GW_ = DI // GROUPS
NCONV = 3072 // P
XH, XHD = 4, 256
NE, TOPK = 32, 4
SLOTS = 64
CHUNKS = SEQ // SLOTS
NCOL = NE * CHUNKS
DUMMY = NCOL
PAIRS = NE // 2
MAX_EXTRA = TOPK * SEQ // (SLOTS + 1)
EXTRA_PAIRS = (MAX_EXTRA + 1) // 2
EPS = 1e-5
LIMIT, ALPHA = 7.0, 1.702
WP = 4096
EP = 2048
EPIECES = 12
RSLOTS = 8
HSLOTS = 4


def build(nc, x, mem, mixer_norm, xattn_norm, mem_norm, ffn_norm, w_in, conv_w, conv_b, dt_bias, a_log,
          d_skip, ssd_norm, w_out, xa_w_q, xa_w_kv, xa_w_o, w_router, b_router, w_gate_up, b_gate_up,
          w_down, b_down, final_norm, out):
    with ExitStack() as ctx:
        def sb(name, shape, dt=F32):
            return ctx.enter_context(nc.sbuf_tensor(name, shape, dt))

        def sem(name):
            return ctx.enter_context(nc.semaphore(name))

        def big(name, floats):
            start = -(-nc.sbuf_base // 32) * 32
            return sb(name, [P, floats]), start

        ring, ring_at = big("ring", (RSLOTS + HSLOTS) * EP)
        wring, wring_at = big("wring", 3 * WP)
        mid, mid_at = big("mid", HSLOTS * EP)
        h = sb("h", [P, TC, D])
        sq, sq_at = big("sq", 2048)

        def part(base, first, end, r=None, **sizes):
            v = base[:, first:end]
            return v.rearrange(r, **sizes) if r else v

        lo_ring = nc.alloc_sbuf_tensor_at("lo_ring", [P, HSLOTS * EP], F32R, offset=ring_at + 4 * RSLOTS * EP)
        hi_ring = nc.alloc_sbuf_tensor_at("hi_ring", [P, HSLOTS * EP], F32R, offset=mid_at)
        wlo = nc.alloc_sbuf_tensor_at("wlo", [P, 3 * WP], F32R, offset=wring_at)
        act_lo = nc.alloc_sbuf_tensor_at("act_lo", [P, 6144], F32R, offset=ring_at)
        uth = nc.alloc_sbuf_tensor_at("uth", [P, 4096], F32R, offset=ring_at + 4 * 12288)
        sq_lo = nc.alloc_sbuf_tensor_at("sq_lo", [P, 2048], F32R, offset=sq_at)
        xT = part(mid, 0, 2048, r="p (k s) -> p k s", k=KD)
        xr = part(mid, 6144, 8192, r="p (k s) -> p k s", k=KD)
        memT = part(mid, 2048, 4096, r="p (k s) -> p k s", k=KD)
        kT = part(mid, 4096, 6144, r="p (k s) -> p k s", k=KD)
        vb = part(mid, 6144, 8192, r="p (t n) -> p t n", t=TC)
        zs = part(ring, 0, 4096, r="p (t n) -> p t n", t=TC)
        yb = part(ring, 4096, 8192, r="p (t n) -> p t n", t=TC)
        xd = part(ring, 8192, 12288, r="p (t n) -> p t n", t=TC)
        uTh = part(uth, 0, 4096, r="p (k s) -> p k s", k=16)
        uTl = part(act_lo, 0, 4096, r="p (k s) -> p k s", k=16)
        x3 = "p (k s) -> p k s"
        xz = part(hi_ring, 4096, 6144, r=x3, k=KD), part(sq_lo, 0, 2048, r=x3, k=KD)
        xq = part(hi_ring, 0, 2048, r=x3, k=KD), part(act_lo, 4096, 6144, r=x3, k=KD)
        xo = part(hi_ring, 0, 2048, r=x3, k=KD), part(hi_ring, 2048, 4096, r=x3, k=KD)
        uT = part(ring, 12288, 16384, r="p (k s) -> p k s", k=16)
        bcT = part(ring, 16384, 18432, r="p (k s) -> p k s", k=8)
        cv = part(ring, 18432, 20480, r="p (b m s) -> p b m s", b=4, m=2)
        btok = part(ring, 18432, 18944, r="p (g n) -> p g n", g=GROUPS)
        xde = part(ring, 18944, 19456)
        ytmp = part(ring, 19456, 19968)
        cbm = part(ring, 19968, 20224, r="p (b l) -> p b l", b=2)
        mt = part(ring, 20480, 22528, r="p (b h l) -> p b h l", b=2, h=HPG)
        du = part(ring, 22528, 24576, r="p (b h l) -> p b h l", b=2, h=HPG)
        rows_a = part(ring, 20480, 20608)
        rows_b = part(ring, 20608, 20736)
        bg_rows = part(ring, 10240, 10752, r="p (n f) -> p n f", n=4)
        xn0 = part(ring, 4096, 6144, r="p (t n) -> p t n", t=TC)
        states = part(sq, 0, 2048, r="p (g n) -> p g n", g=GROUPS)
        xn2 = part(sq, 0, 2048, r="p (t n) -> p t n", t=TC)
        qT = part(sq, 0, 2048, r="p (k s) -> p k s", k=KD)
        g_ffn = part(sq, 0, D)
        mask4 = part(sq, D, D + 2 * NCOL, r="p (t c) -> p t c", t=TC)
        pr = part(ring, 6144, 8192, r="p (t h m) -> p t h m", t=TC, h=XH)
        prT = part(mid, 4096, 6144, r="p (h c s) -> p h c s", h=XH, c=2)
        wslot = [part(wring, WP * s, WP * (s + 1)) for s in range(3)]
        at = [3072]

        def late(n, r=None, **kw):
            v = wring[:, at[0]:at[0] + n]
            at[0] += n
            return v.rearrange(r, **kw) if r else v

        g_fin = late(D)
        xn = late(2048, "p (t n) -> p t n", t=TC)
        xs = part(wlo, 0, 2048, r="p (k j q) -> p k j q", k=KD, j=2)
        act_s = part(wlo, 2048, 3072, r="p (k q) -> p k q", k=KD)
        gus = late(2048)
        gu = late(2 * 512, "p (g m s) -> p g m s", g=2, m=8)
        sg = late(2 * 256, "p (g m s) -> p g m s", g=2, m=4)
        act_f = late(512, "p (k s) -> p k s", k=KD)
        ysb = late(1024)
        onehot = late(256, "p (t s) -> p t s", t=TC)
        scat = late(256, "p (t s) -> p t s", t=TC)
        scatT = late(512, "p (j t) -> p j t", j=2)

        cst = sb("cst", [P, 4, P])
        ident, tri, stri, ones = (cst[:, n, :] for n in range(4))
        wdt = sb("wdt", [P, KD, HEADS])
        wrt = sb("wrt", [P, KD, NE])
        parT = sb("parT", [P, 160])
        convw_c, convb_c, g_mix, g_xa, g_mem, g_ssd = 0, 96, 120, 128, 136, 144
        bguT = sb("bguT", [P, NE * 16])
        stack = sb("stack", [P, SLOTS])
        small = sb("small", [P, 3, HEADS])
        b_rt = sb("b_rt", [P, NE])
        eps = sb("eps", [P, 1])
        warm = sb("warm", [P, 1])
        nrm = sb("nrm", [P, 6, 2])
        rst = sb("rst", [P, 6, 2])
        dtv = sb("dtv", [P, TC, HEADS])
        dta = sb("dta", [P, TC, HEADS])
        dtb_ = sb("dtb_", [P, TC, HEADS])
        acm = sb("acm", [P, TC, HEADS])
        dec = sb("dec", [P, 2, HEADS])
        aneg = sb("aneg", [P, HEADS])
        ssu = sb("ssu", [P, 8])
        rsu = sb("rsu", [P, 8])
        att = sb("att", [P, 3, 8])
        lg = sb("lg", [P, TC, NE])
        mx8 = sb("mx8", [P, TC, 8])
        ix8 = sb("ix8", [P, TC, 8], U32)
        ix8f = sb("ix8f", [P, TC, 8])
        mask = sb("mask", [P, TC, NE])
        gate = sb("gate", [P, TC, NE])
        gsum = sb("gsum", [P, TC, 2])
        rank = sb("rank", [P, TC, NCOL + 4])
        iota_i = sb("iota_i", [P, 2 * SLOTS], I32)
        iota = sb("iota", [P, 2 * SLOTS])
        col_i = sb("col_i", [P, 3], I32)
        col = sb("col", [P, 3])
        cnt = sb("cnt", [P, 3])
        pick = sb("pick", [P, 16])
        lst = sb("lst", [1, 48])
        lst_i = sb("lst_i", [1, 48], I32)

        ps = [ctx.enter_context(nc.psum_tensor(f"ps{b}", [P, 512], F32)) for b in range(8)]

        (ld_x, ld_mem, ld_rows, ld_small, ld_bg, ld_g, ld_bdn, ld_wdt, ld_wrt, cst_step, cst_done) = (
            sem(n) for n in ("ld_x", "ld_mem", "ld_rows", "ld_small", "ld_bg", "ld_g", "ld_bdn", "ld_wdt",
                             "ld_wrt", "cst_step", "cst_done"))
        w_ready = [sem(f"w_ready{s}") for s in range(3)]
        e_ready = [sem(f"e_ready{s}") for s in range(RSLOTS)]
        (e_used, par_ps, par_sb, std, normed, nt_ps, nt_dve, nt_act, dt_ps, dt_e, dt_s, da_ok, ac_ps,
         u_ps, conv_done, silu_done, z_ps, z_done, xs_ps, xs_done, bt_ps, bt_sb, dec_in, dec_ok) = (
            sem(n) for n in ("e_used", "par_ps", "par_sb", "std", "normed", "nt_ps", "nt_dve",
                             "nt_act", "dt_ps", "dt_e", "dt_s", "da_ok", "ac_ps", "u_ps", "conv_done",
                             "silu_done", "z_ps", "z_done", "xs_ps", "xs_done", "bt_ps", "bt_sb", "dec_in",
                             "dec_ok"))
        (du_ok, prep_ps, diff_ok, cb_ok, exp_ok, mt_ok, main_ps, st_ok, xde_ok, y_read, u_ok, ssu_ok, kv_ps,
         kv_sb, stdu, un_ok, ut_ps, ut_hi, ut_lo, wo_ps, h_ok) = (
            sem(n) for n in ("du_ok", "prep_ps", "diff_ok", "cb_ok", "exp_ok", "mt_ok", "main_ps", "st_ok",
                             "xde_ok", "y_read", "u_ok", "ssu_ok", "kv_ps", "kv_sb", "stdu", "un_ok", "ut_ps",
                             "ut_hi", "ut_lo", "wo_ps", "h_ok"))
        (q_ps, q_sb, sc_ps, nmax, pexp, pn_ok, pT_ps, pT_sb, pv_ps, pv_sb) = (
            sem(n) for n in ("q_ps", "q_sb", "sc_ps", "nmax", "pexp", "pn_ok", "pT_ps", "pT_sb", "pv_ps",
                             "pv_sb"))
        (rt_ps, lmax, rexp, mask_ok, gate_ok, rank_ps, cnt_ps, val_ok, pos_ps, pick_ok, lst_ps, lst_ok) = (
            sem(n) for n in ("rt_ps", "lmax", "rexp", "mask_ok", "gate_ok", "rank_ps", "cnt_ps", "val_ok",
                             "pos_ps", "pick_ok", "lst_ps", "lst_ok"))
        stack_ok, fadd, ld_gf, wh_ok, wl_ok, xz_hi, oh_ok = (
            sem(n) for n in ("stack_ok", "fadd", "ld_gf", "wh_ok", "wl_ok", "xz_hi", "oh_ok"))
        tap_ok = sem("tap_ok")
        (hi_ok, lo_ok, hot_ok, gathered, xh_ok, xs_ok, gv_ok, t_ps, gu_free, gb_ok, sg_ok, av_ok, sc_ok, st_ps,
         sT_ok, y_ok, fin_ps, fsum, stdf, o_ok, ld_out) = (
            sem(n) for n in ("hi_ok", "lo_ok", "hot_ok", "gathered", "xh_ok", "xs_ok", "gv_ok", "t_ps",
                             "gu_free", "gb_ok", "sg_ok", "av_ok", "sc_ok", "st_ps", "sT_ok", "y_ok", "fin_ps", "fsum", "stdf", "o_ok", "ld_out"))

        def cols(w, row0, c0):
            return w[row0:row0 + D, c0:c0 + 512].rearrange("(k p) n -> p k n", p=P)

        pieces = [cols(w_in, 0, DI + DI), cols(w_in, 0, DI + DI + 512)]
        pieces += [cols(w_in, 0, DI + 512 * n) for n in range(4)]
        pieces += [cols(w_in, 0, 512 * n) for n in range(4)]
        pieces += [cols(xa_w_kv, 0, 512 * n) for n in range(3)]
        pieces += [cols(w_out, D * k, 512 * n) for k in range(2) for n in range(2)]
        pieces += [cols(xa_w_kv, 0, 512 * 3)]
        pieces += [cols(xa_w_q, 0, 512 * n) for n in range(2)]
        pieces += [cols(xa_w_o, 0, 512 * n) for n in range(2)]
        W_U, W_Z, W_OUT, W_Q, W_O = 0, 6, 13, 18, 20
        KV_PIECE = (10, 11, 12, 17)
        KV_BANK = (0, 1, 0, 1, 0, 1, 0, 7)
        KV_FILL = (2, 1, 1, 1, 1, 1, 1, 1)

        def used(n):
            if n < W_Z:
                return u_ps, 2 * (n - W_U) + 2
            if n < KV_PIECE[0]:
                return z_ps, 2 * (n - W_Z) + 2
            if n in KV_PIECE:
                return kv_ps, 2 * KV_PIECE.index(n) + 2
            if n < W_Q:
                return wo_ps, (1, 2, 5, 6)[n - W_OUT]
            return (q_ps, 2 * (n - W_Q) + 2) if n < W_O else (wo_ps, 9 + n - W_O)

        SPLIT = (2, 3, 4, 5, 6, 7, 8, 9, 13, 14, 15, 16, 18, 19, 20, 21)
        even, odd = ((lo_ring, 2), (lo_ring, 3)), ((lo_ring, 1), (hi_ring, 0))
        over_zs = (act_lo, 0), (act_lo, 1)
        late_ = ((lo_ring, 0), (lo_ring, 1)), ((lo_ring, 2), (lo_ring, 3))
        HI_AT = (even, over_zs, even, over_zs) + (even, odd, even, odd) + 4 * late_
        HI_FREE = ((), (), ((u_ps, 6),) * 2, ((u_ps, 8),) * 2, ((u_ps, 10),) * 2, (), ((z_ps, 1), (z_ps, 2)), ((z_ps, 3), (z_ps, 4)), (), (),
                   ((wo_ps, 1),) * 2, ((wo_ps, 2),) * 2, ((wo_ps, 5),) * 2, ((wo_ps, 6),) * 2,
                   ((q_ps, 2),) * 2, ((q_ps, 4),) * 2)

        def w_parts(n, k):
            base, slot = HI_AT[SPLIT.index(n)][k // 4]
            c0 = EP * slot + 512 * (k % 4)
            return base[:, c0:c0 + 512], wlo[:, WP * (n % 3) + 512 * k:WP * (n % 3) + 512 * (k + 1)]

        def w_half(n, half):
            base, slot = HI_AT[SPLIT.index(n)][half]
            c0 = WP * (n % 3) + EP * half
            return wring[:, c0:c0 + EP], base[:, EP * slot:EP * (slot + 1)], wlo[:, c0:c0 + EP]

        def wpiece(n):
            return wslot[n % 3].rearrange("p (k n) -> p k n", k=KD)

        gu_dram = w_gate_up.rearrange("e (k p) (a g n) -> e g a p k n", p=P, a=2, g=2)
        dn_dram = w_down.rearrange("e (k p) n -> e p k n", p=P)

        def view(base, slot, s):
            return base[:, EP * slot:EP * (slot + 1)].rearrange("p (k n) -> p k n", k=4 if s < 8 else 2)

        def raw(n):
            return view(ring, n % RSLOTS, n % EPIECES)

        def split(s):
            return view(hi_ring, s % HSLOTS, s), view(lo_ring, s % HSLOTS, s)


        def load_expert_piece(sp, e, n):
            s = n % EPIECES
            if s < 8:
                k = 4 * (s // 2 % 2)
                src = gu_dram[e, s // 4, s % 2, :, k:k + 4, :]
            else:
                k = 2 * (s - 8)
                src = dn_dram[e, :, k:k + 2, :]
            sp.dma_start(raw(n), src).then_inc(e_ready[n % RSLOTS], 16)

        block = ctx.enter_context(nc.Block())

        @block.sync
        def _(sp):
            for t in range(TC):
                sp.dma_start(h[:, t, :], x[P * t:P * (t + 1), :]).then_inc(ld_x, 16)
            for r0, v in ((16, mem_norm), (24, ssd_norm)):
                n = v.shape[0] // P
                sp.dma_start(rows_b[r0:r0 + n, :], v.rearrange("(c p) -> c p", p=P)).then_inc(ld_rows, 16)
            sp.wait_ge(ld_rows, 96)
            sp.dma_start(wpiece(0), pieces[0]).then_inc(w_ready[0], 16)
            sp.dma_start(wdt[:, :, :], w_in[:, 5120:5152].rearrange("(k p) n -> p k n", p=P)).then_inc(ld_wdt, 16)
            for n, v in enumerate((dt_bias, a_log, d_skip)):
                sp.dma_start(small[:, n, :], v.partition_broadcast(P)).then_inc(ld_small, 16)
            sp.dma_start(b_rt[:, :], b_router.partition_broadcast(P)).then_inc(ld_small, 16)
            sp.dma_start(bg_rows, b_gate_up.rearrange("e (f q) -> (e f) q", q=P).rearrange(
                "(n p) q -> p n q", p=P)).then_inc(ld_bg, 16)
            sp.dma_start(wpiece(1), pieces[1]).then_inc(w_ready[1], 16)
            sp.dma_start(vb[:, :, :], mem.rearrange("(t p) d -> p t d", p=P)).then_inc(ld_mem, 16)
            sp.dma_start(wpiece(2), pieces[2]).then_inc(w_ready[2], 16)
            sp.dma_start(wrt[:, :, :], w_router.rearrange("(k p) n -> p k n", p=P)).then_inc(ld_wrt, 16)
            for n in range(3, len(pieces)):
                signal, count = used(n - 3)
                sp.wait_ge(signal, count)
                sp.dma_start(wpiece(n), pieces[n]).then_inc(w_ready[n % 3], 16)
            sp.wait_ge(sc_ps, XH)
            sp.dma_start(g_ffn, ffn_norm.partition_broadcast(P)).then_inc(ld_g, 16)
            sp.wait_ge(pT_ps, XH)
            for s in range(RSLOTS):
                load_expert_piece(sp, 0, s)
            sp.wait_ge(wo_ps, 10)
            sp.dma_start(g_fin, final_norm.partition_broadcast(P)).then_inc(ld_gf, 16)
            sp.dma_start(ysb[0:NE, :], b_down).then_inc(ld_bdn, 16)
            with sp.Fori(0, PAIRS - 1, 1) as i:
                for n in range(RSLOTS, RSLOTS + 2 * EPIECES):
                    sp.wait_ge(lo_ok, 2 * EPIECES * i + (n - RSLOTS + 1))
                    load_expert_piece(sp, 2 * i + n // EPIECES, n)
            for n in range(RSLOTS, 2 * EPIECES):
                sp.wait_ge(lo_ok, EPIECES * (NE - 2) + n - RSLOTS + 1)
                load_expert_piece(sp, NE - 2 + n // EPIECES, n)
            sp.wait_ge(lst_ok, 1)
            extra = sp.value_load(lst_i[0:1, 32:33], min_val=0, max_val=MAX_EXTRA)
            with sp.Fori(0, EXTRA_PAIRS, 1) as q:
                with sp.If(extra > 2 * q):
                    for j in range(2):
                        e = sp.value_load(lst_i[0:1, ds(2 * q + (16 + j), 1)], min_val=0, max_val=NE - 1)
                        for n in range(EPIECES * j, EPIECES * (j + 1)):
                            sp.wait_ge(lo_ok, 2 * EPIECES * q + (EPIECES * NE + n - RSLOTS + 1))
                            load_expert_piece(sp, e, n)
            for t in range(TC):
                sp.wait_ge(o_ok, t + 1)
                sp.dma_start(out[P * t:P * (t + 1), :], h[:, t, :]).then_inc(ld_out, 16)
            sp.wait_ge(ld_out, 16 * TC)

        @block.gpsimd
        def _(pool):
            step = [0]

            def settle(ins):
                ins.then_inc(cst_step, 1)
                step[0] += 1
                pool.wait_ge(cst_step, step[0])

            pool.sem_inc(e_used, HSLOTS - 1)
            nc.gpsimd.memset(eps[:, :], EPS)
            nc.gpsimd.memset(ident, 0.0)
            settle(nc.gpsimd.memset(cst[:, 1:4, :], 1.0))
            nc.gpsimd.affine_select(out=ident, in_=ident, compare_op=ALU.not_equal, fill=1.0, base=0,
                                    pattern=[[-1, P]], channel_multiplier=1)
            nc.gpsimd.affine_select(out=tri, in_=tri, compare_op=ALU.is_ge, fill=0.0, base=0,
                                    pattern=[[1, P]], channel_multiplier=-1)
            settle(nc.gpsimd.affine_select(out=stri, in_=stri, compare_op=ALU.is_gt, fill=0.0, base=0,
                                           pattern=[[1, P]], channel_multiplier=-1))
            settle(nc.gpsimd.iota(iota_i[:, :], pattern=[[0, 2], [1, SLOTS]], base=0, channel_multiplier=0))
            for chunk in range(CHUNKS):
                r = slice(NE * chunk, NE * (chunk + 1))
                settle(nc.gpsimd.iota(col_i[r, 0:1], pattern=[[0, 1]], base=NE * chunk - DUMMY, channel_multiplier=1))
                settle(nc.gpsimd.iota(col_i[r, 1:2], pattern=[[0, 1]], base=0, channel_multiplier=1))
                least = SLOTS * chunk if chunk else 2 * SEQ
                settle(nc.gpsimd.iota(col_i[r, 2:3], pattern=[[0, 1]], base=least, channel_multiplier=0))
            nc.gpsimd.tensor_copy(iota[:, :], iota_i[:, :])
            nc.gpsimd.tensor_copy(col[:, :], col_i[:, :]).then_inc(cst_done, 1)
            pool.wait_ge(da_ok, 1)
            pool.wait_ge(z_ps, 8)
            for i in range(2 * GROUPS):
                g, c = i // 2, i % 2
                if i >= 2:
                    pool.wait_ge(prep_ps, i - 1)
                a = dta[:, c, HPG * g:HPG * (g + 1)]
                nc.gpsimd.tensor_tensor(du[:, i % 2, :, :], tri.unsqueeze(1).to_broadcast([P, HPG, P]),
                                        a.unsqueeze(2).to_broadcast([P, HPG, P]), ALU.mult).then_inc(du_ok, 1)

        @block.tensor
        def _(pe):
            mm, tr = nc.tensor.matmul, nc.tensor.transpose

            def take(n):
                pe.wait_ge(w_ready[n % 3], 16 * (n // 3 + 1))
                return wpiece(n)

            pe.wait_ge(cst_done, 1)
            pe.wait_ge(ld_rows, 96)
            tr(ps[7][:, 0:120], rows_a[0:120, :], ident[0:120, 0:120])
            tr(ps[7][:, 128:168], rows_b[0:40, :], ident[0:40, 0:40]).then_inc(par_ps, 1)

            def norm_transposes(n, src, bank0=0, filler=None):
                for t in range(TC):
                    pe.wait_ge(normed, 2 * n + t + 1)
                    for b in range(4):
                        for k in (2 * b, 2 * b + 1):
                            at_ = (k % 2) * SEQ + t * P
                            last = tr(ps[bank0 + b][:, at_:at_ + P], src[:, t, k * P:(k + 1) * P], ident)
                        if t == TC - 1:
                            last.then_inc(nt_ps, 1)
                    if t == 0 and filler:
                        filler(t)

            def await_nt(n):
                pe.wait_ge(nt_dve, 4 * n + 4)
                pe.wait_ge(nt_act, 4 * n + 4)

            norm_transposes(0, xn0)
            await_nt(0)

            def dt_and_biases():
                pe.wait_ge(ld_wdt, 16)
                for t in range(TC):
                    for k in range(KD):
                        last = mm(ps[6][:, HEADS * t:HEADS * (t + 1)], xT[:, k, P * t:P * (t + 1)],
                                  wdt[:, k, :], start=k == 0, stop=k == KD - 1)
                last.then_inc(dt_ps, 1)
                pe.wait_ge(ld_bg, 16)
                for n in range(4):
                    last = tr(ps[5][:, n * P:(n + 1) * P], bg_rows[:, n, :], ident)
                last.then_inc(par_ps, 1)

            def project_T(n, banks, src, done, guard):
                w = take(n)
                for b in range(2):
                    guard(b)
                    for m in range(2):
                        for k in range(KD):
                            c0 = (2 * b + m) * P
                            last = mm(ps[banks[b]][:, SEQ * m:SEQ * (m + 1)], w[:, k, c0:c0 + P], src[:, k, :],
                                      start=k == 0, stop=k == KD - 1)
                    last.then_inc(done, 1)

            def split_tokens(n, t, bank, x_hl, k0=0, ks=range(KD), start=True, stop=True):
                xh, xl = x_hl
                for k in ks:
                    if k % 4 == 0:
                        pe.wait_ge(wl_ok, 2 * SPLIT.index(n) + k // 4 + 1)
                    wh, wl = w_parts(n, k)
                    tok = slice(P * t, P * (t + 1))
                    mm(ps[bank][:, :], xh[:, k0 + k, tok], wh, start=start and k == 0, stop=False)
                    mm(ps[bank][:, :], xh[:, k0 + k, tok], wl, start=False, stop=False)
                    last = mm(ps[bank][:, :], xl[:, k0 + k, tok], wh, start=False, stop=stop and k == KD - 1)
                return last

            def split_T(n, banks, x_hl, done, guard):
                for b in range(2):
                    guard(b)
                    for m in range(2):
                        for k in range(KD):
                            if k % 4 == 0:
                                pe.wait_ge(wl_ok, 2 * SPLIT.index(n) + k // 4 + 1)
                            wh, wl = w_parts(n, k)
                            c0, dst = (2 * b + m) * P, ps[banks[b]][:, SEQ * m:SEQ * (m + 1)]
                            mm(dst, wh[:, c0:c0 + P], x_hl[0][:, k, :], start=k == 0, stop=False)
                            mm(dst, wh[:, c0:c0 + P], x_hl[1][:, k, :], start=False, stop=False)
                            last = mm(dst, wl[:, c0:c0 + P], x_hl[0][:, k, :], start=False, stop=k == KD - 1)
                    last.then_inc(done, 1)

            for p in range(6):
                (project_T if p < 2 else split_T)(W_U + p, (2 * (p % 2), 2 * (p % 2) + 1), xT if p < 2 else xz, u_ps,
                          lambda b: pe.wait_ge(conv_done, 2 * (p - 2) + b + 1) if p >= 2 else None)
                if p == 0:
                    dt_and_biases()
            def x_tokens(q):
                pe.wait_ge(silu_done, 2 * q + 6)
                for t in range(TC):
                    if q >= 1:
                        pe.wait_ge(xs_done, 2 * (q - 1) + t + 1)
                    for m in range(4):
                        last = tr(ps[4 + t][:, P * m:P * (m + 1)], uT[:, 4 * q + m, P * t:P * (t + 1)], ident)
                    last.then_inc(xs_ps, 1)

            for q in range(4):
                for half in range(2):
                    for t in range(TC):
                        if half == 0:
                            if q >= 2:
                                pe.wait_ge(z_done, 2 * (q - 2) + t + 1)
                            else:
                                pe.wait_ge(conv_done, 9 + 2 * q + t)
                        last = split_tokens(W_Z + q, t, 2 * (q % 2) + t, xz, ks=range(4 * half, 4 * half + 4))
                        if half == 1:
                            last.then_inc(z_ps, 1)
                if q == 0:
                    pe.wait_ge(par_sb, 2)
                    pe.wait_ge(dt_e, 1)
                    norm_transposes(1, vb, 4)
                else:
                    if q == 1:
                        await_nt(1)
                    x_tokens(q - 1)
            x_tokens(3)
            for g in range(GROUPS):
                last = tr(ps[7][:, P * g:P * (g + 1)], bcT[:, g, 0:P], ident)
            last.then_inc(bt_ps, 1)
            pe.wait_ge(da_ok, 1)
            for c in range(TC):
                mm(ps[6][:, 32 * c:32 * c + 32], tri, dta[:, c, :], start=True, stop=True)
            mm(ps[6][:, 64:96], ones, dta[:, 0, :], start=True, stop=True).then_inc(ac_ps, 1)

            def prep(i):
                g, c = i // 2, i % 2
                pe.wait_ge(du_ok, i + 1)
                if i:
                    pe.wait_ge(diff_ok, i)
                    pe.wait_ge(cb_ok, i)
                else:
                    pe.wait_ge(z_done, 8)
                    pe.wait_ge(xs_done, 8)
                for b in range(2):
                    mm(ps[2 + b][:, :], ones, du[:, i % 2, 4 * b:4 * b + 4, :], start=True, stop=True)
                mm(ps[4][:, 0:P], bcT[:, g, P * c:P * (c + 1)], bcT[:, 4 + g, P * c:P * (c + 1)],
                   start=True, stop=True).then_inc(prep_ps, 1)

            def keys_values(quarter):
                i, half = quarter // 2, quarter // 2 % 2
                w = take(KV_PIECE[i // 2])
                bank = ps[KV_BANK[i]]
                if 2 <= i < 6 and quarter % 2 == 0:
                    pe.wait_ge(kv_sb, i - 1)
                if i < 4:
                    m = quarter % 2
                    for k in range(KD):
                        c0 = (2 * half + m) * P
                        last = mm(bank[:, SEQ * m:SEQ * (m + 1)], w[:, k, c0:c0 + P], memT[:, k, :],
                                  start=k == 0, stop=k == KD - 1)
                else:
                    for k in range(4 * (quarter % 2), 4 * (quarter % 2) + 4):
                        last = mm(bank[:, :], memT[:, k, P * half:P * (half + 1)], w[:, k, :],
                                  start=k == 0, stop=k == KD - 1)
                if quarter % 2:
                    last.then_inc(kv_ps, 1)

            def scan(i):
                g, c = i // 2, i % 2
                pe.wait_ge(mt_ok, i + 1)
                if i:
                    pe.wait_ge(y_read, i)
                for j in range(HPG):
                    c0 = GW_ * g + HD * j
                    last = mm(ps[5][:, HD * j:HD * (j + 1)], mt[:, i % 2, j, :], xd[:, c, c0:c0 + HD],
                              start=True, stop=True)
                if c == 0:
                    pe.wait_ge(xde_ok, g + 1)
                    pe.wait_ge(bt_sb, 1)
                    if g == 0:
                        pe.wait_ge(dec_in, 1)
                    mm(ps[6][:, :], btok[:, g, :], xde, start=True, stop=True).then_inc(main_ps, 1)
                else:
                    pe.wait_ge(st_ok, g + 1)
                    mm(ps[6][:, :], bcT[:, 4 + g, P:2 * P], states[:, g, :], start=True,
                       stop=True).then_inc(main_ps, 1)

            prep(0)
            quarter = 0
            for i in range(2 * GROUPS):
                for _ in range(KV_FILL[i]):
                    keys_values(quarter)
                    quarter += 1
                if i + 1 < 2 * GROUPS:
                    prep(i + 1)
                scan(i)
            for quarter in range(quarter, 12):
                keys_values(quarter)
            pe.wait_ge(diff_ok, 8)
            for j in range(8):
                if j == 2:
                    pe.wait_ge(kv_sb, 6)
                pe.wait_ge(un_ok, 2 * (j // 2) + 2)
                if j >= 4:
                    pe.wait_ge(ut_lo, j - 3)
                for k in (2 * j, 2 * j + 1):
                    for t in range(TC):
                        at_ = (k % 2) * SEQ + t * P
                        last = tr(ps[(j + 2) % 4][:, at_:at_ + P], yb[:, t, k * P:(k + 1) * P], ident)
                last.then_inc(ut_ps, 1)
            pe.wait_ge(y_read, 8)
            for kh in range(2):
                pe.wait_ge(ut_lo, 4 * kh + 4)
                for n, t in ((0, 0), (0, 1), (1, 0), (1, 1)) if kh == 0 else ((0, 0), (1, 0), (0, 1), (1, 1)):
                    last = split_tokens(W_OUT + 2 * kh + n, t, 4 + 2 * n + t, (uTh, uTl), k0=KD * kh,
                                        start=kh == 0, stop=kh == 1)
                    if t == 1 or kh == 1:
                        last.then_inc(wo_ps, 1)

            keys_values(12)
            keys_values(13)
            pe.wait_ge(kv_sb, 7)
            norm_transposes(2, xn2)
            await_nt(2)
            for a in range(2):
                split_T(W_Q + a, (4 + 2 * a, 5 + 2 * a), xq, q_ps, lambda b: None)
            for hd in range(XH):
                pe.wait_ge(q_sb, hd + 1)
                for t in range(TC):
                    for kk in (2 * hd, 2 * hd + 1):
                        last = mm(ps[hd][:, SEQ * t:SEQ * (t + 1)], qT[:, kk, P * t:P * (t + 1)], kT[:, kk, :],
                                  start=kk == 2 * hd, stop=kk == 2 * hd + 1)
                last.then_inc(sc_ps, 1)
            keys_values(14)
            keys_values(15)
            for hd in range(XH):
                if hd == XH - 1:
                    pe.wait_ge(kv_sb, 8)
                pe.wait_ge(pn_ok, 2 * hd + 2)
                for mc in range(2):
                    for t in range(TC):
                        at_ = mc * SEQ + t * P
                        last = tr(ps[4 + hd][:, at_:at_ + P], pr[:, t, hd, P * mc:P * (mc + 1)], ident)
                last.then_inc(pT_ps, 1)
            for hd in range(XH):
                pe.wait_ge(pT_sb, hd + 1)
                for dv in range(2):
                    for mc in range(2):
                        c0 = XHD * hd + P * dv
                        last = mm(ps[hd][:, SEQ * dv:SEQ * (dv + 1)], vb[:, mc, c0:c0 + P], prT[:, hd, mc, :],
                                  start=mc == 0, stop=mc == 1)
                last.then_inc(pv_ps, 1)
            pe.wait_ge(pv_sb, XH)
            for t in range(TC):
                for n in range(2):
                    split_tokens(W_O + n, t, 4 + 2 * n + t, xo).then_inc(wo_ps, 1)

            def start_sums(t):
                for n in range(2):
                    mm(ps[4 + 2 * n + t][:, :], ident, h[:, t, 512 * n:512 * (n + 1)], start=True, stop=True)

            norm_transposes(3, xn, 0, start_sums)
            await_nt(3)
            pe.wait_ge(ld_wrt, 16)
            for t in range(TC):
                for k in range(KD):
                    last = mm(ps[0][:, NE * t:NE * (t + 1)], xr[:, k, P * t:P * (t + 1)], wrt[:, k, :],
                              start=k == 0, stop=k == KD - 1)
            last.then_inc(rt_ps, 1)
            start_sums(1)
            pe.wait_ge(mask_ok, 1)
            mm(ps[1][:, 0:NE], stri, mask[:, 0, :], start=True, stop=True)
            mm(ps[1][:, NE:2 * NE], stri, mask[:, 1, :], start=True, stop=False)
            mm(ps[1][:, NE:2 * NE], ones, mask[:, 0, :], start=False, stop=True).then_inc(rank_ps, 1)
            for t in range(TC):
                last = mm(ps[3][:, 64:65], mask4[:, t, :], ones[:, 0:1], start=t == 0, stop=t == TC - 1)
            last.then_inc(cnt_ps, 1)
            def scatter_transpose(bank, count):
                pe.wait_ge(sc_ok, count)
                for t in range(TC):
                    last = tr(ps[bank][:, P * t:P * (t + 1)], scat[:, t, :], ident)
                last.then_inc(st_ps, 1)

            def scatter(j, y_count, t_count):
                pe.wait_ge(y_ok, y_count)
                pe.wait_ge(sT_ok, t_count)
                for n in range(2):
                    for t in range(TC):
                        last = mm(ps[4 + 2 * n + t][:, :], scatT[:, j, P * t:P * (t + 1)],
                                  ysb[:, 512 * n:512 * (n + 1)], start=False, stop=True,
                                  skip_group_check=True)
                return last

            def gather(count):
                pe.wait_ge(hot_ok, count)
                for k in range(KD):
                    for t in range(TC):
                        last = mm(ps[k // 4][:, P * (k % 4):P * (k % 4 + 1)], xn[:, t, P * k:P * (k + 1)],
                                  onehot[:, t, :], start=t == 0, stop=t == TC - 1)
                    if k % 4 == 3:
                        last.then_inc(gathered, 1)

            gather(1)
            pe.wait_ge(stack_ok, 1)
            scatter_transpose(2, 1)
            pe.wait_ge(val_ok, 1)
            mm(ps[3][:, 66:67], stri, cnt[:, 0:1], start=True, stop=True).then_inc(pos_ps, 1)
            pe.wait_ge(pick_ok, 1)
            mm(ps[3][0:1, 0:16], col[:, 0:1], pick[:, :], start=True, stop=True)
            mm(ps[3][0:1, 16:32], col[:, 1:2], pick[:, :], start=True, stop=True)
            mm(ps[3][0:1, 32:33], cnt[:, 0:1], ones[:, 0:1], start=True, stop=True).then_inc(lst_ps, 1)
            pe.wait_ge(ld_bdn, 16)
            pe.wait_ge(sT_ok, 1)
            pe.wait_ge(lst_ok, 1)
            for n in range(2):
                last = mm(ps[2 + n][:, :], ident[0:NE, :], ysb[0:NE, 512 * n:512 * (n + 1)], start=True, stop=True)
            last.then_inc(e_used, 1)

            def expert_pass(i, j, further, last_round=False):
                def parts(s):
                    pe.wait_ge(lo_ok, 2 * EPIECES * i + (EPIECES * j + s + 1))
                    return split(s)

                if j == 0:
                    pe.wait_ge(xs_ok, 2 * i + 2)
                else:
                    pe.wait_ge(gu_free, 4 * i + 2)
                for g in range(2):
                    if g == 1:
                        pe.wait_ge(y_ok, 4 * i + (2 * j + 2))
                    for s in range(4 * g, 4 * g + 4):
                        a, k0 = s % 2, 4 * (s // 2 % 2)
                        w = parts(s)
                        for kk in range(4):
                            k = k0 + kk
                            for h_l in range(2):
                                last = mm(ps[2 * g + a][:, :], xs[:, k, j, :], w[h_l][:, kk, :],
                                          start=k == 0 and h_l == 0, stop=k == KD - 1 and h_l == 1)
                        last.then_inc(e_used, 1)
                for g in range(2):
                    pe.wait_ge(gv_ok, 8 * i + (4 * j + 2 * g + 2))
                    for f in range(8):
                        c0 = 1024 * g + P * f
                        last = mm(ps[g][:, SLOTS * f:SLOTS * (f + 1)], gus[:, c0:c0 + P], stack[:, :],
                                  start=True, stop=True)
                    last.then_inc(t_ps, 1)
                scatter_transpose(2, 2 * i + (j + 2))
                if not further:
                    scatter(1 - j, 4 * i + (2 * j + 2), 2 * i + (j + 1))
                    if j == 1 and not last_round:
                        pe.wait_ge(gu_free, 4 * i + 4)
                        gather(i + 2)
                pe.wait_ge(sT_ok, 2 * i + (j + 2))
                for s in range(8, EPIECES):
                    if s % 2 == 0:
                        pe.wait_ge(av_ok, 4 * i + (2 * j + (s - 8) // 2 + 1))
                    w = parts(s)
                    for kk in range(2):
                        k = 2 * (s - 8) + kk
                        for n in range(2):
                            for h_l in range(2):
                                last = mm(ps[2 + n][:, :], act_s[:, k, :],
                                          w[h_l][:, kk, 512 * n:512 * (n + 1)],
                                          start=k == 0 and h_l == 0, stop=k == KD - 1 and h_l == 1)
                    last.then_inc(e_used, 1)
                if further:
                    scatter(j, 4 * i + (2 * j + 4), 2 * i + (j + 2))

            with pe.Fori(0, PAIRS - 1, 1) as i:
                expert_pass(i, 0, False)
                expert_pass(i, 1, False)
            expert_pass(PAIRS - 1, 0, False, True)
            expert_pass(PAIRS - 1, 1, False, True)
            scatter(1, 2 * NE + 2, NE + 1)
            extra = pe.value_load(lst_i[0:1, 32:33], min_val=0, max_val=MAX_EXTRA)
            with pe.Fori(PAIRS, PAIRS + EXTRA_PAIRS, 1) as i:
                with pe.If(extra > 2 * i - 2 * PAIRS):
                    pe.wait_ge(gu_free, 4 * i)
                    gather(i + 1)
                    expert_pass(i, 0, True)
                    expert_pass(i, 1, True)
            mm(ps[0][:, 0:1], ones, ones[:, 0:1], start=True, stop=True).then_inc(fin_ps, 1)

        @block.scalar
        def _(act):
            def fn(out_, in_, func, **kw):
                return nc.scalar.activation(out_, in_, func, **kw)

            act.dma_start(rows_a[0:96, :], conv_w.rearrange("j (c p) -> (j c) p", p=P)).then_inc(ld_rows, 16)
            act.dma_start(rows_a[96:120, :], conv_b.rearrange("(c p) -> c p", p=P)).then_inc(ld_rows, 16)
            for r0, v in ((0, mixer_norm), (8, xattn_norm)):
                act.dma_start(rows_b[r0:r0 + KD, :], v.rearrange("(c p) -> c p", p=P)).then_inc(ld_rows, 16)

            def norm_stats(n, src, junk):
                for t in range(TC):
                    if n >= 2:
                        act.wait_ge(h_ok, 4 * (n - 2) + 2 * t + 2)
                    fn(junk[:, t, :], src[:, t, :], ACT.Square, accum_out=nrm[:, n, t:t + 1])
                    act.drain()
                    fn(nrm[:, n, t:t + 1], nrm[:, n, t:t + 1], ACT.Sqrt, bias=eps[:, 0:1],
                       scale=1.0 / D).then_inc(std, 1)

            def load_sqrt():
                fn(warm[:, 0:1], eps[:, 0:1], ACT.Sqrt)
                act.drain()

            def norm_out(n, dst, gains, bank0=0):
                for k in range(4, KD):
                    act.wait_ge(nt_ps, 4 * n + k // 2 + 1)
                    src = ps[bank0 + k // 2][:, SEQ * (k % 2):SEQ * (k % 2 + 1)]
                    scale = 1.0 if gains is None else parT[:, gains + k:gains + k + 1]
                    fn(dst[:, k, :], src, ACT.Copy, scale=scale).then_inc(nt_act, 1)

            def w_hi(n, half):
                i = SPLIT.index(n)
                act.wait_ge(w_ready[n % 3], 16 * (n // 3 + 1))
                if HI_FREE[i]:
                    signal, count = HI_FREE[i][half]
                    act.wait_ge(signal, count)
                raw_, hi, _ = w_half(n, half)
                fn(hi, raw_, ACT.Copy).then_inc(wh_ok, 1)

            act.wait_ge(cst_done, 1)
            load_sqrt()
            act.wait_ge(ld_x, 32)
            norm_stats(0, h, xn0)
            act.wait_ge(par_sb, 1)
            norm_out(0, xT, g_mix)
            act.wait_ge(nt_dve, 4)
            act.drain()
            fn(xz[0], xT[:, :, :], ACT.Copy).then_inc(xz_hi, 1)
            w_hi(2, 0)
            w_hi(2, 1)
            act.wait_ge(ld_small, 64)
            fn(aneg[:, :], small[:, 1, :], ACT.Exp)
            act.wait_ge(dt_e, 1)
            fn(dta[:, :, :], dta[:, :, :], ACT.Exp).then_inc(dt_s, 1)
            act.wait_ge(ld_mem, 16)
            norm_stats(1, vb, part(ring, 8192, 10240, r="p (t n) -> p t n", t=TC))
            def tap(n):
                p, b = n // 2, n % 2
                c0 = (16 + 4 * p if p < 2 else 4 * (p - 2)) + 2 * b
                act.wait_ge(u_ps, n + 1)
                if n >= 4:
                    act.wait_ge(silu_done, n - 3)
                for m in range(2):
                    w = convw_c + 3 * NCONV + c0 + m
                    last = fn(cv[:, n % 4, m, :], ps[2 * (p % 2) + b][:, SEQ * m:SEQ * (m + 1)], ACT.Identity,
                              scale=parT[:, w:w + 1], bias=parT[:, convb_c + c0 + m:convb_c + c0 + m + 1])
                last.then_inc(tap_ok, 1)

            tap(0)
            for n in range(12):
                if n + 1 < 12:
                    tap(n + 1)
                if 2 <= n < 10:
                    w_hi(3 + (n - 2) // 2, n % 2)
                act.wait_ge(conv_done, n + 1)
                p, b = n // 2, n % 2
                dst = bcT[:, 4 * p + 2 * b:4 * p + 2 * b + 2, :] if p < 2 else \
                    uT[:, 4 * (p - 2) + 2 * b:4 * (p - 2) + 2 * b + 2, :]
                fn(dst, cv[:, n % 4, :, :], ACT.Silu).then_inc(silu_done, 1)
            act.drain()
            w_hi(W_Z + 1, 0)
            w_hi(W_Z + 1, 1)
            norm_out(1, memT, g_mem, 4)
            for n in range(8):
                q, t = n // 2, n % 2
                act.wait_ge(z_ps, n + 1)
                fn(zs[:, t, 512 * q:512 * (q + 1)], ps[2 * (q % 2) + t][:, :], ACT.Silu).then_inc(z_done, 1)
                if q < 2:
                    w_hi(W_Z + q + 2, t)
            act.wait_ge(bt_ps, 1)
            act.drain()
            fn(btok, ps[7][:, :].rearrange("p (g n) -> p g n", g=GROUPS), ACT.Copy).then_inc(bt_sb, 1)
            act.wait_ge(dec_in, 1)
            fn(dec[:, :, :], dec[:, :, :], ACT.Exp).then_inc(dec_ok, 1)

            def square_u(i):
                g, c = i // 2, i % 2
                u = slice(GW_ * g, GW_ * (g + 1))
                act.wait_ge(u_ok, i + 1)
                fn(zs[:, c, u], yb[:, c, u], ACT.Square, accum_out=ssu[:, i:i + 1])

            def state_out(i):
                if i % 2 == 0:
                    act.wait_ge(main_ps, i + 1)
                    fn(states[:, i // 2, :], ps[6][:, :], ACT.Copy).then_inc(st_ok, 1)

            def kv_out(i):
                act.wait_ge(kv_ps, i + 1)
                src = ps[KV_BANK[i]][:, :]
                if i < 4:
                    fn(kT[:, 2 * i:2 * i + 2, :], src.rearrange("p (m s) -> p m s", m=2),
                       ACT.Copy).then_inc(kv_sb, 1)
                else:
                    n = (i - 4) // 2
                    fn(vb[:, i % 2, 512 * n:512 * (n + 1)], src, ACT.Copy).then_inc(kv_sb, 1)

            for i in range(2 * GROUPS):
                act.wait_ge(diff_ok, i + 1)
                fn(mt[:, i % 2, :, :], mt[:, i % 2, :, :], ACT.Exp).then_inc(exp_ok, 1)
                for half in range(sum(KV_FILL[:i]) // 2, sum(KV_FILL[:i + 1]) // 2):
                    kv_out(half)
                if i:
                    state_out(i - 1)
                    square_u(i - 1)
            square_u(2 * GROUPS - 1)
            act.drain()
            fn(rsu[:, :], ssu[:, :], ACT.Sqrt, bias=eps[:, 0:1], scale=1.0 / GW_).then_inc(stdu, 1)
            w_hi(W_OUT, 0)
            w_hi(W_OUT, 1)
            for half in range(sum(KV_FILL) // 2, 6):
                kv_out(half)
                if half == 4:
                    w_hi(W_OUT + 1, 0)
            for j in range(8):
                act.wait_ge(ut_ps, j + 1)
                for k in (2 * j, 2 * j + 1):
                    last = fn(uTh[:, k, :], ps[(j + 2) % 4][:, SEQ * (k % 2):SEQ * (k % 2 + 1)], ACT.Copy,
                              scale=parT[:, g_ssd + k:g_ssd + k + 1])
                last.then_inc(ut_hi, 1)
            w_hi(W_OUT + 1, 1)
            for n in (2, 3):
                w_hi(W_OUT + n, 0)
                w_hi(W_OUT + n, 1)

            norm_stats(2, h, xn2)
            w_hi(W_Q, 0)
            kv_out(6)
            for b in range(4):
                act.wait_ge(nt_ps, 8 + b + 1)
                for k in (2 * b, 2 * b + 1):
                    last = fn(xq[0][:, k, :], ps[b][:, SEQ * (k % 2):SEQ * (k % 2 + 1)], ACT.Copy,
                              scale=parT[:, g_xa + k:g_xa + k + 1])
                last.then_inc(nt_act, 1)
            w_hi(W_Q, 1)
            w_hi(W_Q + 1, 0)
            w_hi(W_Q + 1, 1)
            for b in range(4):
                act.wait_ge(q_ps, b + 1)
                fn(qT[:, 2 * b:2 * b + 2, :], ps[4 + b][:, :].rearrange("p (m s) -> p m s", m=2), ACT.Copy,
                   scale=XHD ** -0.5).then_inc(q_sb, 1)
            for hd in range(XH):
                act.wait_ge(nmax, hd + 1)
                for t in range(TC):
                    n = 2 * hd + t
                    last = fn(pr[:, t, hd, :], ps[hd][:, SEQ * t:SEQ * (t + 1)], ACT.Exp,
                              bias=att[:, 0, n:n + 1], accum_out=att[:, 1, n:n + 1])
                last.then_inc(pexp, 1)
            kv_out(7)
            for hd in range(XH):
                act.wait_ge(pv_ps, hd + 1)
                fn(xo[0][:, 2 * hd:2 * hd + 2, :], ps[hd][:, :].rearrange("p (m s) -> p m s", m=2),
                   ACT.Copy).then_inc(oh_ok, 1)
                if hd >= 2:
                    w_hi(W_O, hd - 2)
            w_hi(W_O + 1, 0)
            w_hi(W_O + 1, 1)

            def tokens_hi(count):
                for b in range(2):
                    act.wait_ge(gathered, count + b)
                    fn(xs[:, 4 * b:4 * b + 4, :, 0:SLOTS],
                       ps[b][:, :].rearrange("p (k j s) -> p k j s", k=4, j=2), ACT.Copy).then_inc(xh_ok, 1)

            def scatter_out(j, bank, count):
                act.wait_ge(st_ps, count)
                fn(scatT[:, j, :], ps[bank][:, 0:SEQ], ACT.Copy).then_inc(sT_ok, 1)

            def down_out(used_count):
                act.wait_ge(e_used, used_count)
                for n in range(2):
                    fn(ysb[:, 512 * n:512 * (n + 1)], ps[2 + n][:, :], ACT.Copy).then_inc(y_ok, 1)

            def hi(s, i, j):
                n = EPIECES * j + s
                act.wait_ge(e_ready[n % RSLOTS], 48 * i + 16 * (n // RSLOTS + 1))
                act.wait_ge(e_used, 2 * EPIECES * i + (n + 1))
                fn(split(s)[0], raw(n), ACT.Copy).then_inc(hi_ok, 1)

            load_sqrt()
            norm_stats(3, h, xn)
            act.wait_ge(wo_ps, 10)
            hi(0, 0, 0)
            norm_out(3, xr, None)
            hi(1, 0, 0)
            hi(2, 0, 0)
            act.wait_ge(lmax, 1)
            for t in range(TC):
                last = fn(gate[:, t, :], lg[:, t, :], ACT.Exp, bias=gsum[:, t, 0:1])
            last.then_inc(rexp, 1)

            tokens_hi(1)
            scatter_out(1, 2, 1)
            hi(3, 0, 0)

            def expert_pass(i, j, further, last_round=False):
                def gate_up_out(g):
                    act.wait_ge(e_used, 2 * EPIECES * i + (HSLOTS + EPIECES * j + 4 * g + 4))
                    for a in range(2):
                        c0 = 1024 * g + 512 * a
                        fn(gus[:, c0:c0 + 512], ps[2 * g + a][:, :], ACT.Copy).then_inc(gv_ok, 1)

                if further:
                    for s in range(4):
                        hi(s, i, j)
                else:
                    down_out(2 * EPIECES * i + (HSLOTS + EPIECES * j))
                hi(4, i, j)
                hi(5, i, j)
                gate_up_out(0)
                for s in range(6, 10):
                    hi(s, i, j)
                gate_up_out(1)
                hi(10, i, j)
                for g in range(2):
                    act.wait_ge(gb_ok, 4 * i + (2 * j + g + 1))
                    fn(sg[:, g, :, :], gu[:, g, 0:4, :], ACT.Sigmoid, scale=ALPHA).then_inc(sg_ok, 1)
                scatter_out(j, 2, 2 * i + (j + 2))
                hi(11, i, j)
                if further:
                    down_out(2 * EPIECES * i + (HSLOTS + EPIECES * (j + 1)))
                elif j == 1 and not last_round:
                    tokens_hi(2 * i + 3)
                if not further and j == 0:
                    for s in range(4):
                        hi(s, i, 1)
                elif not further and not last_round:
                    for s in range(4):
                        hi(s, i + 1, 0)

            with act.Fori(0, PAIRS - 1, 1) as i:
                expert_pass(i, 0, False)
                expert_pass(i, 1, False)
            expert_pass(PAIRS - 1, 0, False, True)
            expert_pass(PAIRS - 1, 1, False, True)
            down_out(HSLOTS + EPIECES * NE)
            act.wait_ge(lst_ok, 1)
            extra = act.value_load(lst_i[0:1, 32:33], min_val=0, max_val=MAX_EXTRA)
            with act.Fori(PAIRS, PAIRS + EXTRA_PAIRS, 1) as i:
                with act.If(extra > 2 * i - 2 * PAIRS):
                    tokens_hi(2 * i + 1)
                    expert_pass(i, 0, True)
                    expert_pass(i, 1, True)
            load_sqrt()
            act.wait_ge(fin_ps, 1)
            for t in range(TC):
                for n in range(2):
                    last = fn(xn[:, t, 512 * n:512 * (n + 1)], ps[4 + 2 * n + t][:, :], ACT.Square,
                              accum_out=nrm[:, 4 + t, n:n + 1])
                last.then_inc(fsum, 1)
            for t in range(TC):
                act.wait_ge(fadd, t + 1)
                fn(rst[:, 4, t:t + 1], rst[:, 4, t:t + 1], ACT.Sqrt, bias=eps[:, 0:1],
                   scale=1.0 / D).then_inc(stdf, 1)

        @block.vector
        def _(dve):
            v = nc.vector
            dve.wait_ge(cst_done, 1)
            v.tensor_tensor(stack[:, :], ident[:, 0:SLOTS], ident[:, SLOTS:P], ALU.add).then_inc(stack_ok, 1)
            dve.wait_ge(par_ps, 1)
            v.tensor_copy(parT[:, 0:120], ps[7][:, 0:120])
            v.tensor_copy(parT[:, 120:160], ps[7][:, 128:168]).then_inc(par_sb, 1)

            def norm_chunk(n, t, dst, src, gains=None):
                dve.wait_ge(std, 2 * n + t + 1)
                v.reciprocal(rst[:, n, t:t + 1], nrm[:, n, t:t + 1])
                dve.drain()
                if gains is None:
                    v.tensor_scalar(dst[:, t, :], src[:, t, :], rst[:, n, t:t + 1], None,
                                    ALU.mult).then_inc(normed, 1)
                else:
                    v.scalar_tensor_tensor(out=dst[:, t, :], in0=src[:, t, :], scalar=rst[:, n, t:t + 1],
                                           in1=gains, op0=ALU.mult, op1=ALU.mult).then_inc(normed, 1)

            def norm_out(n, dst, gains, bank0=0):
                for k in range(4):
                    dve.wait_ge(nt_ps, 4 * n + k // 2 + 1)
                    src = ps[bank0 + k // 2][:, SEQ * (k % 2):SEQ * (k % 2 + 1)]
                    if gains is None:
                        v.tensor_copy(dst[:, k, :], src).then_inc(nt_dve, 1)
                    else:
                        v.tensor_scalar(dst[:, k, :], src, parT[:, gains + k:gains + k + 1], None,
                                        ALU.mult).then_inc(nt_dve, 1)

            def w_lo(n, half):
                raw_, hi, lo_ = w_half(n, half)
                dve.wait_ge(wh_ok, 2 * SPLIT.index(n) + half + 1)
                v.tensor_tensor(lo_, raw_, hi.bitcast(F32), ALU.subtract).then_inc(wl_ok, 1)

            for t in range(TC):
                norm_chunk(0, t, xn0, h)
            norm_out(0, xT, g_mix)
            dve.wait_ge(xz_hi, 1)
            v.tensor_tensor(xz[1], xT[:, :, :], xz[0].bitcast(F32), ALU.subtract)
            w_lo(2, 0)
            w_lo(2, 1)
            dve.wait_ge(dt_ps, 1)
            dve.wait_ge(ld_small, 64)
            v.tensor_tensor(dtv[:, :, :], ps[6][:, 0:64].rearrange("p (t n) -> p t n", t=TC),
                            small[:, 0, :].unsqueeze(1).to_broadcast([P, TC, HEADS]), ALU.add)
            dve.drain()
            v.tensor_scalar(dta[:, :, :], dtv[:, :, :], 0.0, None, ALU.min)
            dve.drain()
            v.tensor_scalar(dtv[:, :, :], dtv[:, :, :], 0.0, None, ALU.max)
            dve.drain()
            v.tensor_tensor(dta[:, :, :], dta[:, :, :], dtv[:, :, :], ALU.subtract).then_inc(dt_e, 1)
            dve.wait_ge(dt_s, 1)
            v.tensor_scalar(dtb_[:, :, :], dta[:, :, :], 2.0, None, ALU.add)
            dve.drain()
            v.reciprocal(dtb_[:, :, :], dtb_[:, :, :])
            dve.drain()
            v.tensor_tensor(dta[:, :, :], dta[:, :, :], dtb_[:, :, :], ALU.mult)
            dve.drain()
            v.tensor_tensor(dtb_[:, :, :], dta[:, :, :], dta[:, :, :], ALU.mult)
            dve.drain()
            v.tensor_scalar(acm[:, :, :], dtb_[:, :, :], 1.0 / 17, None, ALU.mult)
            for n in (15, 13, 11, 9, 7, 5, 3):
                dve.drain()
                v.scalar_tensor_tensor(out=acm[:, :, :], in0=acm[:, :, :], scalar=1.0 / n, in1=dtb_[:, :, :],
                                       op0=ALU.add, op1=ALU.mult)
            dve.drain()
            v.scalar_tensor_tensor(out=dta[:, :, :], in0=acm[:, :, :], scalar=1.0, in1=dta[:, :, :],
                                   op0=ALU.add, op1=ALU.mult)
            dve.drain()
            v.scalar_tensor_tensor(out=dtv[:, :, :], in0=dta[:, :, :], scalar=2.0, in1=dtv[:, :, :],
                                   op0=ALU.mult, op1=ALU.add)
            dve.drain()
            for t in range(TC):
                last = v.scalar_tensor_tensor(out=dta[:, t, :], in0=dtv[:, t, :], scalar=-1.0, in1=aneg[:, :],
                                              op0=ALU.mult, op1=ALU.mult)
            last.then_inc(da_ok, 1)
            dve.wait_ge(par_ps, 2)
            v.tensor_copy(bguT[:, :], ps[5][:, :]).then_inc(par_sb, 1)

            for n in range(12):
                if n == 8:
                    for t in range(TC):
                        norm_chunk(1, t, vb, vb)
                if 3 <= n < 11:
                    w_lo(3 + (n - 3) // 2, (n - 3) % 2)
                p, b = n // 2, n % 2
                c0 = (16 + 4 * p if p < 2 else 4 * (p - 2)) + 2 * b
                dve.wait_ge(tap_ok, n + 1)
                for j in (2, 1, 0):
                    if j < 2:
                        dve.drain()
                    for m in range(2):
                        w = convw_c + j * NCONV + c0 + m
                        back = 3 - j
                        src = ps[2 * (p % 2) + b][:, SEQ * m:SEQ * (m + 1) - back]
                        last = v.scalar_tensor_tensor(out=cv[:, n % 4, m, back:], in0=src,
                                                      scalar=parT[:, w:w + 1], in1=cv[:, n % 4, m, back:],
                                                      op0=ALU.mult, op1=ALU.add)
                last.then_inc(conv_done, 1)
            w_lo(W_Z + 1, 0)
            w_lo(W_Z + 1, 1)
            norm_out(1, memT, g_mem, 4)

            def by_head(ap):
                return ap.rearrange("p (j d) -> p j d", d=HD)

            def spread(ap):
                return ap.unsqueeze(2).to_broadcast([P, HPG, HD])

            for n in range(8):
                q, t = n // 2, n % 2
                hs, cs = slice(HPG * q, HPG * (q + 1)), slice(GW_ * q, GW_ * (q + 1))
                if q < 2:
                    w_lo(W_Z + q + 2, t)
                dve.wait_ge(xs_ps, n + 1)
                v.tensor_tensor(by_head(xd[:, t, cs]), by_head(ps[4 + t][:, :]), spread(dtv[:, t, hs]), ALU.mult)
                v.tensor_tensor(by_head(yb[:, t, cs]), by_head(ps[4 + t][:, :]), spread(small[:, 2, hs]),
                                ALU.mult).then_inc(xs_done, 1)
            dve.wait_ge(ac_ps, 1)
            v.tensor_copy(acm[:, :, :], ps[6][:, 0:64].rearrange("p (t n) -> p t n", t=TC))
            dve.drain()
            v.tensor_copy(dec[:, 1, :], acm[:, 1, :])
            v.tensor_tensor(dec[:, 0, :], ps[6][:, 64:96], acm[:, 0, :], ALU.subtract).then_inc(dec_in, 1)

            def decays(i):
                g, c = i // 2, i % 2
                dve.wait_ge(prep_ps, i + 1)
                v.tensor_tensor(cbm[:, i % 2, :], ps[4][:, 0:P], tri, ALU.mult).then_inc(cb_ok, 1)
                for j in range(HPG):
                    hcol = HPG * g + j
                    last = v.tensor_scalar(mt[:, i % 2, j, :], ps[2 + j // 4][:, P * (j % 4):P * (j % 4 + 1)],
                                           acm[:, c, hcol:hcol + 1], 0.0, ALU.subtract, ALU.min)
                last.then_inc(diff_ok, 1)

            decays(0)
            for i in range(2 * GROUPS):
                g, c = i // 2, i % 2
                gs, hs = slice(GW_ * g, GW_ * (g + 1)), slice(HPG * g, HPG * (g + 1))
                if c == 0:
                    dve.wait_ge(dec_ok, 1)
                    v.tensor_tensor(by_head(xde), by_head(xd[:, 0, gs]), spread(dec[:, 0, hs]),
                                    ALU.mult).then_inc(xde_ok, 1)
                dve.wait_ge(exp_ok, i + 1)
                v.tensor_tensor(mt[:, i % 2, :, :], mt[:, i % 2, :, :],
                                cbm[:, i % 2, :].unsqueeze(1).to_broadcast([P, HPG, P]), ALU.mult).then_inc(mt_ok, 1)
                if i + 1 < 2 * GROUPS:
                    decays(i + 1)
                dve.wait_ge(main_ps, i + 1)
                if c == 1:
                    v.tensor_tensor(by_head(ytmp), by_head(ps[6][:, :]), spread(dec[:, 1, hs]), ALU.mult)
                v.tensor_tensor(yb[:, c, gs], yb[:, c, gs], ps[5][:, :], ALU.add).then_inc(y_read, 1)
                if c == 1:
                    dve.drain()
                    v.tensor_tensor(yb[:, c, gs], yb[:, c, gs], ytmp, ALU.add)
                dve.drain()
                v.tensor_tensor(yb[:, c, gs], yb[:, c, gs], zs[:, c, gs], ALU.mult).then_inc(u_ok, 1)
            dve.wait_ge(stdu, 1)
            v.reciprocal(rsu[:, :], rsu[:, :])
            dve.drain()
            for i in range(2 * GROUPS):
                g, c = i // 2, i % 2
                gs = slice(GW_ * g, GW_ * (g + 1))
                v.tensor_scalar(yb[:, c, gs], yb[:, c, gs], rsu[:, i:i + 1], None, ALU.mult).then_inc(un_ok, 1)
            w_lo(W_OUT, 0)
            w_lo(W_OUT, 1)
            w_lo(W_OUT + 1, 0)
            for j in range(8):
                dve.wait_ge(ut_hi, j + 1)
                for k in (2 * j, 2 * j + 1):
                    last = v.scalar_tensor_tensor(out=uTl[:, k, :], scalar=parT[:, g_ssd + k:g_ssd + k + 1],
                                                  in0=ps[(j + 2) % 4][:, SEQ * (k % 2):SEQ * (k % 2 + 1)],
                                                  in1=uTh[:, k, :].bitcast(F32), op0=ALU.mult, op1=ALU.subtract)
                last.then_inc(ut_lo, 1)
            w_lo(W_OUT + 1, 1)
            for n in (2, 3):
                w_lo(W_OUT + n, 0)
                w_lo(W_OUT + n, 1)

            def add_out(first, t):
                for n in range(2):
                    dve.wait_ge(wo_ps, first + 2 * t + n)
                    r = h[:, t, 512 * n:512 * (n + 1)]
                    v.tensor_tensor(r, r, ps[4 + 2 * n + t][:, :], ALU.add).then_inc(h_ok, 1)

            for t in range(TC):
                add_out(3, t)
                norm_chunk(2, t, xn2, h)
            w_lo(W_Q, 0)
            for b in range(4):
                dve.wait_ge(nt_act, 8 + b + 1)
                for k in (2 * b, 2 * b + 1):
                    last = v.scalar_tensor_tensor(out=xq[1][:, k, :], scalar=parT[:, g_xa + k:g_xa + k + 1],
                                                  in0=ps[b][:, SEQ * (k % 2):SEQ * (k % 2 + 1)],
                                                  in1=xq[0][:, k, :].bitcast(F32), op0=ALU.mult, op1=ALU.subtract)
                last.then_inc(nt_dve, 1)
            w_lo(W_Q, 1)
            w_lo(W_Q + 1, 0)
            w_lo(W_Q + 1, 1)
            for hd in range(XH):
                dve.wait_ge(sc_ps, hd + 1)
                v.tensor_reduce(att[:, 0, 2 * hd:2 * hd + 2], ps[hd][:, :].rearrange("p (t m) -> p t m", t=TC),
                                AX_X, ALU.max, negate=True).then_inc(nmax, 1)
            for hd in range(XH):
                dve.wait_ge(pexp, hd + 1)
                v.reciprocal(att[:, 2, 2 * hd:2 * hd + 2], att[:, 1, 2 * hd:2 * hd + 2])
                dve.drain()
                for t in range(TC):
                    n = 2 * hd + t
                    v.tensor_scalar(pr[:, t, hd, :], pr[:, t, hd, :], att[:, 2, n:n + 1], None,
                                    ALU.mult).then_inc(pn_ok, 1)
            for hd in range(XH):
                dve.wait_ge(pT_ps, hd + 1)
                v.tensor_copy(prT[:, hd, :, :], ps[4 + hd][:, :].rearrange("p (c s) -> p c s", c=2)).then_inc(pT_sb, 1)
            for hd in range(XH):
                dve.wait_ge(oh_ok, hd + 1)
                dst = slice(2 * hd, 2 * hd + 2)
                v.tensor_tensor(xo[1][:, dst, :], ps[hd][:, :].rearrange("p (m s) -> p m s", m=2),
                                xo[0][:, dst, :].bitcast(F32), ALU.subtract).then_inc(pv_sb, 1)
                if hd >= 2:
                    w_lo(W_O, hd - 2)
            w_lo(W_O + 1, 0)
            w_lo(W_O + 1, 1)

            def lo(s, i, j):
                n = EPIECES * j + s
                hi, lo_ = split(s)
                dve.wait_ge(hi_ok, 2 * EPIECES * i + (n + 1))
                v.tensor_tensor(lo_, raw(n), hi.bitcast(F32), ALU.subtract).then_inc(lo_ok, 1)

            v.memset(rank[:, :, NCOL:NCOL + 4], -1.0)
            dve.wait_ge(ld_g, 16)
            for t in range(TC):
                add_out(7, t)
                norm_chunk(3, t, xn, h, g_ffn)
            norm_out(3, xr, None)
            lo(0, 0, 0)
            dve.wait_ge(rt_ps, 1)
            v.tensor_tensor(lg[:, :, :], ps[0][:, 0:2 * NE].rearrange("p (t n) -> p t n", t=TC),
                            b_rt[:, :].unsqueeze(1).to_broadcast([P, TC, NE]), ALU.add)
            dve.drain()
            for t in range(TC):
                v.max(mx8[:, t, :], lg[:, t, :])
            dve.drain()
            v.tensor_scalar(gsum[:, :, 0], mx8[:, :, 0], -1.0, None, ALU.mult).then_inc(lmax, 1)
            for t in range(TC):
                v.max_index(ix8[:, t, :], mx8[:, t, :], lg[:, t, :])
            dve.drain()
            v.tensor_copy(ix8f[:, :, :], ix8[:, :, :])
            dve.drain()
            for t in range(TC):
                v.tensor_scalar(mask[:, t, :], iota[:, 0:NE], ix8f[:, t, 0:1], None, ALU.is_equal)
            for n in range(1, TOPK):
                dve.drain()
                for t in range(TC):
                    v.scalar_tensor_tensor(out=mask[:, t, :], in0=iota[:, 0:NE], scalar=ix8f[:, t, n:n + 1],
                                           in1=mask[:, t, :], op0=ALU.is_equal, op1=ALU.add)
            dve.drain()
            for t in range(TC):
                last = v.tensor_copy(mask4[:, t, :].rearrange("p (c e) -> p c e", e=NE),
                                     mask[:, t, :].unsqueeze(1).to_broadcast([P, CHUNKS, NE]))
            last.then_inc(mask_ok, 1)
            dve.wait_ge(rexp, 1)
            v.tensor_tensor(gate[:, :, :], gate[:, :, :], mask[:, :, :], ALU.mult)
            dve.drain()
            v.tensor_reduce(gsum[:, :, 1], gate[:, :, :], AX_X, ALU.add)
            dve.drain()
            v.reciprocal(gsum[:, :, 0], gsum[:, :, 1])
            dve.drain()
            v.tensor_tensor(gate[:, :, :], gate[:, :, :], gsum[:, :, 0].unsqueeze(2).to_broadcast([P, TC, NE]),
                            ALU.mult).then_inc(gate_ok, 1)
            dve.wait_ge(rank_ps, 1)
            v.scalar_tensor_tensor(out=rank[:, :, 0:NE], in0=ps[1][:, 0:2 * NE].rearrange("p (t n) -> p t n", t=TC),
                                   scalar=1.0, in1=mask[:, :, :], op0=ALU.add, op1=ALU.mult)
            dve.drain()
            for chunk in range(CHUNKS - 1, -1, -1):
                v.tensor_scalar(rank[:, :, NE * chunk:NE * (chunk + 1)], rank[:, :, 0:NE],
                                -1.0 - SLOTS * chunk, None, ALU.add)
            dve.drain()

            def one_hot(column):
                for j in range(2):
                    for t in range(TC):
                        last = v.tensor_scalar(onehot[:, t, SLOTS * j:SLOTS * (j + 1)], iota[:, 0:SLOTS],
                                               rank[:, t, ds(column[j], 1)], None, ALU.is_equal)
                last.then_inc(hot_ok, 1)

            def tokens_lo(count):
                for b in range(2):
                    dve.wait_ge(xh_ok, count + b)
                    v.tensor_tensor(xs[:, 4 * b:4 * b + 4, :, SLOTS:2 * SLOTS],
                                    ps[b][:, :].rearrange("p (k j s) -> p k j s", k=4, j=2),
                                    xs[:, 4 * b:4 * b + 4, :, 0:SLOTS].bitcast(F32), ALU.subtract).then_inc(xs_ok, 1)

            one_hot([0, 1])
            v.memset(scat[:, :, :], 0.0)
            dve.drain()
            v.tensor_copy(scat[:, :, 0:NE], gate[:, :, :]).then_inc(sc_ok, 1)
            dve.wait_ge(cnt_ps, 1)
            v.tensor_tensor(cnt[:, 0:1], ps[3][:, 64:65], col[:, 2:3], ALU.is_gt).then_inc(val_ok, 1)
            lo(1, 0, 0)
            lo(2, 0, 0)
            tokens_lo(1)
            dve.wait_ge(pos_ps, 1)
            v.tensor_copy(cnt[:, 1:2], ps[3][:, 66:67])
            dve.drain()
            v.tensor_scalar(pick[:, :], iota[:, 0:16], cnt[:, 1:2], cnt[:, 0:1], ALU.is_equal,
                            ALU.mult).then_inc(pick_ok, 1)
            dve.wait_ge(lst_ps, 1)
            v.tensor_scalar(lst[0:1, 0:16], ps[3][0:1, 0:16], float(DUMMY), None, ALU.add)
            v.tensor_copy(lst[0:1, 16:33], ps[3][0:1, 16:33])
            dve.drain()
            v.tensor_copy(lst_i[0:1, 0:33], lst[0:1, 0:33]).then_inc(lst_ok, 1)
            lo(3, 0, 0)

            def expert_pass(i, j, further, column, expert, last_round=False):
                dve.wait_ge(st_ps, 2 * i + (j + 1))
                for t in range(TC):
                    last = v.tensor_scalar(scat[:, t, :], iota[:, :], rank[:, t, ds(column, 1)],
                                           gate[:, t, ds(expert, 1)], ALU.is_equal, ALU.mult)
                last.then_inc(sc_ok, 1)
                for s in range(0 if further else 4, 10):
                    lo(s, i, j)
                for g in range(2):
                    dve.wait_ge(t_ps, 4 * i + (2 * j + g + 1))
                    bias = bguT[:, ds(expert * 16, 16)].rearrange("p (a f) -> p a f", a=2)[
                        :, :, 4 * g:4 * g + 4].unsqueeze(3).to_broadcast([P, 2, 4, SLOTS])
                    v.tensor_tensor(gu[:, g, :, :].rearrange("p (a m) s -> p a m s", a=2),
                                    ps[g][:, :].rearrange("p (a m s) -> p a m s", a=2, m=4), bias,
                                    ALU.add).then_inc(gu_free, 1)
                    dve.drain()
                    v.tensor_scalar(gu[:, g, 0:4, :], gu[:, g, 0:4, :], LIMIT, None, ALU.min).then_inc(gb_ok, 1)
                    v.tensor_scalar(gu[:, g, 4:8, :], gu[:, g, 4:8, :], LIMIT, -LIMIT, ALU.min, ALU.max)
                dve.drain()
                for g in range(2):
                    v.scalar_tensor_tensor(out=gu[:, g, 4:8, :], in0=gu[:, g, 4:8, :], scalar=1.0,
                                           in1=gu[:, g, 0:4, :], op0=ALU.add, op1=ALU.mult)
                dve.drain()
                for g in range(2):
                    dve.wait_ge(sg_ok, 4 * i + (2 * j + g + 1))
                    v.tensor_tensor(act_f[:, 4 * g:4 * g + 4, :], gu[:, g, 4:8, :], sg[:, g, :, :], ALU.mult)
                dve.drain()
                for g in range(2):
                    v.tensor_copy(act_s[:, 4 * g:4 * g + 4, 0:SLOTS], act_f[:, 4 * g:4 * g + 4, :])
                dve.drain()
                for g in range(2):
                    v.tensor_tensor(act_s[:, 4 * g:4 * g + 4, SLOTS:2 * SLOTS],
                                    act_f[:, 4 * g:4 * g + 4, :], act_s[:, 4 * g:4 * g + 4, 0:SLOTS].bitcast(F32),
                                    ALU.subtract).then_inc(av_ok, 1)
                lo(10, i, j)
                lo(11, i, j)
                if not further and j == 0:
                    for s in range(4):
                        lo(s, i, 1)
                elif not further and not last_round:
                    tokens_lo(2 * i + 3)
                    for s in range(4):
                        lo(s, i + 1, 0)

            with dve.Fori(0, PAIRS - 1, 1) as i:
                dve.wait_ge(gathered, 2 * i + 2)
                one_hot([2 * i + 2, 2 * i + 3])
                expert_pass(i, 0, False, 2 * i, 2 * i)
                expert_pass(i, 1, False, 2 * i + 1, 2 * i + 1)
            for j in range(2):
                expert_pass(PAIRS - 1, j, False, NE - 2 + j, NE - 2 + j, True)
            extra = dve.value_load(lst_i[0:1, 32:33], min_val=0, max_val=MAX_EXTRA)
            with dve.Fori(0, EXTRA_PAIRS, 1) as q:
                with dve.If(extra > 2 * q):
                    column = [dve.value_load(lst_i[0:1, ds(2 * q + j, 1)], min_val=0, max_val=DUMMY)
                              for j in range(2)]
                    expert = [dve.value_load(lst_i[0:1, ds(2 * q + (16 + j), 1)], min_val=0, max_val=NE - 1)
                              for j in range(2)]
                    i = q + PAIRS
                    dve.wait_ge(gathered, 2 * i)
                    one_hot(column)
                    tokens_lo(2 * i + 1)
                    for j in range(2):
                        expert_pass(i, j, True, column[j], expert[j])

            dve.wait_ge(ld_gf, 16)
            for t in range(TC):
                dve.wait_ge(fsum, t + 1)
                v.tensor_tensor(rst[:, 4, t:t + 1], nrm[:, 4 + t, 0:1], nrm[:, 4 + t, 1:2], ALU.add).then_inc(fadd, 1)
            for t in range(TC):
                dve.wait_ge(stdf, t + 1)
                v.reciprocal(rst[:, 5, t:t + 1], rst[:, 4, t:t + 1])
                dve.drain()
                for n in range(2):
                    last = v.scalar_tensor_tensor(out=h[:, t, 512 * n:512 * (n + 1)], in0=ps[4 + 2 * n + t][:, :],
                                                  scalar=rst[:, 5, t:t + 1], in1=g_fin[:, 512 * n:512 * (n + 1)],
                                                  op0=ALU.mult, op1=ALU.mult)
                last.then_inc(o_ok, 1)


_INS = ["x", "mem", "mixer_norm", "xattn_norm", "mem_norm", "ffn_norm", "ssd_w_in", "ssd_conv_w", "ssd_conv_b",
        "ssd_dt_bias", "ssd_a_log", "ssd_d", "ssd_norm", "ssd_w_out", "xa_w_q", "xa_w_kv", "xa_w_o",
        "moe_w_router", "moe_b_router", "moe_w_gate_up", "moe_b_gate_up", "moe_w_down", "moe_b_down",
        "final_norm"]


def kernel(**inputs):
    import numpy as np
    from concourse import bacc
    from concourse.bass_utils import run_bass_kernel_spmd

    nc = bacc.Bacc("TRN2", target_bir_lowering=False, num_devices=1)
    arrays, args = {}, []
    for name in _INS:
        a = np.ascontiguousarray(inputs[name])
        if name != "final_norm":
            a = a.reshape(a.shape[1:])
        arrays[f"in_{name}"] = a
        args.append(nc.dram_tensor(f"in_{name}", a.shape, mybir.dt.from_np(a.dtype), kind="ExternalInput").ap())
    args.append(nc.dram_tensor("out", (SEQ, D), F32, kind="ExternalOutput").ap())
    build(nc, *args)
    r = run_bass_kernel_spmd(nc, [arrays], core_ids=[0])
    return r.results[0]["out"].reshape(1, SEQ, D)
```
